# Optimizing a Trainium2 kernel written in Bass

```python
import math
import jax, jax.numpy as jnp
from jax import lax
import numpy as np

D_MODEL = 1024
BATCH = 1
SEQ = 512
DEPTH = 1

N_MEM = 256
MLA_HEADS = 8
QK_NOPE = 64
QK_ROPE = 32
V_HEAD = 64
Q_LORA = 384
KV_LORA = 256
MLA_WIDTH = MLA_HEADS * V_HEAD
SSM_WIDTH = 512
SSM_GROUP = 16
SSM_GROUPS = SSM_WIDTH // SSM_GROUP
SSM_STATE = 64
DT_MIN = 1e-3
DT_MAX = 1e-1
MIX_WIDTH = MLA_WIDTH + SSM_WIDTH
IN_WIDTH = Q_LORA + KV_LORA + QK_ROPE + SSM_WIDTH
X_HEADS = 4
X_HEAD_DIM = D_MODEL // X_HEADS
N_KEYS = 128
N_EXPERTS = N_KEYS * N_KEYS
PEER_HEADS = 8
PEER_TOPK = 16
D_KEY = 256
HALF_KEY = D_KEY // 2
Q_BLOCK = 128
TOK_BLOCK = 128
ROPE_THETA = 10000.0
LN_EPS = 1e-5
RMS_EPS = 1e-6
ALPHA = (2 * DEPTH) ** 0.25
BETA = (8 * DEPTH) ** -0.25

kernel_name = "hybrid_mla_s5_peer_deepnorm_layer"

def layer_norm(x, g, b):
    xf = x.astype(jnp.float32)
    mu = jnp.mean(xf, -1, keepdims=True)
    var = jnp.mean(jnp.square(xf - mu), -1, keepdims=True)
    return ((xf - mu) * lax.rsqrt(var + LN_EPS) * g + b).astype(x.dtype)

def rms_norm(x, g):
    xf = x.astype(jnp.float32)
    return (xf * lax.rsqrt(jnp.mean(jnp.square(xf), -1, keepdims=True) + RMS_EPS) * g).astype(x.dtype)

def rope_angles(pos, dim):
    half = dim // 2
    freqs = ROPE_THETA ** (-jnp.arange(half, dtype=jnp.float32) / half)
    ang = pos.astype(jnp.float32)[..., None] * freqs
    return jnp.cos(ang), jnp.sin(ang)

def apply_rope(x, cos, sin):
    half = x.shape[-1] // 2
    xf = x.astype(jnp.float32)
    x1, x2 = xf[..., :half], xf[..., half:]
    return jnp.concatenate([x1 * cos - x2 * sin, x2 * cos + x1 * sin], -1).astype(x.dtype)

def mla(c_q, c_kv, k_r, pos, g_cq, w_uq, g_ckv, w_ukv):
    B, L, _ = c_q.shape
    dq = QK_NOPE + QK_ROPE
    q = (rms_norm(c_q, g_cq) @ w_uq).reshape(B, L, MLA_HEADS, dq)
    kv = (rms_norm(c_kv, g_ckv) @ w_ukv).reshape(B, L, MLA_HEADS, QK_NOPE + V_HEAD)
    q_nope, q_rope = q[..., :QK_NOPE], q[..., QK_NOPE:]
    k_nope, v = kv[..., :QK_NOPE], kv[..., QK_NOPE:]
    cos, sin = rope_angles(pos, QK_ROPE)
    q_rope = apply_rope(q_rope, cos[:, :, None], sin[:, :, None])
    k_rope = apply_rope(k_r, cos, sin)
    q = jnp.concatenate([q_nope, q_rope], -1)
    k = jnp.concatenate([k_nope, jnp.broadcast_to(k_rope[:, :, None], (B, L, MLA_HEADS, QK_ROPE))], -1)
    scale = dq ** -0.5
    nb = L // Q_BLOCK
    q_blocks = q.reshape(B, nb, Q_BLOCK, MLA_HEADS, dq).transpose(1, 0, 2, 3, 4)
    key_idx = jnp.arange(L)

    def block(args):
        qb, start = args
        s = jnp.einsum('bqhd,bkhd->bhqk', qb, k).astype(jnp.float32) * scale
        q_idx = start + jnp.arange(Q_BLOCK)
        s = jnp.where(key_idx[None, :] <= q_idx[:, None], s, -jnp.inf)
        p = jax.nn.softmax(s, -1).astype(v.dtype)
        return jnp.einsum('bhqk,bkhd->bqhd', p, v)

    o = lax.map(block, (q_blocks, jnp.arange(nb) * Q_BLOCK))
    return o.transpose(1, 0, 2, 3, 4).reshape(B, L, MLA_WIDTH)

def s5_ssm(u, lam_re, lam_im, log_dt, b_re, b_im, c_re, c_im, d_skip, w_glu, b_glu):
    B, L, _ = u.shape
    f32 = jnp.float32
    ug = u.reshape(B, L, SSM_GROUPS, SSM_GROUP).astype(f32)
    lr, li = lam_re.astype(f32), lam_im.astype(f32)
    b_re, b_im = b_re.astype(f32), b_im.astype(f32)
    c_re, c_im = c_re.astype(f32), c_im.astype(f32)
    dt = jnp.exp(log_dt.astype(f32))[:, None]
    mag = jnp.exp(lr * dt)
    ab_re, ab_im = mag * jnp.cos(li * dt), mag * jnp.sin(li * dt)
    den = lr * lr + li * li
    nr, ni = ab_re - 1.0, ab_im
    f_re = (nr * lr + ni * li) / den
    f_im = (ni * lr - nr * li) / den
    bb_re = f_re[..., None] * b_re - f_im[..., None] * b_im
    bb_im = f_re[..., None] * b_im + f_im[..., None] * b_re
    bu_re = jnp.einsum('blgh,gph->blgp', ug, bb_re)
    bu_im = jnp.einsum('blgh,gph->blgp', ug, bb_im)
    a_re = jnp.broadcast_to(ab_re, bu_re.shape)
    a_im = jnp.broadcast_to(ab_im, bu_im.shape)

    def combine(e1, e2):
        a1r, a1i, b1r, b1i = e1
        a2r, a2i, b2r, b2i = e2
        return (a2r * a1r - a2i * a1i,
                a2r * a1i + a2i * a1r,
                a2r * b1r - a2i * b1i + b2r,
                a2r * b1i + a2i * b1r + b2i)

    _, _, s_re, s_im = lax.associative_scan(combine, (a_re, a_im, bu_re, bu_im), axis=1)
    y = (jnp.einsum('blgp,ghp->blgh', s_re, c_re)
         - jnp.einsum('blgp,ghp->blgh', s_im, c_im)
         + d_skip.astype(f32) * ug)
    y = jax.nn.gelu(y.reshape(B, L, SSM_WIDTH))
    y = y * jax.nn.sigmoid(y @ w_glu.astype(f32) + b_glu.astype(f32))
    return y.astype(u.dtype)

def mem_xattn(x, mem, w_q, w_k, w_v, w_o):
    B, L, _ = x.shape
    M = mem.shape[1]
    q = (x @ w_q).reshape(B, L, X_HEADS, X_HEAD_DIM)
    k = (mem @ w_k).reshape(B, M, X_HEADS, X_HEAD_DIM)
    v = (mem @ w_v).reshape(B, M, X_HEADS, X_HEAD_DIM)
    s = jnp.einsum('blhd,bmhd->bhlm', q, k).astype(jnp.float32) * (X_HEAD_DIM ** -0.5)
    p = jax.nn.softmax(s, -1).astype(v.dtype)
    o = jnp.einsum('bhlm,bmhd->blhd', p, v).reshape(B, L, D_MODEL)
    return o @ w_o

def peer(x, w_query, sub_keys1, sub_keys2, u_tab, v_tab):
    B, L, D = x.shape
    T = B * L
    xt = x.reshape(T, D)
    q = (xt @ w_query).reshape(T, PEER_HEADS, 2, HALF_KEY)
    s1 = jnp.einsum('thd,nd->thn', q[:, :, 0], sub_keys1).astype(jnp.float32)
    s2 = jnp.einsum('thd,nd->thn', q[:, :, 1], sub_keys2).astype(jnp.float32)
    v1, i1 = lax.top_k(s1, PEER_TOPK)
    v2, i2 = lax.top_k(s2, PEER_TOPK)
    cand_s = (v1[..., :, None] + v2[..., None, :]).reshape(T, PEER_HEADS, PEER_TOPK * PEER_TOPK)
    cand_id = (i1[..., :, None] * N_KEYS + i2[..., None, :]).reshape(T, PEER_HEADS, PEER_TOPK * PEER_TOPK)
    top_s, sel = lax.top_k(cand_s, PEER_TOPK)
    ids = jnp.take_along_axis(cand_id, sel, -1)
    gates = jax.nn.softmax(top_s, -1).astype(x.dtype)
    nb = T // TOK_BLOCK

    def block(args):
        xb, idb, gb = args
        u = u_tab[idb]
        h = jax.nn.gelu(jnp.einsum('td,thkd->thk', xb, u))
        return jnp.einsum('thk,thkd->td', gb * h, v_tab[idb])

    out = lax.map(block, (xt.reshape(nb, TOK_BLOCK, D),
                          ids.reshape(nb, TOK_BLOCK, PEER_HEADS, PEER_TOPK),
                          gates.reshape(nb, TOK_BLOCK, PEER_HEADS, PEER_TOPK)))
    return out.reshape(B, L, D)

def setup_inputs(seed: int = 0) -> dict:
    key = jax.random.key(seed)
    ks = iter(jax.random.split(key, 48))

    def nrm(shape, scale):
        return jax.random.normal(next(ks), shape, jnp.float32) * scale

    def gain(n):
        return 1.0 + nrm((DEPTH, n), 0.02)

    G, P, H = SSM_GROUPS, SSM_STATE, SSM_GROUP
    x = nrm((BATCH, SEQ, D_MODEL), 1.0)
    mem = nrm((BATCH, N_MEM, D_MODEL), 1.0)
    positions = (jax.random.randint(next(ks), (BATCH, 1), 0, 4096, dtype=jnp.int32)
                 + jnp.arange(SEQ, dtype=jnp.int32)[None, :])
    n_idx = jnp.arange(P, dtype=jnp.float32)
    return {
        "x": x,
        "mem": mem,
        "positions": positions,
        "w_in": nrm((DEPTH, D_MODEL, IN_WIDTH), D_MODEL ** -0.5),
        "g_cq": gain(Q_LORA),
        "w_uq": nrm((DEPTH, Q_LORA, MLA_HEADS * (QK_NOPE + QK_ROPE)), Q_LORA ** -0.5),
        "g_ckv": gain(KV_LORA),
        "w_ukv": nrm((DEPTH, KV_LORA, MLA_HEADS * (QK_NOPE + V_HEAD)), KV_LORA ** -0.5),
        "lam_re": -0.5 + nrm((DEPTH, G, P), 0.01),
        "lam_im": jnp.pi * n_idx + nrm((DEPTH, G, P), 0.01),
        "log_dt": jax.random.uniform(next(ks), (DEPTH, G), jnp.float32,
                                     minval=math.log(DT_MIN), maxval=math.log(DT_MAX)),
        "b_re": nrm((DEPTH, G, P, H), (2.0 * H) ** -0.5),
        "b_im": nrm((DEPTH, G, P, H), (2.0 * H) ** -0.5),
        "c_re": nrm((DEPTH, G, H, P), (2.0 * P) ** -0.5),
        "c_im": nrm((DEPTH, G, H, P), (2.0 * P) ** -0.5),
        "d_skip": nrm((DEPTH, G, H), 1.0),
        "w_glu": nrm((DEPTH, SSM_WIDTH, SSM_WIDTH), SSM_WIDTH ** -0.5),
        "b_glu": nrm((DEPTH, SSM_WIDTH), 0.01),
        "g_mla_out": gain(MLA_WIDTH),
        "g_ssm_out": gain(SSM_WIDTH),
        "w_out": nrm((DEPTH, MIX_WIDTH, D_MODEL), BETA * MIX_WIDTH ** -0.5),
        "ln1_g": gain(D_MODEL),
        "ln1_b": nrm((DEPTH, D_MODEL), 0.01),
        "xq": nrm((DEPTH, D_MODEL, D_MODEL), D_MODEL ** -0.5),
        "xk": nrm((DEPTH, D_MODEL, D_MODEL), D_MODEL ** -0.5),
        "xv": nrm((DEPTH, D_MODEL, D_MODEL), D_MODEL ** -0.5),
        "xo": nrm((DEPTH, D_MODEL, D_MODEL), BETA * D_MODEL ** -0.5),
        "ln2_g": gain(D_MODEL),
        "ln2_b": nrm((DEPTH, D_MODEL), 0.01),
        "w_query": nrm((DEPTH, D_MODEL, PEER_HEADS * D_KEY), D_MODEL ** -0.5),
        "sub_keys1": nrm((DEPTH, N_KEYS, HALF_KEY), HALF_KEY ** -0.5),
        "sub_keys2": nrm((DEPTH, N_KEYS, HALF_KEY), HALF_KEY ** -0.5),
        "u_tab": nrm((DEPTH, N_EXPERTS, D_MODEL), D_MODEL ** -0.5),
        "v_tab": nrm((DEPTH, N_EXPERTS, D_MODEL), BETA),
        "ln3_g": gain(D_MODEL),
        "ln3_b": nrm((DEPTH, D_MODEL), 0.01),
    }

def reference(x, mem, positions, w_in, g_cq, w_uq, g_ckv, w_ukv, lam_re, lam_im, log_dt,
              b_re, b_im, c_re, c_im, d_skip, w_glu, b_glu, g_mla_out, g_ssm_out, w_out,
              ln1_g, ln1_b, xq, xk, xv, xo, ln2_g, ln2_b, w_query, sub_keys1, sub_keys2,
              u_tab, v_tab, ln3_g, ln3_b):
    split_at = [Q_LORA, Q_LORA + KV_LORA, Q_LORA + KV_LORA + QK_ROPE]
    for l in range(DEPTH):
        proj = x @ w_in[l]
        c_q, c_kv, k_r, u = jnp.split(proj, split_at, axis=-1)
        o_attn = mla(c_q, c_kv, k_r, positions, g_cq[l], w_uq[l], g_ckv[l], w_ukv[l])
        o_ssm = s5_ssm(u, lam_re[l], lam_im[l], log_dt[l], b_re[l], b_im[l], c_re[l], c_im[l],
                       d_skip[l], w_glu[l], b_glu[l])
        mixed = jnp.concatenate([rms_norm(o_attn, g_mla_out[l]),
                                 rms_norm(o_ssm, g_ssm_out[l])], -1) @ w_out[l]
        x = layer_norm(ALPHA * x + mixed, ln1_g[l], ln1_b[l])
        x = layer_norm(ALPHA * x + mem_xattn(x, mem, xq[l], xk[l], xv[l], xo[l]), ln2_g[l], ln2_b[l])
        x = layer_norm(ALPHA * x + peer(x, w_query[l], sub_keys1[l], sub_keys2[l], u_tab[l], v_tab[l]),
                       ln3_g[l], ln3_b[l])
    return x


_drawn_inputs = setup_inputs


def setup_inputs(seed=0):
    import zlib

    import numpy as np

    out = dict(_drawn_inputs(seed))
    spreads = {}
    factors = {'lam_re': 200.0,
     'b_glu': 5.616,
     'ln3_g': 22.971,
     'ln3_b': 47.688,
     'g_cq': 2.699,
     'b_re': 3.033,
     'b_im': 2.877,
     'c_re': 3.001,
     'c_im': 2.912,
     'g_ssm_out': 2.668,
     'g_mla_out': 2.902}
    for name, (base, spread) in spreads.items():
        noise = np.random.default_rng([zlib.crc32(name.encode()), seed]).standard_normal(out[name].shape)
        drawn = base * np.exp(spread * noise) if base else spread * noise
        out[name] = __import__('jax').numpy.asarray(drawn.astype(out[name].dtype))
    for name, factor in factors.items():
        out[name] = (out[name] * factor).astype(out[name].dtype)
    return out
```

```python
import math
from contextlib import ExitStack

import numpy as np
import concourse.bass as bass
from concourse import mybir

F32 = mybir.dt.float32
U32 = mybir.dt.uint32
I32 = mybir.dt.int32
ALU = mybir.AluOpType
ACT = mybir.ActivationFunctionType
AX = mybir.AxisListType

P = 128
D = 1024
T = 512
TC = 256
NC = T // TC
TB = TC // P
NTB = T // P
KD = D // P
M_MEM = 256
MB = M_MEM // P
H = 8
NOPE, ROPE, VH = 64, 32, 64
DQ = NOPE + ROPE
QL, KVL, SW = 384, 256, 512
XH = 4
G, NS, GC = 32, 64, 16
JT = G // 2
PH, NK, TOPK = 8, 128, 16
HK = PH * TOPK
ALPHA = 2.0 ** 0.25
MAGIC = 12582912.0
INV2PI = float(1.0 / (2.0 * math.pi))
C1 = 6.28125
C2 = float(np.float32(round((2 * math.pi - C1) * 2 ** 18) / 2 ** 18))
C3 = float(2 * math.pi - C1 - C2)
PI_IN = 3.1415925
GELU_C = math.sqrt(2.0 / math.pi)
RB = 6
SLOTS = 3
SLOT = 4096
NG = 8
CW = 6 * P + 32 + 16 + 1


def shape_constants():
    c = np.zeros((P, CW), np.float32)
    r = np.arange(P)
    c[:, 0:128] = np.eye(P)
    c[:, 128:256] = np.where(r[None, :] <= r[:, None], 0.0, -1e30)
    c[:, 256:384] = ((r[:, None] // 16) % 2 == (r[None, :] // 64))
    rot = np.zeros((P, P), np.float32)
    for m in range(P):
        if m % 32 < 16:
            rot[m + 16, m] = -1.0
        else:
            rot[m - 16, m] = 1.0
    c[:, 384:512] = rot
    c[0:32, 512:640] = np.tile(np.eye(32), (1, 4))
    c[0:32, 640:768] = np.tile(rot[0:32, 0:32], (1, 4))
    c[:, 768:784] = np.arange(1, 17)
    c[:, 784:800] = 16 * np.arange(16)
    c[:, 800:816] = np.arange(16)
    c[:, 816] = (np.float32(10000.0) ** (-np.arange(16, dtype=np.float32) / 16))[r % 16]
    return c


def bc(ap, axis, n):
    a = ap.unsqueeze(axis)
    shape = list(a.shape)
    shape[axis] = n
    return a.to_broadcast(shape)


def jobs_of_pe():
    jobs = []
    for c in range(NC):
        if c == 0:
            jobs.append((("cols",), "dve"))
        jobs += [(("xT", c, k), "act") for k in range(KD)]
        if c == 0:
            jobs += [(("memT", k), "act") for k in range(KD // 2)]
            jobs.append((("keysT",), "act"))
        jobs += [(("u", c, n), "act") for n in range(4)]
        jobs += [(("kr", c), "act")]
        jobs += [(("ckv", c, n), "act") for n in range(2)]
        jobs += [(("cq", c, n), "act") for n in range(3)]
        jobs.append((("krot", c), "dve"))
        if c == 0:
            jobs += [(("BT", i), "act") for i in range(2)] + [(("CT", i), "act") for i in range(2)]
        jobs.append((("ss", c), "act"))
        jobs += [(("qrope", c, g), "act") for g in range(2)]
        jobs.append((("qrot", c), "dve"))
        jobs += [(("qn", c, i), "act") for i in range(4)]
        jobs += [(("kn", c, i), "act") for i in range(4)]
        jobs += [(("v", c, tb), "act") for tb in range(TB)]
        jobs.append((("bu", c, 0), "dve"))
        jobs.append((("sc", c, 0), "act"))
        for j in range(JT):
            if c == 0 and j < 12:
                jobs.append((("mem", j), "act"))
            if j + 1 < JT:
                jobs.append((("bu", c, j + 1), "dve"))
            jobs.append((("PT", c, j), "act"))
            if j % 4 == 3:
                jobs.append((("pv", c, j // 4), "act"))
            if j + 1 < JT:
                jobs.append((("sc", c, j + 1), "act"))
        jobs += [(("glu", c, n), "act") for n in range(4)]
        jobs.append((("ms", c), "act"))
        for half in range(2):
            for tb in range(TB):
                jobs += [(("mixA", c, half, tb), "dve"), (("mixB", c, half, tb), "dve")]
        jobs += [(("x1T", c, k), "act") for k in range(KD)]
        jobs += [(("qx", c, n), "act") for n in range(8)]
        jobs.append((("xs", c, 0), "act"))
        for i in range(XH * TB):
            if i + 1 < XH * TB:
                jobs.append((("xs", c, i + 1), "act"))
            jobs.append((("xPT", c, i), "act"))
            if i % TB == TB - 1:
                jobs += [(("ox", c, i // TB, dc), "act") for dc in range(2)]
        for half in range(2):
            for tb in range(TB):
                jobs.append((("xo", c, half, tb), "dve"))
        jobs += [(("x2T", c, k), "act") for k in range(KD)]
        jobs += [(("qq", c, n), "act") for n in range(16)]
        for tb in range(TB):
            jobs += [(("ks", c, tb, g), "act") for g in range(4)]
    return jobs


JOBS = jobs_of_pe()
NUM = {name: n for n, (name, _) in enumerate(JOBS)}
EMPTIED = {}
_count = {"act": 0, "dve": 0}
for _name, _eng in JOBS:
    _count[_eng] += 1
    EMPTIED[_name] = _count[_eng]


def weight_pieces():
    out = []
    for c in range(NC):
        out += [("u%d" % c, ("u", c, 3)), ("ckr%d" % c, ("ckv", c, 1)), ("cq%d" % c, ("cq", c, 2))]
        if c == 0:
            out += [("xk0", ("mem", 3)), ("xk1", ("mem", 7)), ("xv0", ("mem", 9)), ("xv1", ("mem", 11))]
        out += [("glu%d" % c, ("glu", c, 3)), ("wo0%d" % c, ("mixB", c, 0, TB - 1)), ("wo1%d" % c, ("mixB", c, 1, TB - 1)),
                ("xq0%d" % c, ("qx", c, 3)), ("xq1%d" % c, ("qx", c, 7)),
                ("xo0%d" % c, ("xo", c, 0, TB - 1)), ("xo1%d" % c, ("xo", c, 1, TB - 1))]
        out += [("wq%d%d" % (i, c), ("qq", c, 4 * i + 3)) for i in range(4)]
    return out


PIECES = weight_pieces()
PNUM = {name: n for n, (name, _) in enumerate(PIECES)}


def build(nc, a, consts, out, stop=None):
    ctx = ExitStack()
    with ctx:
        def sb(name, cols, dt=F32, rows=P):
            return ctx.enter_context(nc.sbuf_tensor(name, [rows, cols], dt))

        def sem(name):
            return ctx.enter_context(nc.semaphore(name))

        ring = sb("weight_ring", SLOTS * SLOT)
        uqkv = sb("uqkv", 3 * 768 + 2 * 1024)
        xcur_t = sb("xcur", NTB * D)
        actT_t = sb("actT", KD * TC)
        kT_t = sb("kT", H * T)
        v_t = sb("v", NTB * H * VH)
        kTx_t = sb("kTx", 8 * M_MEM)
        vx_t = sb("vx", MB * D)
        lngb = sb("lngb", 2 * D)
        BT_t = sb("BT", 4 * 2 * P)
        CT_t = sb("CT", 2 * JT * 32)
        trig_t = sb("trig", 2 * JT * 32)
        cst = sb("cst", CW)
        cols = sb("cols", P)
        ropet = sb("ropet", 2 * T)
        keysT = sb("keysT", 2 * NK)
        ids_t = sb("ids", NTB * HK, U32)
        gates_t = sb("gates", NTB * HK)
        scratch = sb("scratch", 10496)
        kc = sb("kc", 4)
        ones = sb("ones_t", P)[:, :]
        small = sb("small", 96)
        kcol = sb("kcol", 8)
        pool_t = sb("pool_t", 512)

        ident = cst[:, 0:128]
        causal = cst[:, 128:256]
        parity = cst[:, 256:384]
        rot = cst[:, 384:512]
        rep = cst[0:32, 512:640]
        reprot = cst[0:32, 640:768]
        mult32 = cst[:, 768:800]
        iota16 = cst[:, 800:816]
        freq = cst[:, 816:817]

        uq_n = uqkv[:, 0:1536].rearrange("p (k n) -> p k n", k=3)
        uq_r = uqkv[:, 1536:2304].rearrange("p (k n) -> p k n", k=3)
        ukv_n = uqkv[:, 2304:3328].rearrange("p (k n) -> p k n", k=2)
        ukv_v = uqkv[:, 3328:4352].rearrange("p (k n) -> p k n", k=2)
        xcur = xcur_t[:, :].rearrange("p (t d) -> p t d", t=NTB)
        memT = xcur_t[:, 2048:4096].rearrange("p (k m) -> p k m", k=KD)
        actT = actT_t[:, :].rearrange("p (k t) -> p k t", k=KD)
        qT = actT_t[:, :].rearrange("p (h t) -> p h t", h=H)
        kT = kT_t[:, :].rearrange("p (h t) -> p h t", h=H)
        V = v_t[:, :].rearrange("p (t n) -> p t n", t=NTB)
        mem_nat = v_t[:, :].rearrange("p (b d) -> p b d", b=MB)
        kTx = kTx_t[:, :].rearrange("p (n m) -> p n m", n=8)
        vx = vx_t[:, :].rearrange("p (b d) -> p b d", b=MB)
        BT = BT_t[:, :].rearrange("p (i c m) -> p i c m", i=2, c=4)
        CT = CT_t[:, :].rearrange("p (i j h) -> p i j h", i=2, j=JT)
        trig = trig_t[:, :].rearrange("p (i j m) -> p i j m", i=2, j=JT)
        ropeC, ropeS = ropet[:, 0:T], ropet[:, T:2 * T]

        rows = kT_t[:, 0:128]
        bnat = kT_t[:, 128:640].rearrange("p (i j h) -> p i j h", i=2, j=JT)
        cnat = kT_t[:, 640:1152].rearrange("p (i c q) -> p i c q", i=2, c=4)
        bbpad = kT_t[:, 1152:2176].rearrange("p (i c m) -> p i c m", i=2, c=4)
        cdup = kT_t[:, 2176:3200].rearrange("p (i c m) -> p i c m", i=2, c=4)
        par = [kT_t[:, 3200 + 16 * i:3216 + 16 * i] for i in range(24)]
        ldt = kT_t[:, 3600:3602]
        keys_nat = kTx_t[:, 0:256].rearrange("p (i d) -> p i d", i=2)
        ang = scratch[:, 0:3072]
        pos_i = scratch[:, 3072:3584].bitcast(I32)
        bbw = scratch[:, 3584:4608].rearrange("p (i j h) -> p i j h", i=4, j=JT)

        uT = scratch[:, 0:1024].rearrange("p (n t) -> p n t", n=4)
        cT = scratch[:, 1024:2304].rearrange("p (n t) -> p n t", n=5)
        yT = scratch[:, 1024:2048].rearrange("p (n t) -> p n t", n=4)
        oT = scratch[:, 2304:3328].rearrange("p (n t) -> p n t", n=4)
        PTr = scratch[:, 3328:5376]
        PT = PTr.rearrange("p (i k t) -> p i k t", i=2, k=NTB)
        Pr = scratch[:, 5376:6400]
        Pq = Pr.rearrange("p (i n) -> p i n", i=2)
        sq5 = PTr[:, 0:1280].rearrange("p (n t) -> p n t", n=5)
        kraw = PTr[:, 1280:1536]
        kt1, kt2 = PTr[:, 1536:1792], PTr[:, 1792:2048]
        g1, g2 = PTr[:, 0:1024], PTr[:, 1024:2048]
        qraw = Pr[:, 0:512].rearrange("p (g t) -> p g t", g=2)
        qtmp = Pr[:, 512:1024].rearrange("p (g t) -> p g t", g=2)
        s5 = scratch[:, 6400:10496]
        tab = s5[:, 0:1024].rearrange("p (b i t) -> p b i t", b=2, i=2)
        sA = s5[:, 1024:1536].rearrange("p (i t) -> p i t", i=2)
        sB = s5[:, 1536:2048].rearrange("p (i t) -> p i t", i=2)
        sW = s5[:, 2048:2560].rearrange("p (i t) -> p i t", i=2)
        sR = s5[:, 2560:3072].rearrange("p (i t) -> p i t", i=2)
        sS = s5[:, 3072:4096].rearrange("p (b i t) -> p b i t", b=2, i=2)
        rms = s5[:, 1024:1536]

        qTx = scratch[:, 0:2048].rearrange("p (n t) -> p n t", n=8)
        oTx = scratch[:, 2048:4096].rearrange("p (n t) -> p n t", n=8)
        Px = scratch[:, 4096:4608].rearrange("p (i m) -> p i m", i=2)
        PTx = scratch[:, 4608:5632].rearrange("p (i m t) -> p i m t", i=2, m=MB)

        qTq = scratch[:, 0:4096].rearrange("p (n t) -> p n t", n=16)
        S1 = scratch[:, 4096:6144]
        S2 = scratch[:, 6144:8192]
        rv = scratch[:, 8192:8448]
        ridx = scratch[:, 8448:8704].bitcast(U32)
        rif = scratch[:, 8704:8960]
        tops = scratch[:, 8960:9088]
        tpos = scratch[:, 9088:9216].bitcast(U32)
        tab_a = scratch[:, 9216:9344]
        tab_b = scratch[:, 9344:9472]
        tia = scratch[:, 9472:9600]
        tib = scratch[:, 9600:9728]
        tau = scratch[:, 9728:9856].bitcast(U32)
        tbu = scratch[:, 9856:9984].bitcast(U32)

        ubuf = [ring[:, D * s:D * (s + 1)] for s in range(NG)]
        vbuf = [ring[:, D * (NG + s):D * (NG + s + 1)] for s in range(4)] + [scratch[:, D * s:D * (s + 1)] for s in range(4)]
        diag = scratch[:, 4096:6144].rearrange("p (q s m) -> p q s m", q=2, s=NG)
        hbuf = scratch[:, 6144:6400].rearrange("p (q n) -> p q n", q=2)
        wbuf = scratch[:, 6400:6656].rearrange("p (q n) -> p q n", q=2)
        gel = scratch[:, 6656:6912].rearrange("p (q n) -> p q n", q=2)
        h8 = scratch[:, 6912:6928].rearrange("p (q n) -> p q n", q=2)
        w8 = scratch[:, 6928:6944].rearrange("p (q n) -> p q n", q=2)
        idstage = scratch[:, 6944:6976].bitcast(U32).rearrange("p (i q n) -> p i q n", i=2, q=2)

        nmax = small[:, 0:4]
        rsum = small[:, 4:8]
        rsmix = small[:, 8:12]
        st6 = small[:, 12:24].rearrange("p (i n) -> p i n", i=2)
        mv = small[:, 24:26]
        std = small[:, 26:28]
        carry = small[:, 32:64].rearrange("p (j i) -> p j i", j=JT)
        magc = small[:, 64:80]
        gsum = small[:, 80:88]

        psum = ctx.enter_context(nc.psum_tensor("banks", [P, 8, 512], F32))

        def bank_of(name):
            return psum[:, NUM[name] % RB, :]

        pe_done = sem("pe_done")
        emptied = {"act": sem("act_emptied"), "dve": sem("dve_emptied")}
        w_land = [sem("w_land%d" % i) for i in range(SLOTS)]
        x_land = sem("x_land")
        mem_land = sem("mem_land")
        c_land = sem("c_land")
        par_land = sem("par_land")
        pos_land = sem("pos_land")
        keys_land = sem("keys_land")
        uqkv_land = sem("uqkv_land")
        ln_land = sem("ln_land")
        out_land = sem("out_land")
        ldt_ok = sem("ldt_ok")
        fills = sem("fills")
        dve_c = sem("dve_chain")
        act_c = sem("act_chain")
        pool_c = sem("pool_chain")
        rows_ok = sem("rows_ok")
        par_dve = sem("par_dve")
        par_act = sem("par_act")
        bt_ok = sem("bt_ok")
        trig_ok = sem("trig_ok")
        tab_ok = sem("tab_ok")
        tab_used = sem("tab_used")
        sq_ok = sem("sq_ok")
        rms_ok = sem("rms_ok")
        c_ok = sem("c_ok")
        q_ok = sem("q_ok")
        smax = sem("smax")
        pexp = sem("pexp")
        pn = sem("pn")
        st_ok = sem("st_ok")
        y_mm = sem("y_mm")
        y_ok = sem("y_ok")
        gl_act = sem("gl_act")
        gl_dve = sem("gl_dve")
        mixin = sem("mixin")
        sqm = sem("sqm")
        rsm = sem("rsm")
        var_ok = sem("var_ok")
        std_ok = sem("std_ok")
        ln_ok = sem("ln_ok")
        xscaled = sem("xscaled")
        xsmax = sem("xsmax")
        xexp = sem("xexp")
        xpn = sem("xpn")
        s_free = sem("s_free")
        rt_d = sem("rt_d")
        rt_a = sem("rt_a")
        route_ok = sem("route_ok")
        u_land = [sem("u_land%d" % i) for i in range(NG)]
        v_land = [sem("v_land%d" % i) for i in range(NG)]
        u_free = sem("u_free")
        v_free = sem("v_free")
        stage_u = sem("stage_u")
        stage_v = sem("stage_v")
        h_ok = sem("h_ok")
        h_act = sem("h_act")
        w_ok = sem("w_ok")
        diag_ok = sem("diag_ok")
        peer_out = sem("peer_out")
        fin_ok = sem("fin_ok")
        w8_ok = sem("w8_ok")
        h8_ok = sem("h8_ok")
        bc_land = sem("bc_land")

        block = ctx.enter_context(nc.Block())

        def wslot(name, k, n):
            s = PNUM[name] % SLOTS
            return ring[:, s * SLOT:s * SLOT + k * n].rearrange("p (k n) -> p k n", k=k)

        def wait_piece(eng, name):
            n = PNUM[name]
            eng.wait_ge(w_land[n % SLOTS], 16 * (n // SLOTS + 1))

        def wait_emptied(eng, name):
            eng.wait_ge(emptied[JOBS[NUM[name]][1]], EMPTIED[name])

        def wait_job(eng, name):
            eng.wait_ge(pe_done, NUM[name] + 1)

        w_in = a["w_in"][0].rearrange("(k p) n -> p k n", p=P)
        w_out = a["w_out"][0].rearrange("(k p) n -> p k n", p=P)
        wqv = a["w_query"][0].rearrange("(k p) n -> p k n", p=P)
        xw = {n: a[n][0].rearrange("(k p) n -> p k n", p=P) for n in ("xq", "xk", "xv", "xo")}

        def piece_source(name):
            if name[:3] == "ckr":
                return w_in[:, :, QL:QL + KVL + ROPE]
            if name[:2] == "cq":
                return w_in[:, :, 0:QL]
            if name[:3] == "glu":
                return a["w_glu"][0].rearrange("(k p) n -> p k n", p=P)
            if name[0] == "u":
                return w_in[:, :, QL + KVL + ROPE:]
            half = int(name[2])
            if name[:2] == "wo":
                return w_out[:, :, 512 * half:512 * half + 512]
            if name[:2] == "wq":
                return wqv[:, :, 512 * half:512 * half + 512]
            return xw[name[:2]][:, :, 512 * half:512 * half + 512]

        @block.sync
        def _(sp):
            def load_x(c):
                if c:
                    wait_job(sp, ("mem", 11))
                sp.dma_start(xcur[:, c * TB:(c + 1) * TB, :],
                             a["x"][0, c * TC:(c + 1) * TC, :].rearrange("(t p) d -> p t d", p=P)).then_inc(x_land, 16)

            def load_ln(g, b):
                sp.dma_start(lngb[:, 0:D], a[g][0:1, :].to_broadcast([P, D])).then_inc(ln_land, 16)
                sp.dma_start(lngb[:, D:2 * D], a[b][0:1, :].to_broadcast([P, D])).then_inc(ln_land, 16)

            def load_piece(n):
                name = PIECES[n][0]
                if n >= SLOTS:
                    wait_job(sp, PIECES[n - SLOTS][1])
                src = piece_source(name)
                sp.dma_start(wslot(name, src.shape[1], src.shape[2]), src).then_inc(w_land[n % SLOTS], 16)

            sp.dma_start(cst[:, :], consts).then_inc(c_land, 16)
            sp.dma_start(rows[0:16, :], a["lam_re"][0].rearrange("(j g) q -> j (g q)", g=2)).then_inc(par_land, 16)
            sp.dma_start(rows[16:32, :], a["lam_im"][0].rearrange("(j g) q -> j (g q)", g=2)).then_inc(par_land, 16)
            sp.dma_start(ldt[32:48, :], a["log_dt"][0].rearrange("(j g) -> j g", g=2)).then_inc(par_land, 16)
            at = 48
            for name, n in (("g_ckv", 2), ("g_cq", 3), ("d_skip", 4), ("b_glu", 4), ("g_mla_out", 4), ("g_ssm_out", 4)):
                src = a[name][0].rearrange("g h -> (g h)") if name == "d_skip" else a[name][0]
                sp.dma_start(rows[at:at + n, :], src.rearrange("(c p) -> c p", p=P)).then_inc(par_land, 16)
                at += n
            load_x(0)
            load_piece(0)
            sp.dma_start(pos_i, a["positions"][0:1, :].to_broadcast([P, T])).then_inc(pos_land, 16)
            for i, name in enumerate(("b_re", "b_im")):
                sp.dma_start(bnat[:, i], a[name][0].rearrange("(j g) q h -> (g q) j h", g=2)).then_inc(bc_land, 16)
            for i, name in enumerate(("c_re", "c_im")):
                sp.dma_start(cnat[:, i], a[name][0].rearrange("(c g) h q -> (g h) c q", c=4)).then_inc(bc_land, 16)
            load_piece(1)
            load_piece(2)
            sp.dma_start(mem_nat, a["mem"][0].rearrange("(b p) d -> p b d", p=P)).then_inc(mem_land, 16)
            for i, name in enumerate(("sub_keys1", "sub_keys2")):
                sp.dma_start(keys_nat[:, i], a[name][0]).then_inc(keys_land, 16)
            for dst, name, wide, lo, hi in ((uq_n, "w_uq", DQ, 0, NOPE), (uq_r, "w_uq", DQ, NOPE, DQ),
                                            (ukv_n, "w_ukv", NOPE + VH, 0, NOPE), (ukv_v, "w_ukv", NOPE + VH, NOPE, NOPE + VH)):
                for k in range(dst.shape[1]):
                    src = a[name][0, k * P:(k + 1) * P, :].rearrange("p (h d) -> p h d", d=wide)[:, :, lo:hi]
                    sp.dma_start(dst[:, k, :].rearrange("p (h d) -> p h d", h=H), src).then_inc(uqkv_land, 16)
            load_ln("ln1_g", "ln1_b")
            n = 3
            for c in range(NC):
                while n < len(PIECES) and n <= PNUM["wo1%d" % c]:
                    load_piece(n)
                    n += 1
                if c == 0:
                    load_x(1)
                load_piece(n)
                n += 1
                sp.wait_ge(ln_ok, 2 * TB * c + TB)
                load_ln("ln2_g", "ln2_b")
                last = PNUM["wq3%d" % c]
                while n <= last:
                    load_piece(n)
                    n += 1
                sp.wait_ge(ln_ok, 2 * TB * c + 2 * TB)
                load_ln(*(("ln1_g", "ln1_b") if c + 1 < NC else ("ln3_g", "ln3_b")))
            if stop is None:
                for tb in range(NTB):
                    sp.wait_ge(fin_ok, tb + 1)
                    sp.dma_start(out[0, tb * P:(tb + 1) * P, :], xcur[:, tb, :]).then_inc(out_land, 16)
            else:
                sp.wait_ge(fin_ok, 1)
                for tb in range(NTB):
                    sp.dma_start(out[0, tb * P:(tb + 1) * P, :], xcur[:, tb, :]).then_inc(out_land, 16)
            sp.wait_ge(out_land, 16 * NTB)

        @block.tensor
        def _(pe):
            order = iter(JOBS)

            def bank(name):
                assert next(order)[0] == name
                n = NUM[name]
                if n >= RB:
                    wait_emptied(pe, JOBS[n - RB][0])
                return psum[:, n % RB, :]

            def product(outp, pairs):
                for i, (l, r) in enumerate(pairs):
                    last = pe.matmul(outp, l, r, start=(i == 0), stop=(i == len(pairs) - 1))
                return last

            def transposed(name, src, c, stat, first):
                for k in range(KD):
                    b = bank((name, c, k))
                    if k == 0:
                        first()
                    for tb in range(TB):
                        last = pe.transpose(b[:, tb * P:(tb + 1) * P], src[:, c * TB + tb, k * P:(k + 1) * P], ident)
                    last.then_inc(pe_done, 1)

            pe.wait_ge(c_land, 16)
            for c in range(NC):
                if c == 0:
                    pe.wait_ge(rows_ok, 1)
                    pe.transpose(bank(("cols",))[:, 0:69], rows[0:69, :], ident[0:69, 0:69]).then_inc(pe_done, 1)
                transposed("xT", xcur, c, None, lambda: pe.wait_ge(x_land, 16 * (c + 1)))
                if c == 0:
                    pe.wait_ge(mem_land, 16)
                    for kk in range(KD // 2):
                        b = bank(("memT", kk))
                        for i in range(2):
                            for mb in range(MB):
                                k = 2 * kk + i
                                last = pe.transpose(b[:, i * M_MEM + mb * P:i * M_MEM + (mb + 1) * P],
                                                    mem_nat[:, mb, k * P:(k + 1) * P], ident)
                        last.then_inc(pe_done, 1)
                    pe.wait_ge(keys_land, 32)
                    b = bank(("keysT",))
                    for i in range(2):
                        last = pe.transpose(b[:, i * NK:(i + 1) * NK], keys_nat[:, i], ident)
                    last.then_inc(pe_done, 1)
                wait_emptied(pe, ("xT", c, KD - 1))
                w = wslot("u%d" % c, KD, SW)
                wait_piece(pe, "u%d" % c)
                for n in range(4):
                    b = bank(("u", c, n))
                    product(b[:, 0:TC], [(w[:, k, n * P:(n + 1) * P], actT[:, k, :]) for k in range(KD)]).then_inc(pe_done, 1)
                w = wslot("ckr%d" % c, KD, KVL + ROPE)
                wait_piece(pe, "ckr%d" % c)
                b = bank(("kr", c))
                product(b[0:ROPE, 0:TC], [(w[:, k, KVL:KVL + ROPE], actT[:, k, :]) for k in range(KD)]).then_inc(pe_done, 1)
                for n in range(2):
                    b = bank(("ckv", c, n))
                    product(b[:, 0:TC], [(w[:, k, n * P:(n + 1) * P], actT[:, k, :]) for k in range(KD)]).then_inc(pe_done, 1)
                w = wslot("cq%d" % c, KD, QL)
                wait_piece(pe, "cq%d" % c)
                for n in range(3):
                    b = bank(("cq", c, n))
                    product(b[:, 0:TC], [(w[:, k, n * P:(n + 1) * P], actT[:, k, :]) for k in range(KD)]).then_inc(pe_done, 1)
                b = bank(("krot", c))
                wait_emptied(pe, ("kr", c))
                pe.matmul(b[:, 0:TC], rep, kraw[0:ROPE, :], start=True, stop=True)
                pe.matmul(b[:, TC:2 * TC], reprot, kraw[0:ROPE, :], start=True, stop=True).then_inc(pe_done, 1)
                if c == 0:
                    pe.wait_ge(bt_ok, 1)
                    for nm, src in (("BT", bbpad), ("CT", cdup)):
                        for i in range(2):
                            b = bank((nm, i))
                            for q in range(4):
                                last = pe.transpose(b[:, q * P:(q + 1) * P], src[:, i, q, :], ident)
                            last.then_inc(pe_done, 1)
                b = bank(("ss", c))
                pe.wait_ge(sq_ok, 5 * (c + 1))
                pe.wait_ge(fills, 3)
                product(b[:, 0:TC], [(ones, sq5[:, n, :]) for n in (0, 1)])
                product(b[:, TC:2 * TC], [(ones, sq5[:, n, :]) for n in (2, 3, 4)]).then_inc(pe_done, 1)
                pe.wait_ge(c_ok, 5 * (c + 1))
                pe.wait_ge(uqkv_land, 16 * 10)
                for g in range(2):
                    b = bank(("qrope", c, g))
                    product(b[:, 0:TC], [(uq_r[:, k, g * P:(g + 1) * P], cT[:, 2 + k, :]) for k in range(3)]).then_inc(pe_done, 1)
                b = bank(("qrot", c))
                wait_emptied(pe, ("qrope", c, 1))
                for g in range(2):
                    last = pe.matmul(b[:, g * TC:(g + 1) * TC], rot, qraw[:, g, :], start=True, stop=True)
                last.then_inc(pe_done, 1)
                for i in range(4):
                    b = bank(("qn", c, i))
                    product(b[:, 0:TC], [(uq_n[:, k, i * P:(i + 1) * P], cT[:, 2 + k, :]) for k in range(3)]).then_inc(pe_done, 1)
                for i in range(4):
                    b = bank(("kn", c, i))
                    product(b[:, 0:TC], [(ukv_n[:, k, i * P:(i + 1) * P], cT[:, k, :]) for k in range(2)]).then_inc(pe_done, 1)
                for tb in range(TB):
                    b = bank(("v", c, tb))
                    product(b, [(cT[:, k, tb * P:(tb + 1) * P], ukv_v[:, k, :]) for k in range(2)]).then_inc(pe_done, 1)

                def bu(j):
                    b = bank(("bu", c, j))
                    q, r = j // 4, j % 4
                    for i in range(2):
                        last = pe.matmul(b[:, i * TC:(i + 1) * TC], BT[32 * r:32 * r + 32, i, q, :],
                                         uT[32 * r:32 * r + 32, q, :], start=True, stop=True)
                    last.then_inc(pe_done, 1)

                def score(i):
                    h, qb = i // TB, i % TB
                    keys = (c * TB + qb + 1) * P
                    b = bank(("sc", c, i))
                    pe.matmul(b[:, 0:keys], qT[0:DQ, h, qb * P:(qb + 1) * P], kT[0:DQ, h, 0:keys],
                              start=True, stop=True).then_inc(pe_done, 1)

                def mem_kv(i):
                    b = bank(("mem", i))
                    if i % 4 == 0 or i == 10:
                        wait_piece(pe, {0: "xk0", 4: "xk1", 8: "xv0", 10: "xv1"}[i])
                    if i < 8:
                        w = wslot("xk%d" % (i // 4), KD, 512)
                        product(b[:, 0:M_MEM], [(w[:, k, (i % 4) * P:(i % 4 + 1) * P], memT[:, k, :]) for k in range(KD)]).then_inc(pe_done, 1)
                    else:
                        half, mb = (i - 8) // 2, i % 2
                        w = wslot("xv%d" % half, KD, 512)
                        product(b, [(memT[:, k, mb * P:(mb + 1) * P], w[:, k, :]) for k in range(KD)]).then_inc(pe_done, 1)

                if c == 0:
                    wait_emptied(pe, ("BT", 1))
                    wait_emptied(pe, ("CT", 1))
                bu(0)
                pe.wait_ge(q_ok, 2 * (c + 1))
                wait_emptied(pe, ("v", c, TB - 1))
                score(0)
                for j in range(JT):
                    if c == 0 and j < 12:
                        mem_kv(j)
                    if j + 1 < JT:
                        bu(j + 1)
                    h, qb = j // TB, j % TB
                    qg = c * TB + qb
                    b = bank(("PT", c, j))
                    pe.wait_ge(pn, c * JT + j + 1)
                    for kb in range(qg + 1):
                        last = pe.transpose(b[:, kb * P:(kb + 1) * P], Pq[:, j % 2, kb * P:(kb + 1) * P], ident)
                    last.then_inc(pe_done, 1)
                    if j % 4 == 3:
                        b = bank(("pv", c, j // 4))
                        wait_emptied(pe, ("PT", c, j))
                        for hh in range(2):
                            hd = 2 * (j // 4) + hh
                            for kb in range((c + 1) * TB):
                                q0 = max(0, kb - c * TB) * P
                                last = pe.matmul(b[64 * hh:64 * hh + 64, q0:TC], V[:, kb, hd * VH:(hd + 1) * VH],
                                                 PT[:, hd % 2, kb, q0:TC], start=(kb == 0), stop=(kb == (c + 1) * TB - 1))
                        last.then_inc(pe_done, 1)
                    if j + 1 < JT:
                        score(j + 1)
                    q, r = j // 4, j % 4
                    yb = psum[:, 6 + q % 2, 0:TC]
                    pe.wait_ge(st_ok, c * JT + j + 1)
                    if r == 0 and 4 * c + q >= 2:
                        pe.wait_ge(y_ok, 4 * c + q - 1)
                    product(yb[32 * r:32 * r + 32, :],
                            [(CT[:, i, j, :], sS[:, j % 2, i, :]) for i in range(2)]).then_inc(y_mm, 1)
                w = wslot("glu%d" % c, 4, SW)
                wait_piece(pe, "glu%d" % c)
                pe.wait_ge(gl_dve, 4 * c + 3)
                for n in range(4):
                    b = bank(("glu", c, n))
                    product(b[:, 0:TC], [(w[:, k, n * P:(n + 1) * P], yT[:, k, :]) for k in range(4)]).then_inc(pe_done, 1)
                b = bank(("ms", c))
                pe.wait_ge(sqm, 2 * (c + 1))
                for s, sqs in enumerate((Pr, g1)):
                    sv = sqs.rearrange("p (n t) -> p n t", n=4)
                    for tb in range(TB):
                        last = product(b[:, 2 * s + tb:2 * s + tb + 1], [(sv[:, n, tb * P:(tb + 1) * P], ones[:, 0:1]) for n in range(4)])
                last.then_inc(pe_done, 1)
                pe.wait_ge(mixin, c + 1)
                for half in range(2):
                    nm = "wo%d%d" % (half, c)
                    w = wslot(nm, KD, 512)
                    wait_piece(pe, nm)
                    for tb in range(TB):
                        b = bank(("mixA", c, half, tb))
                        product(b, [(oT[:, n, tb * P:(tb + 1) * P], w[:, n, :]) for n in range(4)]).then_inc(pe_done, 1)
                        b = bank(("mixB", c, half, tb))
                        product(b, [(yT[:, n, tb * P:(tb + 1) * P], w[:, 4 + n, :]) for n in range(4)]).then_inc(pe_done, 1)
                transposed("x1T", xcur, c, None, lambda: pe.wait_ge(ln_ok, 2 * TB * c + TB))
                wait_emptied(pe, ("x1T", c, KD - 1))
                for n in range(8):
                    if n % 4 == 0:
                        nm = "xq%d%d" % (n // 4, c)
                        w = wslot(nm, KD, 512)
                        wait_piece(pe, nm)
                    b = bank(("qx", c, n))
                    product(b[:, 0:TC], [(w[:, k, (n % 4) * P:(n % 4 + 1) * P], actT[:, k, :]) for k in range(KD)]).then_inc(pe_done, 1)
                wait_emptied(pe, ("qx", c, 7))

                def xscore(i):
                    h, tb = i // TB, i % TB
                    b = bank(("xs", c, i))
                    product(b[:, 0:M_MEM], [(qTx[:, 2 * h + dc, tb * P:(tb + 1) * P], kTx[:, 2 * h + dc, :]) for dc in range(2)]).then_inc(pe_done, 1)

                xscore(0)
                for i in range(XH * TB):
                    if i + 1 < XH * TB:
                        xscore(i + 1)
                    b = bank(("xPT", c, i))
                    pe.wait_ge(xpn, c * XH * TB + i + 1)
                    for mb in range(MB):
                        last = pe.transpose(b[:, mb * P:(mb + 1) * P], Px[:, i % 2, mb * P:(mb + 1) * P], ident)
                    last.then_inc(pe_done, 1)
                    if i % TB == TB - 1:
                        h = i // TB
                        wait_emptied(pe, ("xPT", c, i))
                        for dc in range(2):
                            b = bank(("ox", c, h, dc))
                            product(b[:, 0:TC], [(vx[:, mb, (2 * h + dc) * P:(2 * h + dc + 1) * P], PTx[:, h % 2, mb, :]) for mb in range(MB)]).then_inc(pe_done, 1)
                wait_emptied(pe, ("ox", c, XH - 1, 1))
                for half in range(2):
                    nm = "xo%d%d" % (half, c)
                    w = wslot(nm, KD, 512)
                    wait_piece(pe, nm)
                    for tb in range(TB):
                        b = bank(("xo", c, half, tb))
                        product(b, [(oTx[:, n, tb * P:(tb + 1) * P], w[:, n, :]) for n in range(KD)]).then_inc(pe_done, 1)
                transposed("x2T", xcur, c, None, lambda: pe.wait_ge(ln_ok, 2 * TB * c + 2 * TB))
                wait_emptied(pe, ("x2T", c, KD - 1))
                for n in range(16):
                    if n % 4 == 0:
                        nm = "wq%d%d" % (n // 4, c)
                        w = wslot(nm, KD, 512)
                        wait_piece(pe, nm)
                    b = bank(("qq", c, n))
                    product(b[:, 0:TC], [(w[:, k, (n % 4) * P:(n % 4 + 1) * P], actT[:, k, :]) for k in range(KD)]).then_inc(pe_done, 1)
                wait_emptied(pe, ("qq", c, 15))
                for tb in range(TB):
                    for g in range(4):
                        b = bank(("ks", c, tb, g))
                        for i in range(4):
                            n = 4 * g + i
                            last = pe.matmul(b[:, i * NK:(i + 1) * NK], qTq[:, n, tb * P:(tb + 1) * P],
                                             keysT[:, (n % 2) * NK:(n % 2 + 1) * NK], start=True, stop=True)
                        last.then_inc(pe_done, 1)
            if stop is not None:
                return
            pe.wait_ge(y_ok, 4 * NC)
            for tb in range(NTB):
                if tb:
                    pe.wait_ge(peer_out, tb)
                first_group = True
                for peeled in (True, False):
                    def body(i, first):
                        for p in range(2):
                            pe.wait_ge(diag_ok, i * 2 + (16 * tb + p + 1))
                            for s in range(NG):
                                pe.wait_ge(v_land[s], i * 32 + (16 * (16 * tb + p + 1)))
                                st = first and p == 0 and s == 0
                                pe.matmul(psum[:, 6, :], diag[:, p, s, :], vbuf[s][:, 0:512], start=st, stop=False, skip_group_check=True)
                                pe.matmul(psum[:, 7, :], diag[:, p, s, :], vbuf[s][:, 512:1024], start=st, stop=False,
                                          skip_group_check=True).then_inc(v_free, 1)
                    if peeled:
                        body(0, True)
                    else:
                        with pe.Fori(1, 8) as i:
                            body(i, False)

        @block.scalar
        def _(act):
            chain = [0]

            def step(ins):
                ins.then_inc(act_c, 1)
                chain[0] += 1
                act.wait_ge(act_c, chain[0])

            order = iter([n for n, e in JOBS if e == "act"])

            def take(name, ops):
                assert next(order) == name, name
                wait_job(act, name)
                b = bank_of(name)
                last = ops(b)
                last.then_inc(emptied["act"], 1)

            def copy(dst, src):
                return act.copy(dst, src)

            lr, li, dtl, dt, mag, cosr, sinr, absr = par[0:8]
            act.wait_ge(par_dve, 1)
            act.activation(dt, cols[:, 32:48], ACT.Exp).then_inc(par_act, 1)
            act.wait_ge(par_dve, 2)
            act.activation(mag, par[8], ACT.Exp).then_inc(par_act, 1)
            act.wait_ge(par_dve, 3)
            act.wait_ge(fills, 3)
            act.activation(sinr, par[9], ACT.Sin).then_inc(par_act, 1)
            step(act.activation(absr, par[9], ACT.Abs))
            act.activation(cosr, absr, ACT.Sin, scale=-1.0, bias=kc[:, 2:3]).then_inc(par_act, 1)
            act.wait_ge(par_dve, 4)
            f = ang[:, 0:512]
            act.activation(trig_t[:, 512:1024], f, ACT.Sin, scale=6.283185).then_inc(trig_ok, 1)
            step(act.activation(ang[:, 512:1024], f, ACT.Abs))
            act.activation(trig_t[:, 0:512], ang[:, 512:1024], ACT.Sin, scale=-6.283185, bias=kc[:, 2:3]).then_inc(trig_ok, 1)
            act.wait_ge(par_dve, 5)
            f = ang[:, 1024:1536]
            act.activation(ropeS, f, ACT.Sin).then_inc(trig_ok, 1)
            step(act.activation(ang[:, 1536:2048], f, ACT.Abs))
            act.activation(ropeC, ang[:, 1536:2048], ACT.Sin, scale=-1.0, bias=kc[:, 2:3]).then_inc(trig_ok, 1)

            for c in range(NC):
                tok = slice(c * TC, (c + 1) * TC)
                if c:
                    wait_job(act, ("qq", c - 1, 15))
                for k in range(KD):
                    take(("xT", c, k), lambda b: copy(actT[:, k, :], b[:, 0:TC]))
                if c == 0:
                    for kk in range(KD // 2):
                        take(("memT", kk), lambda b: copy(memT[:, 2 * kk:2 * kk + 2, :], b.rearrange("p (i m) -> p i m", i=2)))
                    take(("keysT",), lambda b: copy(keysT[:, :], b[:, 0:2 * NK]))
                    act.wait_ge(trig_ok, 4)
                    act.wait_ge(bt_ok, 1)
                else:
                    act.wait_ge(route_ok, TB * c)
                for n in range(4):
                    take(("u", c, n), lambda b: copy(uT[:, n, :], b[:, 0:TC]))
                take(("kr", c), lambda b: copy(kraw[0:ROPE, :], b[0:ROPE, 0:TC]))
                for n in range(5):
                    def ops(b):
                        act.activation(sq5[:, n, :], b[:, 0:TC], ACT.Square).then_inc(sq_ok, 1)
                        return copy(cT[:, n, :], b[:, 0:TC])
                    take(("ckv", c, n) if n < 2 else ("cq", c, n - 2), ops)
                if c == 0:
                    for i in range(2):
                        take(("BT", i), lambda b: copy(BT[:, i], b.rearrange("p (q m) -> p q m", q=4)))
                    for i in range(2):
                        take(("CT", i), lambda b: act.mul(CT[:, i], b.rearrange("p (j h) -> p j h", h=32), -1.0 if i else 1.0))

                def ops(b):
                    act.activation(rms[:, 0:TC], b[:, 0:TC], ACT.Sqrt, scale=1.0 / KVL, bias=kc[:, 0:1])
                    last = act.activation(rms[:, TC:2 * TC], b[:, TC:2 * TC], ACT.Sqrt, scale=1.0 / QL, bias=kc[:, 0:1])
                    return last
                take(("ss", c), ops)
                for g in range(2):
                    take(("qrope", c, g), lambda b: copy(qraw[:, g, :], b[:, 0:TC]))
                for i in range(4):
                    def ops(b):
                        copy(qT[0:NOPE, 2 * i, :], b[0:NOPE, 0:TC])
                        return copy(qT[0:NOPE, 2 * i + 1, :], b[NOPE:2 * NOPE, 0:TC])
                    take(("qn", c, i), ops)
                for i in range(4):
                    def ops(b):
                        copy(kT[0:NOPE, 2 * i, tok], b[0:NOPE, 0:TC])
                        return copy(kT[0:NOPE, 2 * i + 1, tok], b[NOPE:2 * NOPE, 0:TC])
                    take(("kn", c, i), ops)
                for tb in range(TB):
                    take(("v", c, tb), lambda b: copy(V[:, c * TB + tb, :], b))

                def exps(i):
                    keys = (c * TB + i % TB + 1) * P
                    act.wait_ge(smax, c * JT + i + 1)
                    if i == 0 and c == 0:
                        act.wait_ge(q_ok, 2)
                    if i >= 2:
                        wait_job(act, ("PT", c, i - 2))

                    def ops(b):
                        act.activation(Pq[:, i % 2, 0:keys], b[:, 0:keys], ACT.Exp, bias=nmax[:, i % 2:i % 2 + 1],
                                       scale=DQ ** -0.5, accum_out=rsum[:, i % 2:i % 2 + 1]).then_inc(pexp, 1)
                        return None
                    assert next(order) == ("sc", c, i)
                    wait_job(act, ("sc", c, i))
                    ops(bank_of(("sc", c, i)))
                    act.wait_ge(pexp, c * JT + i + 1)
                    act.sem_inc(emptied["act"], 1)

                exps(0)
                for j in range(JT):
                    if c == 0 and j < 12:
                        if j < 8:
                            take(("mem", j), lambda b: copy(kTx[:, j, :], b[:, 0:M_MEM]))
                        else:
                            half, mb = (j - 8) // 2, j % 2
                            take(("mem", j), lambda b: copy(vx[:, mb, 512 * half:512 * half + 512], b))
                    hd, qb = j // TB, j % TB
                    qg = c * TB + qb
                    if j % 4 == 0 and j:
                        wait_job(act, ("pv", c, j // 4 - 1))
                    take(("PT", c, j), lambda b: copy(PT[:, hd % 2, 0:qg + 1, qb * P:(qb + 1) * P],
                                                      b[:, 0:(qg + 1) * P].rearrange("p (k t) -> p k t", k=qg + 1)))
                    if j % 4 == 3:
                        take(("pv", c, j // 4), lambda b: copy(oT[:, j // 4, :], b[:, 0:TC]))
                    if j + 1 < JT:
                        exps(j + 1)
                act.wait_ge(y_ok, 4 * (c + 1))
                wait_job(act, ("pv", c, 3))
                act.activation(g1, scratch[:, 1024:2048], ACT.Square).then_inc(gl_act, 1)
                act.mul(g2, scratch[:, 1024:2048], 0.5).then_inc(gl_act, 1)
                act.wait_ge(gl_dve, 4 * c + 2)
                act.activation(g1, g1, ACT.Tanh, scale=GELU_C).then_inc(gl_act, 1)
                wait_emptied(act, ("pv", c, 3))
                act.activation(Pr, scratch[:, 2304:3328], ACT.Square).then_inc(sqm, 1)
                act.wait_ge(sqm, 2 * c + 1)
                for n in range(4):
                    step(act.mul(oT[:, n, :], oT[:, n, :], cols[:, 61 + n:62 + n]))
                act.wait_ge(gl_dve, 4 * c + 3)
                for n in range(4):
                    take(("glu", c, n), lambda b: act.activation(g1[:, n * TC:(n + 1) * TC], b[:, 0:TC], ACT.Tanh,
                                                                 scale=0.5, bias=kcol[:, n:n + 1]))
                act.wait_ge(gl_dve, 4 * c + 4)
                act.activation(g1, g2, ACT.Square, scale=0.5).then_inc(sqm, 1)
                for n in range(4):
                    last = act.mul(yT[:, n, :], g2[:, n * TC:(n + 1) * TC], kcol[:, 4 + n:5 + n])
                last.then_inc(mixin, 1)
                take(("ms", c), lambda b: act.activation(rsmix, b[:, 0:4], ACT.Sqrt, scale=1.0 / SW, bias=kc[:, 0:1]))

                def deviations(n):
                    for tb in range(TB):
                        act.wait_ge(var_ok, n + tb + 1)
                        act.activation(std[:, 0:1], mv[:, 1:2], ACT.Sqrt, bias=kc[:, 1:2]).then_inc(std_ok, 1)

                deviations(2 * TB * c)
                wait_job(act, ("pv", c, 3))
                for k in range(KD):
                    take(("x1T", c, k), lambda b: copy(actT[:, k, :], b[:, 0:TC]))
                for n in range(8):
                    take(("qx", c, n), lambda b: copy(qTx[:, n, :], b[:, 0:TC]))

                def xexps(i):
                    act.wait_ge(xsmax, c * XH * TB + i + 1)
                    if i >= 2:
                        wait_job(act, ("xPT", c, i - 2))
                    assert next(order) == ("xs", c, i)
                    b = bank_of(("xs", c, i))
                    wait_job(act, ("xs", c, i))
                    act.activation(Px[:, i % 2, :], b[:, 0:M_MEM], ACT.Exp, bias=nmax[:, 2 + i % 2:3 + i % 2], scale=1.0 / 16,
                                   accum_out=rsum[:, 2 + i % 2:3 + i % 2]).then_inc(xexp, 1)
                    act.wait_ge(xexp, c * XH * TB + i + 1)
                    act.sem_inc(emptied["act"], 1)

                xexps(0)
                for i in range(XH * TB):
                    if i + 1 < XH * TB:
                        xexps(i + 1)
                    h, tb = i // TB, i % TB
                    if tb == 0 and h >= 2:
                        wait_job(act, ("ox", c, h - 2, 1))
                    take(("xPT", c, i), lambda b: copy(PTx[:, h % 2, :, tb * P:(tb + 1) * P],
                                                       b[:, 0:M_MEM].rearrange("p (m t) -> p m t", m=MB)))
                    if tb == TB - 1:
                        for dc in range(2):
                            take(("ox", c, h, dc), lambda b: copy(oTx[:, 2 * h + dc, :], b[:, 0:TC]))
                deviations(2 * TB * c + TB)
                for k in range(KD):
                    take(("x2T", c, k), lambda b: copy(actT[:, k, :], b[:, 0:TC]))
                for n in range(16):
                    take(("qq", c, n), lambda b: copy(qTq[:, n, :], b[:, 0:TC]))
                for tb in range(TB):
                    if tb:
                        act.wait_ge(s_free, c * TB + tb)
                    for g in range(4):
                        take(("ks", c, tb, g), lambda b: copy(S1[:, g * 512:(g + 1) * 512], b))
                    act.wait_ge(rt_d, c * TB + tb + 1)
                    act.activation(tia, tia, ACT.Exp).then_inc(rt_a, 1)
            if stop is not None:
                return
            for tb in range(NTB + 1):
                if tb < NTB:
                    act.wait_ge(h_ok, tb + 1)
                    act.activation(gel[:, tb % 2, :], gel[:, tb % 2, :], ACT.Tanh, scale=GELU_C).then_inc(h_act, 1)
                if tb:
                    act.wait_ge(var_ok, 2 * TB * NC + tb)
                    act.activation(std[:, 0:1], mv[:, 1:2], ACT.Sqrt, bias=kc[:, 1:2]).then_inc(std_ok, 1)

        @block.gpsimd
        def _(pool):
            chain = [0]

            def step(ins):
                ins.then_inc(pool_c, 1)
                chain[0] += 1
                pool.wait_ge(pool_c, chain[0])

            pool.memset(ones, 1.0).then_inc(fills, 1)
            pool.memset(kc[:, 0:1], 1e-6)
            pool.memset(kc[:, 1:2], 1e-5)
            pool.memset(kc[:, 3:4], 0.0)
            pool.memset(kc[:, 2:3], math.pi / 2).then_inc(fills, 1)
            pool.memset(small[:, :], 0.0).then_inc(fills, 1)

            def scale_x(c, stage):
                last = ("xT", c, KD - 1) if stage == 0 else ("x1T", c, KD - 1)
                wait_job(pool, last)
                for tb in range(TB):
                    pool.tensor_scalar(xcur[:, c * TB + tb, :], xcur[:, c * TB + tb, :], ALPHA, 0.0, ALU.mult, ALU.add).then_inc(xscaled, 1)

            for c in range(NC):
                scale_x(c, 0)
                pool.wait_ge(trig_ok, 4)
                t1, t2 = pool_t[:, 0:TC].rearrange("p (a b) -> p a b", a=16), pool_t[:, TC:2 * TC].rearrange("p (a b) -> p a b", a=16)
                if c == 0:
                    pool.wait_ge(par_dve, 5)
                else:
                    pool.wait_ge(route_ok, TB * c)
                for j in range(JT):
                    if j >= 2:
                        pool.wait_ge(tab_used, c * JT + j - 1)
                    cb, ca = bc(trig[:, 0, j, 0:16], 1, 16), bc(trig[:, 0, j, 16:32], 2, 16)
                    sb_, sa = bc(trig[:, 1, j, 0:16], 1, 16), bc(trig[:, 1, j, 16:32], 2, 16)
                    o = tab[:, j % 2].rearrange("p i (a b) -> p i a b", a=16)
                    pool.tensor_tensor(o[:, 0], cb, ca, ALU.mult)
                    step(pool.tensor_tensor(t1, sb_, sa, ALU.mult))
                    pool.tensor_tensor(o[:, 0], o[:, 0], t1, ALU.subtract)
                    pool.tensor_tensor(o[:, 1], sb_, ca, ALU.mult)
                    step(pool.tensor_tensor(t2, cb, sa, ALU.mult))
                    pool.tensor_tensor(o[:, 1], o[:, 1], t2, ALU.add).then_inc(tab_ok, 1)
                    if j + 1 < JT:
                        pool.wait_ge(tab_ok, c * JT + j + 1)
                scale_x(c, 1)
            if stop is not None:
                return

            def stage(tab_i, tb, i, p):
                pool.tensor_copy(idstage[:, tab_i, p, :], ids_t[:, bass.ds(i * 16 + (tb * HK + p * 8), NG)]).then_inc(
                    (stage_u, stage_v)[tab_i], 1)

            def gather(tab_i, bufs, table, land, s, p):
                pool.nop(nofuse=True)
                pool.indirect_dma_start(bufs[s], None, table, bass.IndirectOffsetOnAxis(idstage[:, tab_i, p, s:s + 1], 0)).then_inc(land[s], 16)

            wait_job(pool, ("qq", NC - 1, 15))
            for tb in range(NTB + 1):
                if tb < NTB:
                    pool.wait_ge(route_ok, NTB)
                if tb:
                    pool.wait_ge(w_ok, tb)
                with pool.Fori(0, 8) as i:
                    for p in range(2):
                        if tb < NTB:
                            stage(0, tb, i, p)
                        if tb:
                            stage(1, tb - 1, i, p)
                        if tb < NTB:
                            pool.wait_ge(stage_u, i * 2 + (16 * tb + p + 1))
                        if tb:
                            pool.wait_ge(stage_v, i * 2 + (16 * (tb - 1) + p + 1))
                        for s in range(NG):
                            if tb < NTB:
                                pool.wait_ge(u_free, i * 16 + (HK * tb + 8 * p + s + 1 + NG))
                                gather(0, ubuf, a["u_tab"][0], u_land, s, p)
                            if tb:
                                pool.wait_ge(v_free, i * 16 + (HK * (tb - 1) + 8 * p + s + 1 + NG))
                                gather(1, vbuf, a["v_tab"][0], v_land, s, p)

        @block.vector
        def _(dve):
            chain = [0]

            def mark(ins):
                ins.then_inc(dve_c, 1)
                chain[0] += 1

            def settle():
                dve.wait_ge(dve_c, chain[0])

            def step(ins):
                mark(ins)
                settle()

            order = iter([n for n, e in JOBS if e == "dve"])

            def open_job(name):
                assert next(order) == name, name
                wait_job(dve, name)
                return bank_of(name)

            lr, li, dtl, dt, mag, cosr, sinr, absr, a1, red = par[0:10]
            k_, th, t0, t1, nr, ni, den, fre, fim, rden, rt, rhi, rlo = par[10:23]

            dve.wait_ge(par_land, 16 * 9)
            dve.tensor_copy(rows[32:48, :].rearrange("j (g q) -> j g q", g=2), bc(ldt[32:48, :], 2, NS)).then_inc(rows_ok, 1)
            b = open_job(("cols",))
            dve.tensor_copy(cols[:, 0:69], b[:, 0:69]).then_inc(emptied["dve"], 1)
            wait_emptied(dve, ("cols",))
            dve.tensor_copy(par[0], cols[:, 0:16])
            dve.tensor_copy(kcol[:, 0:4], cols[:, 57:61])
            step(dve.tensor_copy(par[1], cols[:, 16:32]))
            dve.tensor_scalar(kcol[:, 0:4], kcol[:, 0:4], 0.5, None, ALU.mult)
            dve.tensor_scalar(kcol[:, 4:8], cols[:, 65:69], 0.5, None, ALU.mult).then_inc(par_dve, 1)
            dve.wait_ge(par_act, 1)
            step(dve.tensor_tensor(th, li, dt, ALU.mult))
            dve.tensor_tensor(a1, lr, dt, ALU.mult).then_inc(par_dve, 1)

            def reduce_angle(dst, src, kbuf):
                step(dve.tensor_scalar(kbuf, src, INV2PI, MAGIC, ALU.mult, ALU.add))
                step(dve.tensor_scalar(kbuf, kbuf, -MAGIC, None, ALU.add))
                step(dve.scalar_tensor_tensor(out=dst, in0=kbuf, scalar=-C1, in1=src, op0=ALU.mult, op1=ALU.add))
                step(dve.scalar_tensor_tensor(out=dst, in0=kbuf, scalar=-C2, in1=dst, op0=ALU.mult, op1=ALU.add))
                step(dve.scalar_tensor_tensor(out=dst, in0=kbuf, scalar=-C3, in1=dst, op0=ALU.mult, op1=ALU.add))
                return dve.tensor_scalar(dst, dst, PI_IN, -PI_IN, ALU.min, ALU.max)

            reduce_angle(red, th, k_).then_inc(par_dve, 1)
            dve.wait_ge(par_dve, 3)
            step(dve.tensor_scalar(rt, red, INV2PI, None, ALU.mult))
            step(dve.tensor_scalar(rhi, rt, MAGIC / 2 ** 14, None, ALU.add))
            step(dve.tensor_scalar(rhi, rhi, -MAGIC / 2 ** 14, None, ALU.add))
            step(dve.tensor_tensor(rlo, rt, rhi, ALU.subtract))
            m3 = bc(mult32, 1, JT)
            fa = ang[:, 0:512].rearrange("p (j m) -> p j m", j=JT)
            fb = ang[:, 2048:2560].rearrange("p (j m) -> p j m", j=JT)
            fc = ang[:, 2560:3072].rearrange("p (j m) -> p j m", j=JT)
            dve.wait_ge(c_land, 16)
            step(dve.tensor_tensor(fa, m3, bc(rhi, 2, 32), ALU.mult))
            step(dve.tensor_scalar(fb, fa, MAGIC, None, ALU.add))
            step(dve.tensor_scalar(fb, fb, -MAGIC, None, ALU.add))
            step(dve.tensor_tensor(fa, fa, fb, ALU.subtract))
            step(dve.tensor_tensor(fc, m3, bc(rlo, 2, 32), ALU.mult))
            step(dve.tensor_tensor(fa, fa, fc, ALU.add))
            step(dve.tensor_scalar(fb, fa, MAGIC, None, ALU.add))
            step(dve.tensor_scalar(fb, fb, -MAGIC, None, ALU.add))
            dve.tensor_tensor(fa, fa, fb, ALU.subtract).then_inc(par_dve, 1)
            dve.wait_ge(pos_land, 16)
            posf = ang[:, 2048:2560]
            dve.wait_ge(par_dve, 4)
            step(dve.tensor_copy(posf, pos_i))
            step(dve.tensor_scalar(posf, posf, freq, None, ALU.mult))
            reduce_angle(ang[:, 1024:1536], posf, ang[:, 2560:3072]).then_inc(par_dve, 1)

            dve.wait_ge(par_act, 4)
            dve.wait_ge(bc_land, 64)
            step(dve.tensor_tensor(t0, mag, cosr, ALU.mult))
            step(dve.tensor_tensor(ni, mag, sinr, ALU.mult))
            step(dve.tensor_scalar(nr, t0, -1.0, None, ALU.add))
            dve.tensor_copy(magc, mag)
            step(dve.tensor_tensor(den, lr, lr, ALU.mult))
            step(dve.tensor_tensor(t1, li, li, ALU.mult))
            step(dve.tensor_tensor(den, den, t1, ALU.add))
            step(dve.reciprocal(rden, den))
            step(dve.tensor_tensor(fre, nr, lr, ALU.mult))
            step(dve.tensor_tensor(t0, ni, li, ALU.mult))
            step(dve.tensor_tensor(fre, fre, t0, ALU.add))
            step(dve.tensor_tensor(fre, fre, rden, ALU.mult))
            step(dve.tensor_tensor(fim, ni, lr, ALU.mult))
            step(dve.tensor_tensor(t1, nr, li, ALU.mult))
            step(dve.tensor_tensor(fim, fim, t1, ALU.subtract))
            step(dve.tensor_tensor(fim, fim, rden, ALU.mult))
            fr, fi = bc(fre, 2, GC), bc(fim, 2, GC)
            dve.tensor_tensor(bbw[:, 0], bnat[:, 0], fr, ALU.mult)
            dve.tensor_tensor(bbw[:, 1], bnat[:, 1], fi, ALU.mult)
            dve.tensor_tensor(bbw[:, 2], bnat[:, 1], fr, ALU.mult)
            step(dve.tensor_tensor(bbw[:, 3], bnat[:, 0], fi, ALU.mult))
            step(dve.memset(bbpad, 0.0))
            for i, op in enumerate((ALU.subtract, ALU.add)):
                for g in range(2):
                    ps = slice(64 * g, 64 * g + 64)
                    o = bbpad[ps, i].rearrange("p q (r g h) -> p q r g h", g=2, h=GC)[:, :, :, g, :]
                    x0 = bbw[ps, 2 * i].rearrange("p (q r) h -> p q r h", r=4)
                    x1 = bbw[ps, 2 * i + 1].rearrange("p (q r) h -> p q r h", r=4)
                    mark(dve.tensor_tensor(o, x0, x1, op))
            for i in range(2):
                for q in range(4):
                    last = dve.tensor_tensor(cdup[:, i, q, :].rearrange("p (g s) -> p g s", g=2), bc(cnat[:, i, q, :], 1, 2),
                                             parity.rearrange("p (g s) -> p g s", g=2), ALU.mult)
            last.then_inc(bt_ok, 1)

            ln_count = [0]

            def layer_norm(tb, ln_value, signal):
                z = xcur[:, tb, :]
                for i in range(2):
                    mark(dve.bn_stats(st6[:, i, :], z[:, 512 * i:512 * i + 512]))
                settle()
                dve.bn_aggr(mv, st6).then_inc(var_ok, 1)
                ln_count[0] += 1
                dve.wait_ge(std_ok, ln_count[0])
                step(dve.reciprocal(std[:, 1:2], std[:, 0:1]))
                step(dve.tensor_scalar(z, z, mv[:, 0:1], std[:, 1:2], ALU.subtract, ALU.mult))
                dve.wait_ge(ln_land, ln_value)
                step(dve.tensor_tensor(z, z, lngb[:, 0:D], ALU.mult))
                dve.tensor_tensor(z, z, lngb[:, D:2 * D], ALU.add).then_inc(signal, 1)

            for c in range(NC):
                tok = slice(c * TC, (c + 1) * TC)
                b = open_job(("krot", c))
                dve.wait_ge(trig_ok, 4)
                rr = slice(64, 96)
                mark(dve.tensor_tensor(kt1[rr, :], b[rr, 0:TC], ropeC[rr, tok], ALU.mult))
                dve.tensor_tensor(kt2[rr, :], b[rr, TC:2 * TC], ropeS[rr, tok], ALU.mult).then_inc(emptied["dve"], 1)
                settle()
                wait_emptied(dve, ("krot", c))
                if c == 0:
                    wait_job(dve, ("CT", 1))
                dve.tensor_tensor(kT[rr, :, tok], bc(kt1[rr, :], 1, H), bc(kt2[rr, :], 1, H), ALU.add).then_inc(q_ok, 1)
                wait_emptied(dve, ("ss", c))
                step(dve.reciprocal(rms, rms))
                for n in range(5):
                    r_ = rms[:, 0:TC] if n < 2 else rms[:, TC:2 * TC]
                    dve.scalar_tensor_tensor(out=cT[:, n, :], in0=cT[:, n, :], scalar=cols[:, 48 + n:49 + n], in1=r_,
                                             op0=ALU.mult, op1=ALU.mult).then_inc(c_ok, 1)
                b = open_job(("qrot", c))
                mark(dve.tensor_tensor(qtmp, b.rearrange("p (g t) -> p g t", g=2), bc(ropeS[:, tok], 1, 2), ALU.mult))
                settle()
                dve.sem_inc(emptied["dve"], 1)
                step(dve.tensor_tensor(qraw, qraw, bc(ropeC[:, tok], 1, 2), ALU.mult))
                for g in range(2):
                    for i in range(4):
                        ps = slice(32 * i, 32 * i + 32)
                        last = dve.tensor_tensor(qT[rr, 4 * g + i, :], qraw[ps, g, :], qtmp[ps, g, :], ALU.add)
                last.then_inc(q_ok, 1)

                def row_max(i):
                    keys = (c * TB + i % TB + 1) * P
                    wait_job(dve, ("sc", c, i))
                    b = bank_of(("sc", c, i))
                    step(dve.tensor_tensor(b[:, keys - P:keys], b[:, keys - P:keys], causal, ALU.add))
                    step(dve.tensor_reduce(gsum[:, 0:1], b[:, 0:keys], AX.X, ALU.max, negate=True))
                    dve.tensor_scalar(nmax[:, i % 2:i % 2 + 1], gsum[:, 0:1], DQ ** -0.5, None, ALU.mult).then_inc(smax, 1)

                for j in range(JT):
                    row_max(j)
                    b = open_job(("bu", c, j)).rearrange("p (i t) -> p i t", i=2)
                    dve.wait_ge(tab_ok, c * JT + j + 1)
                    cs, sn = bc(tab[:, j % 2, 0, :], 1, 2), bc(tab[:, j % 2, 1, :], 1, 2)
                    mark(dve.tensor_tensor(sA, b, cs, ALU.mult))
                    mark(dve.tensor_tensor(sB, b, sn, ALU.mult))
                    settle()
                    dve.sem_inc(emptied["dve"], 1)
                    mark(dve.tensor_tensor(sW[:, 0], sA[:, 0], sB[:, 1], ALU.add))
                    mark(dve.tensor_tensor(sW[:, 1], sA[:, 1], sB[:, 0], ALU.subtract))
                    settle()
                    for i in range(2):
                        mark(dve.tensor_tensor_scan(sR[:, i, :], magc[:, j:j + 1].to_broadcast([P, TC]), sW[:, i, :],
                                                    0.0 if c == 0 else carry[:, j, i:i + 1], ALU.mult, ALU.add))
                    settle()
                    keys = (c * TB + j % TB + 1) * P
                    dve.wait_ge(pexp, c * JT + j + 1)
                    step(dve.reciprocal(gsum[:, 1:2], rsum[:, j % 2:j % 2 + 1]))
                    dve.tensor_scalar(Pq[:, j % 2, 0:keys], Pq[:, j % 2, 0:keys], gsum[:, 1:2], None, ALU.mult).then_inc(pn, 1)
                    mark(dve.tensor_tensor(sA, sR, cs, ALU.mult))
                    mark(dve.tensor_tensor(sB, sR, sn, ALU.mult))
                    settle()
                    dve.sem_inc(tab_used, 1)
                    if c * JT + j >= 2:
                        dve.wait_ge(y_mm, c * JT + j - 1)
                    mark(dve.tensor_tensor(sS[:, j % 2, 0, :], sA[:, 0], sB[:, 1], ALU.subtract))
                    mark(dve.tensor_tensor(sS[:, j % 2, 1, :], sA[:, 1], sB[:, 0], ALU.add))
                    settle()
                    dve.tensor_copy(carry[:, j, :], sS[:, j % 2, :, TC - 1]).then_inc(st_ok, 1)
                    if j % 4 == 3:
                        q = j // 4
                        dve.wait_ge(y_mm, c * JT + j + 1)
                        dve.scalar_tensor_tensor(out=yT[:, q, :], in0=uT[:, q, :], scalar=cols[:, 53 + q:54 + q],
                                                 in1=psum[:, 6 + q % 2, 0:TC], op0=ALU.mult, op1=ALU.add).then_inc(y_ok, 1)
                dve.wait_ge(gl_act, 3 * c + 1)
                dve.tensor_scalar(g1, g1, 0.044715, 1.0, ALU.mult, ALU.add).then_inc(gl_dve, 1)
                dve.wait_ge(gl_dve, 4 * c + 1)
                yTf = scratch[:, 1024:2048]
                dve.tensor_tensor(g1, g1, yTf, ALU.mult).then_inc(gl_dve, 1)
                dve.wait_ge(gl_act, 3 * c + 3)
                dve.scalar_tensor_tensor(out=yTf, in0=g1, scalar=1.0, in1=g2, op0=ALU.add, op1=ALU.mult).then_inc(gl_dve, 1)
                wait_emptied(dve, ("glu", c, 3))
                dve.wait_ge(gl_dve, 4 * c + 3)
                dve.scalar_tensor_tensor(out=g2, in0=g1, scalar=1.0, in1=yTf, op0=ALU.add, op1=ALU.mult).then_inc(gl_dve, 1)
                wait_emptied(dve, ("ms", c))
                step(dve.reciprocal(rsmix, rsmix))
                dve.wait_ge(xscaled, TB * (2 * c + 1))
                for half in range(2):
                    for tb in range(TB):
                        z = xcur[:, c * TB + tb, 512 * half:512 * half + 512]
                        for s, nm in enumerate(("mixA", "mixB")):
                            b = open_job((nm, c, half, tb))
                            dve.scalar_tensor_tensor(out=z, in0=b, scalar=rsmix[:, 2 * s + tb:2 * s + tb + 1], in1=z,
                                                     op0=ALU.mult, op1=ALU.add).then_inc(emptied["dve"], 1)
                            wait_emptied(dve, (nm, c, half, tb))
                for tb in range(TB):
                    layer_norm(c * TB + tb, 32 * (2 * c + 1), ln_ok)
                for i in range(XH * TB):
                    wait_job(dve, ("xs", c, i))
                    b = bank_of(("xs", c, i))
                    step(dve.tensor_reduce(gsum[:, 2:3], b[:, 0:M_MEM], AX.X, ALU.max, negate=True))
                    dve.tensor_scalar(nmax[:, 2 + i % 2:3 + i % 2], gsum[:, 2:3], 1.0 / 16, None, ALU.mult).then_inc(xsmax, 1)
                    dve.wait_ge(xexp, c * XH * TB + i + 1)
                    step(dve.reciprocal(gsum[:, 3:4], rsum[:, 2 + i % 2:3 + i % 2]))
                    dve.tensor_scalar(Px[:, i % 2, :], Px[:, i % 2, :], gsum[:, 3:4], None, ALU.mult).then_inc(xpn, 1)
                dve.wait_ge(xscaled, TB * (2 * c + 2))
                for half in range(2):
                    for tb in range(TB):
                        z = xcur[:, c * TB + tb, 512 * half:512 * half + 512]
                        b = open_job(("xo", c, half, tb))
                        dve.tensor_tensor(z, b, z, ALU.add).then_inc(emptied["dve"], 1)
                        wait_emptied(dve, ("xo", c, half, tb))
                for tb in range(TB):
                    layer_norm(c * TB + tb, 32 * (2 * c + 2), ln_ok)
                for tb in range(TB):
                    tg = c * TB + tb
                    wait_emptied(dve, ("ks", c, tb, 3))
                    for n in range(2 * PH):
                        s0 = S1[:, n * NK:(n + 1) * NK]
                        s1 = S2[:, n * NK:(n + 1) * NK]
                        mark(dve.max(rv[:, 16 * n:16 * n + 8], s0))
                        settle()
                        mark(dve.max_index(ridx[:, 16 * n:16 * n + 8], rv[:, 16 * n:16 * n + 8], s0))
                        step(dve.match_replace(s1, rv[:, 16 * n:16 * n + 8], s0, -3e38))
                        step(dve.max(rv[:, 16 * n + 8:16 * n + 16], s1))
                        mark(dve.max_index(ridx[:, 16 * n + 8:16 * n + 16], rv[:, 16 * n + 8:16 * n + 16], s1))
                    settle()
                    mark(dve.tensor_copy(rif, ridx))
                    rvv = rv.rearrange("p (h s k) -> p h s k", h=PH, s=2)
                    cand = S1.rearrange("p (h a b) -> p h a b", h=PH, a=TOPK)
                    step(dve.tensor_tensor(cand, bc(rvv[:, :, 0, :], 3, TOPK), bc(rvv[:, :, 1, :], 2, TOPK), ALU.add))
                    for h in range(PH):
                        s0 = S1[:, h * 256:(h + 1) * 256]
                        s1 = S2[:, h * 256:(h + 1) * 256]
                        step(dve.max(tops[:, 16 * h:16 * h + 8], s0))
                        mark(dve.max_index(tpos[:, 16 * h:16 * h + 8], tops[:, 16 * h:16 * h + 8], s0))
                        step(dve.match_replace(s1, tops[:, 16 * h:16 * h + 8], s0, -3e38))
                        step(dve.max(tops[:, 16 * h + 8:16 * h + 16], s1))
                        mark(dve.max_index(tpos[:, 16 * h + 8:16 * h + 16], tops[:, 16 * h + 8:16 * h + 16], s1))
                    settle()
                    mark(dve.tensor_scalar(tau, tpos, 4, None, ALU.logical_shift_right))
                    step(dve.tensor_scalar(tbu, tpos, 15, None, ALU.bitwise_and))
                    mark(dve.tensor_copy(tab_a, tau))
                    step(dve.tensor_copy(tab_b, tbu))
                    rifv = rif.rearrange("p (h s k) -> p h s k", h=PH, s=2)
                    for s, place, dst in ((0, tab_a, tia), (1, tab_b, tib)):
                        e = (S1, S2)[s].rearrange("p (h k m) -> p h k m", h=PH, k=TOPK)
                        pl = bc(place.rearrange("p (h k) -> p h k", h=PH), 3, TOPK)
                        io = bc(bc(iota16, 1, TOPK), 1, PH)
                        step(dve.tensor_tensor(e, pl, io, ALU.is_equal))
                        step(dve.tensor_tensor(e, e, bc(rifv[:, :, s, :], 2, TOPK), ALU.mult))
                        step(dve.tensor_reduce(dst, e, AX.X, ALU.add))
                    idv = ids_t[:, tg * HK:(tg + 1) * HK]
                    step(dve.scalar_tensor_tensor(out=idv, in0=tia, scalar=float(NK), in1=tib, op0=ALU.mult, op1=ALU.add))
                    tv = tops.rearrange("p (h k) -> p h k", h=PH)
                    dve.tensor_tensor(tia.rearrange("p (h k) -> p h k", h=PH), tv, bc(tv[:, :, 0], 2, TOPK), ALU.subtract).then_inc(rt_d, 1)
                    dve.wait_ge(rt_a, tg + 1)
                    step(dve.tensor_reduce(gsum[:, 0:8], tia.rearrange("p (h k) -> p h k", h=PH), AX.X, ALU.add))
                    step(dve.reciprocal(gsum[:, 0:8], gsum[:, 0:8]))
                    step(dve.tensor_tensor(gates_t[:, tg * HK:(tg + 1) * HK].rearrange("p (h k) -> p h k", h=PH),
                                           tia.rearrange("p (h k) -> p h k", h=PH), bc(gsum[:, 0:8], 2, TOPK), ALU.mult))
                    dve.sem_inc(s_free, 1)
                    dve.sem_inc(route_ok, 1)
            if stop is not None:
                dve.wait_ge(xscaled, TB * 2 * NC)
                dve.sem_inc(fin_ok, 1)
                return

            dve.sem_inc(u_free, 2 * NG)
            dve.sem_inc(v_free, 2 * NG)
            for tb in range(NTB + 1):
                with dve.Fori(0, 8) as i:
                    for p in range(2):
                        if tb:
                            dve.tensor_copy(w8[:, p, :], wbuf[:, (tb - 1) % 2, bass.ds(i * 16 + 8 * p, NG)]).then_inc(w8_ok, 1)
                            dve.wait_ge(w8_ok, i * 2 + (16 * (tb - 1) + p + 1))
                            dve.wait_ge(v_free, i * 16 + (HK * (tb - 1) + 8 * p + NG))
                            dve.tensor_tensor(diag[:, p], bc(ident, 1, NG), bc(w8[:, p, :], 2, P), ALU.mult).then_inc(diag_ok, 1)
                        if tb < NTB:
                            for s in range(NG):
                                dve.wait_ge(u_land[s], i * 32 + 16 * (16 * tb + p + 1))
                                dve.tensor_tensor_reduce(out=ubuf[s], in0=ubuf[s], in1=xcur[:, tb, :], scale=1.0, scalar=0.0,
                                                         op0=ALU.mult, op1=ALU.add, accum_out=h8[:, p, s:s + 1]).then_inc(u_free, 1)
                            dve.wait_ge(u_free, i * 16 + (HK * tb + 8 * p + 8 + 2 * NG))
                            dve.tensor_copy(hbuf[:, tb % 2, bass.ds(i * 16 + 8 * p, NG)], h8[:, p, :]).then_inc(h8_ok, 1)
                            dve.wait_ge(h8_ok, i * 2 + (16 * tb + p + 1))
                if tb < NTB:
                    h_, g_, w_ = hbuf[:, tb % 2, :], gel[:, tb % 2, :], wbuf[:, tb % 2, :]
                    step(dve.tensor_tensor(g_, h_, h_, ALU.mult))
                    step(dve.tensor_scalar(g_, g_, 0.044715, 1.0, ALU.mult, ALU.add))
                    dve.tensor_tensor(g_, g_, h_, ALU.mult).then_inc(h_ok, 1)
                    step(dve.tensor_scalar(h_, h_, 0.5, None, ALU.mult))
                    dve.wait_ge(h_act, tb + 1)
                    step(dve.scalar_tensor_tensor(out=g_, in0=g_, scalar=1.0, in1=h_, op0=ALU.add, op1=ALU.mult))
                    dve.tensor_tensor(w_, g_, gates_t[:, tb * HK:(tb + 1) * HK], ALU.mult).then_inc(w_ok, 1)
                    dve.wait_ge(w_ok, tb + 1)
                if tb:
                    dve.wait_ge(v_free, HK * tb + 2 * NG)
                    z = xcur[:, tb - 1, :]
                    z2 = z.rearrange("p (i n) -> p i n", i=2)
                    dve.scalar_tensor_tensor(out=z2, in0=z2, scalar=ALPHA, in1=psum[:, 6:8, :], op0=ALU.mult, op1=ALU.add).then_inc(peer_out, 1)
                    dve.wait_ge(peer_out, tb)
                    layer_norm(tb - 1, 32 * (2 * NC + 1), fin_ok)


NAMES = ["x", "mem", "positions", "w_in", "g_cq", "w_uq", "g_ckv", "w_ukv", "lam_re", "lam_im", "log_dt", "b_re", "b_im",
         "c_re", "c_im", "d_skip", "w_glu", "b_glu", "g_mla_out", "g_ssm_out", "w_out", "ln1_g", "ln1_b", "xq", "xk", "xv",
         "xo", "ln2_g", "ln2_b", "w_query", "sub_keys1", "sub_keys2", "u_tab", "v_tab", "ln3_g", "ln3_b"]
STOP = None


def kernel(**inputs):
    import concourse.bacc as bacc
    from concourse.bass_utils import run_bass_kernel_spmd

    nc = bacc.Bacc("TRN2", target_bir_lowering=False, num_devices=1)
    arrays, args = {}, {}
    for name in NAMES:
        arr = np.ascontiguousarray(inputs[name])
        arrays["in_" + name] = arr
        args[name] = nc.dram_tensor("in_" + name, arr.shape, mybir.dt.from_np(arr.dtype), kind="ExternalInput").ap()
    arrays["in_consts"] = shape_constants()
    consts = nc.dram_tensor("in_consts", (P, CW), F32, kind="ExternalInput").ap()
    out = nc.dram_tensor("out", (1, T, D), F32, kind="ExternalOutput").ap()
    build(nc, args, consts, out, STOP)
    r = run_bass_kernel_spmd(nc, [arrays], core_ids=[0])
    return r.results[0]["out"]
```

```python
import math
from contextlib import ExitStack

import numpy as np
import concourse.bass as bass
from concourse import mybir

F32 = mybir.dt.float32
U32 = mybir.dt.uint32
I32 = mybir.dt.int32
ALU = mybir.AluOpType
ACT = mybir.ActivationFunctionType
AX = mybir.AxisListType

P = 128
D = 1024
T = 512
TC = 256
NC = T // TC
TB = TC // P
NTB = T // P
KD = D // P
M_MEM = 256
MB = M_MEM // P
H = 8
NOPE, ROPE, VH = 64, 32, 64
DQ = NOPE + ROPE
QL, KVL, SW = 384, 256, 512
XH = 4
G, NS, GC = 32, 64, 16
JT = G // 2
PH, NK, TOPK = 8, 128, 16
HK = PH * TOPK
ALPHA = 2.0 ** 0.25
MAGIC = 12582912.0
INV2PI = float(1.0 / (2.0 * math.pi))
C1 = 6.28125
C2 = float(np.float32(round((2 * math.pi - C1) * 2 ** 18) / 2 ** 18))
C3 = float(2 * math.pi - C1 - C2)
PI_IN = 3.1415925
GELU_C = math.sqrt(2.0 / math.pi)
RB = 5
YBANK = 5
OB = 6
SLOTS = 4
SLOT = 2048
PW = 256
NSL = 8
DB = 4
CW = 6 * P + 32 + 16 + 1


def shape_constants():
    c = np.zeros((P, CW), np.float32)
    r = np.arange(P)
    c[:, 0:128] = np.eye(P)
    c[:, 128:256] = np.where(r[None, :] <= r[:, None], 0.0, -1e30)
    c[:, 256:384] = ((r[:, None] // 16) % 2 == (r[None, :] // 64))
    rot = np.zeros((P, P), np.float32)
    for m in range(P):
        if m % 32 < 16:
            rot[m + 16, m] = -1.0
        else:
            rot[m - 16, m] = 1.0
    c[:, 384:512] = rot
    c[0:32, 512:640] = np.tile(np.eye(32), (1, 4))
    c[0:32, 640:768] = np.tile(rot[0:32, 0:32], (1, 4))
    c[:, 768:784] = np.arange(1, 17)
    c[:, 784:800] = 16 * np.arange(16)
    c[:, 800:816] = np.arange(16)
    c[:, 816] = (np.float32(10000.0) ** (-np.arange(16, dtype=np.float32) / 16))[r % 16]
    return c


def bc(ap, axis, n):
    a = ap.unsqueeze(axis)
    shape = list(a.shape)
    shape[axis] = n
    return a.to_broadcast(shape)


def jobs_of_pe():
    jobs = []
    for c in range(NC):
        if c == 0:
            jobs.append((("cols",), "dve"))
        jobs += [(("xT", c, k), "act") for k in range(KD)]
        if c == 0:
            jobs += [(("memT", k), "act") for k in range(KD // 2)]
            jobs.append((("keysT",), "act"))
        jobs += [(("u", c, n), "act") for n in range(4)]
        jobs += [(("kr", c), "act")]
        jobs += [(("ckv", c, n), "act") for n in range(2)]
        jobs += [(("cq", c, n), "act") for n in range(3)]
        jobs.append((("krot", c), "dve"))
        if c == 0:
            jobs += [(("BT", i), "act") for i in range(2)] + [(("CT", i), "act") for i in range(2)]
        jobs.append((("ss", c), "act"))
        jobs += [(("qrope", c, g), "act") for g in range(2)]
        jobs.append((("qrot", c), "dve"))
        jobs += [(("qn", c, i), "act") for i in range(4)]
        jobs += [(("kn", c, i), "act") for i in range(4)]
        jobs += [(("v", c, tb), "act") for tb in range(TB)]
        jobs.append((("bu", c, 0), "dve"))
        jobs.append((("sc", c, 0), "act"))
        for j in range(JT + 1):
            if c == 0 and j < JT:
                jobs.append((("mem", j), "act"))
            if j + 1 < JT:
                jobs.append((("bu", c, j + 1), "dve"))
            if j:
                jobs.append((("PT", c, j - 1), "act"))
            if j and j % TB == 0:
                jobs.append((("pv", c, j // TB - 1), "act"))
            if j + 1 < JT:
                jobs.append((("sc", c, j + 1), "act"))
        jobs += [(("glu", c, n), "act") for n in range(4)]
        jobs.append((("ms", c), "act"))
        jobs += [(("mix", c, n, tb), "dve") for n in range(4) for tb in range(TB)]
        jobs += [(("x1T", c, k), "act") for k in range(KD)]
        jobs += [(("qx", c, n), "act") for n in range(8)]
        jobs.append((("xs", c, 0), "act"))
        for i in range(XH * TB + 1):
            if i:
                jobs.append((("xPT", c, i - 1), "act"))
            if i and i % TB == 0:
                jobs += [(("ox", c, i // TB - 1, dc), "act") for dc in range(2)]
            if i + 1 < XH * TB:
                jobs.append((("xs", c, i + 1), "act"))
        jobs += [(("xo", c, n, tb), "dve") for n in range(4) for tb in range(TB)]
        jobs += [(("x2T", c, k), "act") for k in range(KD)]
        jobs += [(("qq", c, n), "act") for n in range(16)]
        for tb in range(TB):
            jobs += [(("ks", c, tb, g), "act") for g in range(4)]
    return jobs


JOBS = jobs_of_pe()
NUM = {name: n for n, (name, _) in enumerate(JOBS)}
EMPTIED = {}
_count = {"act": 0, "dve": 0}
for _name, _eng in JOBS:
    _count[_eng] += 1
    EMPTIED[_name] = _count[_eng]


def weight_pieces():
    out = []
    for c in range(NC):
        out += [("u", c, n, ("u", c, 2 * n + 1), KD, PW, 1) for n in range(2)]
        out += [("kr", c, 0, ("kr", c), KD, ROPE, 1), ("ckv", c, 0, ("ckv", c, 1), KD, PW, 1)]
        out += [("cq", c, 0, ("cq", c, 1), KD, PW, 1), ("cq", c, 1, ("cq", c, 2), KD, P, 1)]
        out += [("uqr", c, 0, ("qrope", c, 1), 3, H * ROPE, 3), ("uqn", c, 0, ("qn", c, 3), 3, H * NOPE, 3)]
        out += [("ukn", c, 0, ("kn", c, 3), 2, H * NOPE, 2), ("ukv", c, 0, ("v", c, TB - 1), 2, H * VH, 2)]
        if c == 0:
            out += [("xk", 0, n, ("mem", 2 * n + 1), KD, PW, 1) for n in range(4)]
            out += [("xv", 0, n, ("mem", 8 + 2 * n + 1), KD, PW, 1) for n in range(4)]
        out += [("glu", c, 0, ("glu", c, 3), 4, SW, 1)]
        out += [("wo", c, n, ("mix", c, n, TB - 1), KD, PW, 1) for n in range(4)]
        out += [("xq", c, n, ("qx", c, 2 * n + 1), KD, PW, 1) for n in range(4)]
        out += [("xo", c, n, ("xo", c, n, TB - 1), KD, PW, 1) for n in range(4)]
        out += [("wq", c, n, ("qq", c, 2 * n + 1), KD, PW, 1) for n in range(8)]
    return [(p[0:3],) + p[3:] for p in out]


PIECES = weight_pieces()
PNUM = {p[0]: n for n, p in enumerate(PIECES)}
LANDED = {}
_landed = [0] * SLOTS
for _n, _p in enumerate(PIECES):
    _landed[_n % SLOTS] += 16 * _p[4]
    LANDED[_p[0]] = _landed[_n % SLOTS]


def peer_items():
    out = [("u", 0, n) for n in range(HK // NSL)] + [("w", 0)]
    out += [("uv", 1, n) for n in range(2 * HK // NSL)] + [("w", 1), ("o", 0)]
    return out + [("v", 1, n) for n in range(HK // NSL)] + [("o", 1)]


def chain_ticks():
    out = [(("rt", 0, 1, n), 7.0) for n in range(9)]
    c = 1
    out += [(("xT", c, k), 1.0) for k in (3, 7)]
    out += [(("proj", c, n), 3.5) for n in range(10)]
    out += [(("lat", c), 5.0), (("qrot", c), 4.0), (("qn", c), 5.0), (("kn", c), 4.0), (("v", c), 3.0)]
    out += [(("step", c, j), 8.0) for j in range(JT)]
    out += [(("gelu", c), 5.0), (("glu", c), 9.0)]
    out += [(("mix", c, n), 4.5) for n in range(4)]
    out += [(("ln1", c, tb), 6.0) for tb in range(TB)]
    out += [(("x1T", c, k), 1.5) for k in (3, 7)]
    out += [(("qx", c, n), 3.5) for n in range(8)]
    out += [(("xu", c, i), 3.0) for i in range(XH * TB)]
    out += [(("xo", c, n), 4.0) for n in range(4)]
    out += [(("ln2", c, tb), 6.0) for tb in range(TB)]
    out += [(("x2T", c, k), 1.5) for k in (3, 7)]
    out += [(("qq", c, n), 3.5) for n in range(16)]
    out += [(("rt", c, tb, n), 7.0) for tb in range(TB) for n in range(9)]
    return out


ITEMS = peer_items()
TICKS = chain_ticks()
LEFT_OVER = 6


def items_at_ticks():
    whole = sum(w for _, w in TICKS)
    n = len(ITEMS) - LEFT_OVER
    at, served, out = 0.0, 0, {}
    for key, w in TICKS:
        at += w
        upto = int(n * at / whole + 1e-6)
        out[key] = ITEMS[served:upto]
        served = upto
    return out, ITEMS[served:]


AT_TICK, LAST_ITEMS = items_at_ticks()
STAGE = {item: key[0] for key, items in AT_TICK.items() for item in items}

RUNS = [("u", 0, 16), ("uv", 1, 32), ("v", 1, 16), ("u", 2, 16), ("uv", 3, 32), ("v", 3, 16)]
UNITS = [(kind, tb, n) for kind, tb, units in RUNS for n in range(units)]
UNIT_NO = {unit: i for i, unit in enumerate(UNITS)}
V_SLOTS = {"u": (), "uv": (1, 3, 5, 7), "v": tuple(range(NSL))}
FEW = {"proj": 1, "lat": 1, "glu": 1, "mix": 2, "ln1": 1, "x1T": 2, "qx": 2, "xu": 1, "xo": 1, "ln2": 1, "x2T": 2, "qq": 2}


def vector_slots(kind, tb, n):
    if kind == "v":
        return (3, 7)
    return V_SLOTS[kind][4 - FEW.get(STAGE.get((kind, tb, n)), 0):] if kind == "uv" else ()


def rows_used():
    count = {"u": 0, "v": 0, "x": 0}
    used, after = {}, []
    for unit in UNITS:
        used[unit] = {}
        v = 0
        for s in range(NSL):
            eng = "u" if s not in V_SLOTS[unit[0]] else "x" if s in vector_slots(*unit) else "v"
            count[eng] += 1
            used[unit][s] = (eng, count[eng])
            v += s in V_SLOTS[unit[0]]
            if eng != "u" and v % DB == 0:
                after.append(count["v"])
    return used, after


USED, AFTER_BATCH = rows_used()


def in_loop(unit, s, back):
    kind, tb, n = unit
    eng, at = USED[(kind, tb, 1)][s]
    per = sum(e == eng for e, _ in USED[(kind, tb, 1)].values())
    return eng, per, at + (n - 1 - back) * per


def rows_of_block(tb, eng):
    last = ("uv", tb + 1, 31) if tb % 2 == 0 else ("v", tb, 15)
    return max((n for i in range(UNIT_NO[last] + 1) for e, n in USED[UNITS[i]].values() if e == eng), default=0)



def build(nc, a, consts, out, stop=None):
    ctx = ExitStack()
    with ctx:
        def sb(name, cols, dt=F32, rows=P):
            return ctx.enter_context(nc.sbuf_tensor(name, [rows, cols], dt))

        def sem(name):
            return ctx.enter_context(nc.semaphore(name))

        ring = sb("weight_ring", SLOTS * SLOT)
        xcur_t = sb("xcur", NTB * D)
        actT_t = sb("actT", KD * TC)
        kT_t = sb("kT", H * T)
        v_t = sb("v", NTB * H * VH)
        kTx_t = sb("kTx", 8 * M_MEM)
        vx_t = sb("vx", MB * D)
        lngb = sb("lngb", 2 * D)
        BT_t = sb("BT", 4 * 2 * P)
        CT_t = sb("CT", 2 * JT * 32)
        trig_t = sb("trig", 2 * JT * 32)
        cst = sb("cst", CW)
        cols = sb("cols", P)
        ropet = sb("ropet", 2 * T)
        keysT = sb("keysT", 2 * NK)
        ids_t = sb("ids", NTB * HK, U32)
        gates_t = sb("gates", NTB * HK)
        scratch = sb("scratch", 8960)
        rowbuf_t = sb("expert_rows", NSL * D)
        diag_t = sb("diag", 2 * DB * P)
        peer_t = sb("peer_small", 3 * 2 * HK + 3 * 2 * NSL)
        kc = sb("kc", 4)
        ones = sb("ones_t", P)[:, :]
        small = sb("small", 96)
        kcol = sb("kcol", 8)
        pool_t = sb("pool_t", 512)

        ident = cst[:, 0:128]
        causal = cst[:, 128:256]
        parity = cst[:, 256:384]
        rot = cst[:, 384:512]
        rep = cst[0:32, 512:640]
        reprot = cst[0:32, 640:768]
        mult32 = cst[:, 768:800]
        iota16 = cst[:, 800:816]
        freq = cst[:, 816:817]

        xcur = xcur_t[:, :].rearrange("p (t d) -> p t d", t=NTB)
        memT = xcur_t[:, 2048:4096].rearrange("p (k m) -> p k m", k=KD)
        actT = actT_t[:, :].rearrange("p (k t) -> p k t", k=KD)
        qT = actT_t[:, :].rearrange("p (h t) -> p h t", h=H)
        kT = kT_t[:, :].rearrange("p (h t) -> p h t", h=H)
        V = v_t[:, :].rearrange("p (t n) -> p t n", t=NTB)
        mem_nat = v_t[:, :].rearrange("p (b d) -> p b d", b=MB)
        kTx = kTx_t[:, :].rearrange("p (n m) -> p n m", n=8)
        vx = vx_t[:, :].rearrange("p (b d) -> p b d", b=MB)
        BT = BT_t[:, :].rearrange("p (i c m) -> p i c m", i=2, c=4)
        CT = CT_t[:, :].rearrange("p (i j h) -> p i j h", i=2, j=JT)
        trig = trig_t[:, :].rearrange("p (i j m) -> p i j m", i=2, j=JT)
        ropeC, ropeS = ropet[:, 0:T], ropet[:, T:2 * T]

        rows = kT_t[:, 0:128]
        bnat = kT_t[:, 128:640].rearrange("p (i j h) -> p i j h", i=2, j=JT)
        cnat = kT_t[:, 640:1152].rearrange("p (i c q) -> p i c q", i=2, c=4)
        bbpad = kT_t[:, 1152:2176].rearrange("p (i c m) -> p i c m", i=2, c=4)
        cdup = kT_t[:, 2176:3200].rearrange("p (i c m) -> p i c m", i=2, c=4)
        par = [kT_t[:, 3200 + 16 * i:3216 + 16 * i] for i in range(24)]
        ldt = kT_t[:, 3600:3602]
        keys_nat = kTx_t[:, 0:256].rearrange("p (i d) -> p i d", i=2)
        ang = scratch[:, 0:3072]
        pos_i = scratch[:, 3072:3584].bitcast(I32)
        bbw = scratch[:, 3584:4608].rearrange("p (i j h) -> p i j h", i=4, j=JT)

        uT = scratch[:, 0:1024].rearrange("p (n t) -> p n t", n=4)
        cT = scratch[:, 1024:2304].rearrange("p (n t) -> p n t", n=5)
        yT = scratch[:, 1024:2048].rearrange("p (n t) -> p n t", n=4)
        oT = scratch[:, 2304:3328].rearrange("p (n t) -> p n t", n=4)
        PT = scratch[:, 3328:4352].rearrange("p (k t) -> p k t", k=NTB)
        Pr = scratch[:, 4352:5376]
        Pq = Pr.rearrange("p (i n) -> p i n", i=2)
        qraw = Pr[:, 0:512].rearrange("p (g t) -> p g t", g=2)
        qtmp = Pr[:, 512:1024].rearrange("p (g t) -> p g t", g=2)
        s5 = scratch[:, 5376:8960]
        tab = s5[:, 0:1024].rearrange("p (b i t) -> p b i t", b=2, i=2)
        sA = s5[:, 1024:1536].rearrange("p (i t) -> p i t", i=2)
        sB = s5[:, 1536:2048].rearrange("p (i t) -> p i t", i=2)
        sW = s5[:, 2048:2560].rearrange("p (i t) -> p i t", i=2)
        sS = s5[:, 2560:3584].rearrange("p (b i t) -> p b i t", b=2, i=2)
        sq5 = s5[:, 1024:2304].rearrange("p (n t) -> p n t", n=5)
        kraw = s5[:, 2304:2560]
        kt1, kt2 = s5[:, 2560:2816], s5[:, 2816:3072]
        rms = s5[:, 3072:3584]
        g1, g2 = s5[:, 1024:2048], s5[:, 2048:3072]

        qTx = scratch[:, 0:2048].rearrange("p (n t) -> p n t", n=8)
        oTx = scratch[:, 2048:4096].rearrange("p (n t) -> p n t", n=8)
        Px = scratch[:, 4096:4608].rearrange("p (i m) -> p i m", i=2)
        PTx = scratch[:, 4608:5632].rearrange("p (i m t) -> p i m t", i=2, m=MB)

        qTq = scratch[:, 0:4096].rearrange("p (n t) -> p n t", n=16)
        S1 = scratch[:, 4096:6144]
        rv = scratch[:, 6144:6400]
        ridx = scratch[:, 6400:6656].bitcast(U32)
        rif = scratch[:, 6656:6912]
        tops = scratch[:, 6912:7040]
        tpos = scratch[:, 7040:7168].bitcast(U32)
        tab_a = scratch[:, 7168:7296]
        tab_b = scratch[:, 7296:7424]
        tia = scratch[:, 7424:7552]
        tib = scratch[:, 7552:7680]
        tau = scratch[:, 7680:7808].bitcast(U32)
        tbu = scratch[:, 7808:7936].bitcast(U32)
        rest = scratch[:, 7936:8448].rearrange("p (i n) -> p i n", i=2)

        rowbuf = [rowbuf_t[:, D * s:D * (s + 1)] for s in range(NSL)]
        diag = diag_t[:, :].rearrange("p (q s m) -> p q s m", q=2, s=DB)
        hbuf = peer_t[:, 0:256].rearrange("p (q n) -> p q n", q=2)
        wbuf = peer_t[:, 256:512].rearrange("p (q n) -> p q n", q=2)
        gel = peer_t[:, 512:768].rearrange("p (q n) -> p q n", q=2)
        h8 = peer_t[:, 768:784].rearrange("p (q n) -> p q n", q=2)
        w8 = peer_t[:, 784:800].rearrange("p (q n) -> p q n", q=2)
        idstage = peer_t[:, 800:816].bitcast(U32).rearrange("p (q n) -> p q n", q=2)

        nmax = small[:, 0:4]
        rsum = small[:, 4:8]
        rsmix = small[:, 8:12]
        st6 = small[:, 12:24].rearrange("p (i n) -> p i n", i=2)
        mv = small[:, 24:26]
        std = small[:, 26:28]
        carry = small[:, 32:64].rearrange("p (j i) -> p j i", j=JT)
        magc = small[:, 64:80]
        gsum = small[:, 80:88]

        psum = ctx.enter_context(nc.psum_tensor("banks", [P, 8, 512], F32))

        def bank_of(name):
            return psum[:, NUM[name] % RB, :]

        pe_done = sem("pe_done")
        emptied = {"act": sem("act_emptied"), "dve": sem("dve_emptied")}
        w_land = [sem("w_land%d" % i) for i in range(SLOTS)]
        x_land = sem("x_land")
        mem_land = sem("mem_land")
        c_land = sem("c_land")
        par_land = sem("par_land")
        pos_land = sem("pos_land")
        keys_land = sem("keys_land")
        ln_land = sem("ln_land")
        out_land = sem("out_land")
        ldt_ok = sem("ldt_ok")
        fills = sem("fills")
        dve_c = sem("dve_chain")
        act_c = sem("act_chain")
        pool_c = sem("pool_chain")
        rows_ok = sem("rows_ok")
        par_dve = sem("par_dve")
        par_act = sem("par_act")
        bt_ok = sem("bt_ok")
        trig_ok = sem("trig_ok")
        tab_ok = sem("tab_ok")
        tab_used = sem("tab_used")
        sq_ok = sem("sq_ok")
        rms_ok = sem("rms_ok")
        c_ok = sem("c_ok")
        q_ok = sem("q_ok")
        smax = sem("smax")
        pexp = sem("pexp")
        pn = sem("pn")
        st_ok = sem("st_ok")
        y_mm = sem("y_mm")
        y_ok = sem("y_ok")
        gl_act = sem("gl_act")
        gl_dve = sem("gl_dve")
        mixin = sem("mixin")
        sqm = sem("sqm")
        rsm = sem("rsm")
        var_ok = sem("var_ok")
        std_ok = sem("std_ok")
        ln_ok = sem("ln_ok")
        xscaled = sem("xscaled")
        xsmax = sem("xsmax")
        xexp = sem("xexp")
        xpn = sem("xpn")
        s_free = sem("s_free")
        rt_d = sem("rt_d")
        rt_a = sem("rt_a")
        route_ok = sem("route_ok")
        row_land = [sem("row_land%d" % i) for i in range(NSL)]
        u_done = sem("u_done")
        v_done = sem("v_done")
        x_done = sem("x_done")
        used_sem = {"u": u_done, "v": v_done, "x": x_done}
        stage_ok = sem("stage_ok")
        dots_ok = sem("dots_ok")
        w8_ok = sem("w8_ok")
        h_ok = sem("h_ok")
        h_act = sem("h_act")
        w_ok = sem("w_ok")
        diag_ok = sem("diag_ok")
        peer_out = sem("peer_out")
        fin_ok = sem("fin_ok")
        bc_land = sem("bc_land")

        block = ctx.enter_context(nc.Block())

        def wslot(name):
            n = PNUM[name]
            _, _, k, cols_, _ = PIECES[n]
            at = n % SLOTS * SLOT
            return ring[:, at:at + k * cols_].rearrange("p (k n) -> p k n", k=k)

        def wait_piece(eng, name):
            eng.wait_ge(w_land[PNUM[name] % SLOTS], LANDED[name])
            return wslot(name)

        def wait_emptied(eng, name):
            eng.wait_ge(emptied[JOBS[NUM[name]][1]], EMPTIED[name])

        def wait_job(eng, name):
            eng.wait_ge(pe_done, NUM[name] + 1)

        deep = {n: a[n][0].rearrange("(k p) n -> p k n", p=P) for n in ("w_in", "w_out", "w_query", "xq", "xk", "xv", "xo", "w_glu")}

        def piece_transfers(name):
            kind, _, n = name
            dst = wslot(name)
            if kind in ("uqr", "uqn", "ukn", "ukv"):
                src, wide, lo, hi = {"uqr": ("w_uq", DQ, NOPE, DQ), "uqn": ("w_uq", DQ, 0, NOPE),
                                     "ukn": ("w_ukv", NOPE + VH, 0, NOPE), "ukv": ("w_ukv", NOPE + VH, NOPE, NOPE + VH)}[kind]
                return [(dst[:, k, :].rearrange("p (h d) -> p h d", h=H),
                         a[src][0, k * P:(k + 1) * P, :].rearrange("p (h d) -> p h d", d=wide)[:, :, lo:hi])
                        for k in range(dst.shape[1])]
            src, at = {"u": ("w_in", QL + KVL + ROPE), "kr": ("w_in", QL + KVL), "ckv": ("w_in", QL), "cq": ("w_in", 0),
                       "glu": ("w_glu", 0), "wo": ("w_out", 0), "wq": ("w_query", 0)}.get(kind, (kind, 0))
            at += PW * n
            return [(dst, deep[src][:, :, at:at + dst.shape[2]])]

        @block.sync
        def _(sp):
            def load_x(c):
                if c:
                    wait_job(sp, ("mem", 15))
                sp.dma_start(xcur[:, c * TB:(c + 1) * TB, :],
                             a["x"][0, c * TC:(c + 1) * TC, :].rearrange("(t p) d -> p t d", p=P)).then_inc(x_land, 16)

            def load_piece(n):
                name = PIECES[n][0]
                if n >= SLOTS:
                    wait_job(sp, PIECES[n - SLOTS][1])
                for dst, src in piece_transfers(name):
                    sp.dma_start(dst, src).then_inc(w_land[n % SLOTS], 16)

            sp.dma_start(cst[:, :], consts).then_inc(c_land, 16)
            sp.dma_start(rows[0:16, :], a["lam_re"][0].rearrange("(j g) q -> j (g q)", g=2)).then_inc(par_land, 16)
            sp.dma_start(rows[16:32, :], a["lam_im"][0].rearrange("(j g) q -> j (g q)", g=2)).then_inc(par_land, 16)
            sp.dma_start(ldt[32:48, :], a["log_dt"][0].rearrange("(j g) -> j g", g=2)).then_inc(par_land, 16)
            at = 48
            for name, n in (("g_ckv", 2), ("g_cq", 3), ("d_skip", 4), ("b_glu", 4), ("g_mla_out", 4), ("g_ssm_out", 4)):
                src = a[name][0].rearrange("g h -> (g h)") if name == "d_skip" else a[name][0]
                sp.dma_start(rows[at:at + n, :], src.rearrange("(c p) -> c p", p=P)).then_inc(par_land, 16)
                at += n
            load_x(0)
            load_piece(0)
            sp.dma_start(pos_i, a["positions"][0:1, :].to_broadcast([P, T])).then_inc(pos_land, 16)
            for i, name in enumerate(("b_re", "b_im")):
                sp.dma_start(bnat[:, i], a[name][0].rearrange("(j g) q h -> (g q) j h", g=2)).then_inc(bc_land, 16)
            for i, name in enumerate(("c_re", "c_im")):
                sp.dma_start(cnat[:, i], a[name][0].rearrange("(c g) h q -> (g h) c q", c=4)).then_inc(bc_land, 16)
            for n in range(1, SLOTS):
                load_piece(n)
            sp.dma_start(mem_nat, a["mem"][0].rearrange("(b p) d -> p b d", p=P)).then_inc(mem_land, 16)
            for i, name in enumerate(("sub_keys1", "sub_keys2")):
                sp.dma_start(keys_nat[:, i], a[name][0]).then_inc(keys_land, 16)
            for n in range(SLOTS, len(PIECES)):
                load_piece(n)
                if PIECES[n][0] == ("glu", 0, 0):
                    load_x(1)
            for tb in range(NTB):
                sp.wait_ge(fin_ok, tb + 1)
                sp.dma_start(out[0, tb * P:(tb + 1) * P, :], xcur[:, tb, :]).then_inc(out_land, 16)
            sp.wait_ge(out_land, 16 * NTB)

        def server(serve):
            left = [key for key, _ in TICKS]

            def tick(*key):
                if key in AT_TICK:
                    assert left.pop(0) == key, key
                    for item in AT_TICK[key]:
                        serve(*item)
            return tick

        @block.tensor
        def _(pe):
            order = iter(JOBS)

            def bank(name):
                assert next(order)[0] == name
                n = NUM[name]
                if n >= RB:
                    wait_emptied(pe, JOBS[n - RB][0])
                return psum[:, n % RB, :]

            def product(outp, pairs):
                for i, (l, r) in enumerate(pairs):
                    last = pe.matmul(outp, l, r, start=(i == 0), stop=(i == len(pairs) - 1))
                return last

            def serve_at(kind, tb, n, p, i=0):
                if kind not in ("uv", "v"):
                    return
                first = n == 0 and type(i) is int
                vt = tb - 1 if kind == "uv" else tb
                unit = (kind, tb, n)
                if first and vt:
                    pe.wait_ge(peer_out, vt)
                for m, s in enumerate(V_SLOTS[kind]):
                    half = p if kind == "uv" else m // DB
                    per = len(V_SLOTS[kind]) // DB
                    if m % DB == 0:
                        pe.wait_ge(diag_ok, i * per + (HK * vt // DB + per * n + m // DB + 1))
                    if s in vector_slots(*unit):
                        continue
                    pe.wait_ge(row_land[s], i * 16 + 16 * (UNIT_NO[unit] + 1))
                    row, d = rowbuf[s], diag[:, half, m % DB, :]
                    st = first and m == 0
                    pe.matmul(psum[:, OB, :], d, row[:, 0:512], start=st, stop=False, skip_group_check=True)
                    pe.matmul(psum[:, OB + 1, :], d, row[:, 512:D], start=st, stop=False,
                              skip_group_check=True).then_inc(v_done, 1)

            def serve(kind, tb, n=0):
                serve_at(kind, tb, n, n % 2)

            tick = server(serve)

            def transposed(name, c, ready):
                for k in range(KD):
                    b = bank((name, c, k))
                    if k == 0:
                        ready()
                    for tb in range(TB):
                        last = pe.transpose(b[:, tb * P:(tb + 1) * P], xcur[:, c * TB + tb, k * P:(k + 1) * P], ident)
                    last.then_inc(pe_done, 1)
                    if k in (3, 7):
                        tick(name, c, k)

            def channels(name, w, j, act_in, depth):
                b = bank(name)
                product(b[:, 0:TC], [(w[:, k, j * P:(j + 1) * P], act_in(k)) for k in range(depth)]).then_inc(pe_done, 1)

            pe.wait_ge(c_land, 16)
            for c in range(NC):
                if c == 0:
                    pe.wait_ge(rows_ok, 1)
                    pe.transpose(bank(("cols",))[:, 0:69], rows[0:69, :], ident[0:69, 0:69]).then_inc(pe_done, 1)
                transposed("xT", c, lambda: pe.wait_ge(x_land, 16 * (c + 1)))
                if c == 0:
                    pe.wait_ge(mem_land, 16)
                    for kk in range(KD // 2):
                        b = bank(("memT", kk))
                        for i in range(2):
                            for mb in range(MB):
                                k = 2 * kk + i
                                last = pe.transpose(b[:, i * M_MEM + mb * P:i * M_MEM + (mb + 1) * P],
                                                    mem_nat[:, mb, k * P:(k + 1) * P], ident)
                        last.then_inc(pe_done, 1)
                    pe.wait_ge(keys_land, 32)
                    b = bank(("keysT",))
                    for i in range(2):
                        last = pe.transpose(b[:, i * NK:(i + 1) * NK], keys_nat[:, i], ident)
                    last.then_inc(pe_done, 1)
                wait_emptied(pe, ("xT", c, KD - 1))
                x_of = lambda k: actT[:, k, :]
                for n in range(4):
                    if n % 2 == 0:
                        w = wait_piece(pe, ("u", c, n // 2))
                    channels(("u", c, n), w, n % 2, x_of, KD)
                    tick("proj", c, n)
                w = wait_piece(pe, ("kr", c, 0))
                b = bank(("kr", c))
                product(b[0:ROPE, 0:TC], [(w[:, k, :], actT[:, k, :]) for k in range(KD)]).then_inc(pe_done, 1)
                tick("proj", c, 4)
                w = wait_piece(pe, ("ckv", c, 0))
                for n in range(2):
                    channels(("ckv", c, n), w, n, x_of, KD)
                    tick("proj", c, 5 + n)
                for n in range(3):
                    if n % 2 == 0:
                        w = wait_piece(pe, ("cq", c, n // 2))
                    channels(("cq", c, n), w, n % 2, x_of, KD)
                    tick("proj", c, 7 + n)
                b = bank(("krot", c))
                wait_emptied(pe, ("kr", c))
                pe.matmul(b[:, 0:TC], rep, kraw[0:ROPE, :], start=True, stop=True)
                pe.matmul(b[:, TC:2 * TC], reprot, kraw[0:ROPE, :], start=True, stop=True).then_inc(pe_done, 1)
                if c == 0:
                    pe.wait_ge(bt_ok, 1)
                    for nm, src in (("BT", bbpad), ("CT", cdup)):
                        for i in range(2):
                            b = bank((nm, i))
                            for q in range(4):
                                last = pe.transpose(b[:, q * P:(q + 1) * P], src[:, i, q, :], ident)
                            last.then_inc(pe_done, 1)
                b = bank(("ss", c))
                pe.wait_ge(sq_ok, 5 * (c + 1))
                pe.wait_ge(fills, 3)
                product(b[:, 0:TC], [(ones, sq5[:, n, :]) for n in (0, 1)])
                product(b[:, TC:2 * TC], [(ones, sq5[:, n, :]) for n in (2, 3, 4)]).then_inc(pe_done, 1)
                tick("lat", c)
                pe.wait_ge(c_ok, 5 * (c + 1))
                cq_of = lambda k: cT[:, 2 + k, :]
                w = wait_piece(pe, ("uqr", c, 0))
                for g in range(2):
                    channels(("qrope", c, g), w, g, cq_of, 3)
                b = bank(("qrot", c))
                wait_emptied(pe, ("qrope", c, 1))
                for g in range(2):
                    last = pe.matmul(b[:, g * TC:(g + 1) * TC], rot, qraw[:, g, :], start=True, stop=True)
                last.then_inc(pe_done, 1)
                tick("qrot", c)
                w = wait_piece(pe, ("uqn", c, 0))
                for i in range(4):
                    channels(("qn", c, i), w, i, cq_of, 3)
                tick("qn", c)
                w = wait_piece(pe, ("ukn", c, 0))
                for i in range(4):
                    channels(("kn", c, i), w, i, lambda k: cT[:, k, :], 2)
                tick("kn", c)
                w = wait_piece(pe, ("ukv", c, 0))
                for tb in range(TB):
                    b = bank(("v", c, tb))
                    product(b, [(cT[:, k, tb * P:(tb + 1) * P], w[:, k, :]) for k in range(2)]).then_inc(pe_done, 1)
                tick("v", c)

                def bu(j):
                    b = bank(("bu", c, j))
                    q, r = j // 4, j % 4
                    for i in range(2):
                        last = pe.matmul(b[:, i * TC:(i + 1) * TC], BT[32 * r:32 * r + 32, i, q, :],
                                         uT[32 * r:32 * r + 32, q, :], start=True, stop=True)
                    last.then_inc(pe_done, 1)

                def score(i):
                    h, qb = i // TB, i % TB
                    keys = (c * TB + qb + 1) * P
                    b = bank(("sc", c, i))
                    pe.matmul(b[:, 0:keys], qT[0:DQ, h, qb * P:(qb + 1) * P], kT[0:DQ, h, 0:keys],
                              start=True, stop=True).then_inc(pe_done, 1)

                def mem_kv(i):
                    b = bank(("mem", i))
                    w = wait_piece(pe, ("xk" if i < 8 else "xv", 0, i % 8 // 2))
                    if i < 8:
                        pairs = [(w[:, k, (i % 2) * P:(i % 2 + 1) * P], memT[:, k, :]) for k in range(KD)]
                    else:
                        pairs = [(memT[:, k, (i % 2) * P:(i % 2 + 1) * P], w[:, k, :]) for k in range(KD)]
                    product(b[:, 0:PW], pairs).then_inc(pe_done, 1)

                def behind(j):
                    h, qb = j // TB, j % TB
                    qg = c * TB + qb
                    b = bank(("PT", c, j))
                    pe.wait_ge(pn, c * JT + j + 1)
                    for kb in range(qg + 1):
                        last = pe.transpose(b[:, kb * P:(kb + 1) * P], Pq[:, j % 2, kb * P:(kb + 1) * P], ident)
                    last.then_inc(pe_done, 1)
                    if qb == TB - 1:
                        b = bank(("pv", c, h))
                        wait_emptied(pe, ("PT", c, j))
                        half = 64 * (h % 2)
                        for kb in range((c + 1) * TB):
                            q0 = max(0, kb - c * TB) * P
                            last = pe.matmul(b[half:half + 64, q0:TC], V[:, kb, h * VH:(h + 1) * VH],
                                             PT[:, kb, q0:TC], start=(kb == 0), stop=(kb == (c + 1) * TB - 1))
                        last.then_inc(pe_done, 1)

                def state_out(j):
                    q, r = j // 4, j % 4
                    yb = psum[:, YBANK, (q % 2) * TC:(q % 2 + 1) * TC]
                    pe.wait_ge(st_ok, c * JT + j + 1)
                    if r == 0 and 4 * c + q >= 1:
                        pe.wait_ge(y_ok, 4 * c + q)
                    product(yb[32 * r:32 * r + 32, :],
                            [(CT[:, i, j, :], sS[:, j % 2, i, :]) for i in range(2)]).then_inc(y_mm, 1)

                if c == 0:
                    wait_emptied(pe, ("BT", 1))
                    wait_emptied(pe, ("CT", 1))
                bu(0)
                pe.wait_ge(q_ok, 2 * (c + 1))
                wait_emptied(pe, ("v", c, TB - 1))
                score(0)
                for j in range(JT + 1):
                    if c == 0 and j < JT:
                        mem_kv(j)
                    if j + 1 < JT:
                        bu(j + 1)
                    if j:
                        behind(j - 1)
                    if j + 1 < JT:
                        score(j + 1)
                    if j:
                        state_out(j - 1)
                    if j < JT:
                        tick("step", c, j)
                tick("gelu", c)
                w = wait_piece(pe, ("glu", c, 0))
                pe.wait_ge(gl_dve, 4 * c + 3)
                for n in range(4):
                    channels(("glu", c, n), w, n, lambda k: yT[:, k, :], 4)
                b = bank(("ms", c))
                pe.wait_ge(sqm, 2 * (c + 1))
                for s, sqs in enumerate((Pr, g1)):
                    sv = sqs.rearrange("p (n t) -> p n t", n=4)
                    for tb in range(TB):
                        last = product(b[:, 2 * s + tb:2 * s + tb + 1], [(sv[:, n, tb * P:(tb + 1) * P], ones[:, 0:1]) for n in range(4)])
                last.then_inc(pe_done, 1)
                tick("glu", c)
                pe.wait_ge(mixin, c + 1)
                for n in range(4):
                    w = wait_piece(pe, ("wo", c, n))
                    for tb in range(TB):
                        b = bank(("mix", c, n, tb))
                        ts = slice(tb * P, (tb + 1) * P)
                        product(b[:, 0:PW], [(oT[:, k, ts], w[:, k, :]) for k in range(4)])
                        product(b[:, PW:2 * PW], [(yT[:, k, ts], w[:, 4 + k, :]) for k in range(4)]).then_inc(pe_done, 1)
                    tick("mix", c, n)
                for tb in range(TB):
                    tick("ln1", c, tb)
                transposed("x1T", c, lambda: pe.wait_ge(ln_ok, 2 * TB * c + TB))
                wait_emptied(pe, ("x1T", c, KD - 1))
                for n in range(8):
                    if n % 2 == 0:
                        w = wait_piece(pe, ("xq", c, n // 2))
                    channels(("qx", c, n), w, n % 2, x_of, KD)
                    tick("qx", c, n)
                wait_emptied(pe, ("qx", c, 7))

                def xscore(i):
                    h, tb = i // TB, i % TB
                    b = bank(("xs", c, i))
                    product(b[:, 0:M_MEM], [(qTx[:, 2 * h + dc, tb * P:(tb + 1) * P], kTx[:, 2 * h + dc, :]) for dc in range(2)]).then_inc(pe_done, 1)

                def xbehind(i):
                    b = bank(("xPT", c, i))
                    pe.wait_ge(xpn, c * XH * TB + i + 1)
                    for mb in range(MB):
                        last = pe.transpose(b[:, mb * P:(mb + 1) * P], Px[:, i % 2, mb * P:(mb + 1) * P], ident)
                    last.then_inc(pe_done, 1)
                    if i % TB == TB - 1:
                        h = i // TB
                        wait_emptied(pe, ("xPT", c, i))
                        for dc in range(2):
                            b = bank(("ox", c, h, dc))
                            product(b[:, 0:TC], [(vx[:, mb, (2 * h + dc) * P:(2 * h + dc + 1) * P], PTx[:, h % 2, mb, :]) for mb in range(MB)]).then_inc(pe_done, 1)

                xscore(0)
                for i in range(XH * TB + 1):
                    if i:
                        xbehind(i - 1)
                    if i + 1 < XH * TB:
                        xscore(i + 1)
                    if i < XH * TB:
                        tick("xu", c, i)
                wait_emptied(pe, ("ox", c, XH - 1, 1))
                for n in range(4):
                    w = wait_piece(pe, ("xo", c, n))
                    for tb in range(TB):
                        b = bank(("xo", c, n, tb))
                        product(b[:, 0:PW], [(oTx[:, k, tb * P:(tb + 1) * P], w[:, k, :]) for k in range(KD)]).then_inc(pe_done, 1)
                    tick("xo", c, n)
                for tb in range(TB):
                    tick("ln2", c, tb)
                transposed("x2T", c, lambda: pe.wait_ge(ln_ok, 2 * TB * c + 2 * TB))
                wait_emptied(pe, ("x2T", c, KD - 1))
                for n in range(16):
                    if n % 2 == 0:
                        w = wait_piece(pe, ("wq", c, n // 2))
                    channels(("qq", c, n), w, n % 2, x_of, KD)
                    tick("qq", c, n)
                wait_emptied(pe, ("qq", c, 15))
                for tb in range(TB):
                    for g in range(4):
                        b = bank(("ks", c, tb, g))
                        for i in range(4):
                            n = 4 * g + i
                            last = pe.matmul(b[:, i * NK:(i + 1) * NK], qTq[:, n, tb * P:(tb + 1) * P],
                                             keysT[:, (n % 2) * NK:(n % 2 + 1) * NK], start=True, stop=True)
                        last.then_inc(pe_done, 1)
                    for n in range(9):
                        tick("rt", c, tb, n)
            for item in LAST_ITEMS:
                serve(*item)
            for kind, units in (("uv", 32), ("v", 16)):
                for p in range(2):
                    serve_at(kind, 3, p, p)
                with pe.Fori(1, units // 2) as m:
                    i = m * 2
                    for p in range(2):
                        serve_at(kind, 3, p, p, i)

        @block.scalar
        def _(act):
            chain = [0]

            def step(ins):
                ins.then_inc(act_c, 1)
                chain[0] += 1
                act.wait_ge(act_c, chain[0])

            order = iter([n for n, e in JOBS if e == "act"])

            def take(name, ops):
                assert next(order) == name, name
                wait_job(act, name)
                ops(bank_of(name)).then_inc(emptied["act"], 1)

            def take_exp(name, out_, scale, bias, total, signal, count):
                assert next(order) == name, name
                wait_job(act, name)
                b = bank_of(name)
                act.activation(out_, b[:, 0:out_.shape[1]], ACT.Exp, bias=bias, scale=scale, accum_out=total).then_inc(signal, 1)
                act.wait_ge(signal, count)
                act.sem_inc(emptied["act"], 1)

            def copy(dst, src):
                return act.copy(dst, src)

            devs = [0]

            def deviation():
                devs[0] += 1
                act.wait_ge(var_ok, devs[0])
                act.activation(std[:, 0:1], mv[:, 1:2], ACT.Sqrt, bias=kc[:, 1:2]).then_inc(std_ok, 1)

            loads = [0]

            def load_ln(g, b, after):
                if after:
                    act.wait_ge(ln_ok, after)
                act.dma_start(lngb[:, 0:D], a[g][0:1, :].to_broadcast([P, D])).then_inc(ln_land, 16)
                act.dma_start(lngb[:, D:2 * D], a[b][0:1, :].to_broadcast([P, D])).then_inc(ln_land, 16)

            def make_diag(unit, half, q, weights, i=0):
                kind, tb, n = unit
                vt = tb - 1 if kind == "uv" else tb
                batches = len(V_SLOTS[kind]) // DB
                batch = HK * vt // DB + batches * n + half
                if type(i) is not int:
                    per = AFTER_BATCH[batch + batches] - AFTER_BATCH[batch]
                    act.wait_ge(v_done, i * per + (AFTER_BATCH[batch] - 2 // batches * per))
                elif batch >= 2:
                    act.wait_ge(v_done, AFTER_BATCH[batch - 2])
                for d in range(DB):
                    if V_SLOTS[kind][DB * half + d] not in vector_slots(*unit):
                        last = act.mul(diag[:, q, d, :], ident, weights[:, d:d + 1])
                last.then_inc(diag_ok, 1)

            def serve(kind, tb, n=0):
                if kind == "w":
                    act.wait_ge(h_ok, tb + 1)
                    act.activation(gel[:, tb % 2, :], gel[:, tb % 2, :], ACT.Tanh, scale=GELU_C).then_inc(h_act, 1)
                elif kind == "uv":
                    if n == 0:
                        act.wait_ge(w_ok, tb)
                    make_diag((kind, tb, n), 0, n % 2, wbuf[:, (tb - 1) % 2, DB * n:DB * (n + 1)])
                elif kind == "v":
                    if n == 0:
                        act.wait_ge(w_ok, tb + 1)
                    for half in range(2):
                        at = NSL * n + DB * half
                        make_diag((kind, tb, n), half, half, wbuf[:, tb % 2, at:at + DB])

            staged = [0]

            def serve_loop(kind, tb, units):
                w0 = staged[0]
                wide, vt = (DB, tb - 1) if kind == "uv" else (NSL, tb)
                with act.Fori(1, units // 2) as m:
                    i = m * 2
                    for p in range(2):
                        for x in vector_slots(kind, tb, 1)[-1:]:
                            _, per, at = in_loop((kind, tb, p), x, 2)
                            act.wait_ge(x_done, i * per + at)
                        act.copy(w8[:, p, 0:wide], wbuf[:, vt % 2, bass.ds(i * wide + wide * p, wide)]).then_inc(w8_ok, 1)
                        act.wait_ge(w8_ok, i + (w0 - 2 + p + 1))
                        for half in range(wide // DB):
                            q = p if kind == "uv" else half
                            make_diag((kind, tb, p), half, q, w8[:, p, DB * half:DB * half + DB], i)
                staged[0] += units - 2

            tick = server(serve)

            load_ln("ln1_g", "ln1_b", 0)
            dt, mag, cosr, sinr, absr, a1, red = par[3:10]
            act.wait_ge(par_dve, 1)
            act.activation(dt, cols[:, 32:48], ACT.Exp).then_inc(par_act, 1)
            act.wait_ge(par_dve, 2)
            act.activation(mag, a1, ACT.Exp).then_inc(par_act, 1)
            act.wait_ge(par_dve, 3)
            act.wait_ge(fills, 3)
            act.activation(sinr, red, ACT.Sin).then_inc(par_act, 1)
            step(act.activation(absr, red, ACT.Abs))
            act.activation(cosr, absr, ACT.Sin, scale=-1.0, bias=kc[:, 2:3]).then_inc(par_act, 1)
            act.wait_ge(par_dve, 4)
            f = ang[:, 0:512]
            act.activation(trig_t[:, 512:1024], f, ACT.Sin, scale=6.283185).then_inc(trig_ok, 1)
            step(act.activation(ang[:, 512:1024], f, ACT.Abs))
            act.activation(trig_t[:, 0:512], ang[:, 512:1024], ACT.Sin, scale=-6.283185, bias=kc[:, 2:3]).then_inc(trig_ok, 1)
            act.wait_ge(par_dve, 5)
            f = ang[:, 1024:1536]
            act.activation(ropeS, f, ACT.Sin).then_inc(trig_ok, 1)
            step(act.activation(ang[:, 1536:2048], f, ACT.Abs))
            act.activation(ropeC, ang[:, 1536:2048], ACT.Sin, scale=-1.0, bias=kc[:, 2:3]).then_inc(trig_ok, 1)

            for c in range(NC):
                tok = slice(c * TC, (c + 1) * TC)

                def transposed(name):
                    for k in range(KD):
                        take((name, c, k), lambda b: copy(actT[:, k, :], b[:, 0:TC]))
                        if k in (3, 7):
                            tick(name, c, k)

                if c:
                    wait_job(act, ("qq", c - 1, 15))
                transposed("xT")
                if c == 0:
                    for kk in range(KD // 2):
                        take(("memT", kk), lambda b: copy(memT[:, 2 * kk:2 * kk + 2, :], b.rearrange("p (i m) -> p i m", i=2)))
                    take(("keysT",), lambda b: copy(keysT[:, :], b[:, 0:2 * NK]))
                    act.wait_ge(trig_ok, 4)
                    act.wait_ge(bt_ok, 1)
                else:
                    act.wait_ge(route_ok, TB * c)
                for n in range(4):
                    take(("u", c, n), lambda b: copy(uT[:, n, :], b[:, 0:TC]))
                    tick("proj", c, n)
                take(("kr", c), lambda b: copy(kraw[0:ROPE, :], b[0:ROPE, 0:TC]))
                tick("proj", c, 4)
                for n in range(5):
                    def ops(b):
                        act.activation(sq5[:, n, :], b[:, 0:TC], ACT.Square).then_inc(sq_ok, 1)
                        return copy(cT[:, n, :], b[:, 0:TC])
                    take(("ckv", c, n) if n < 2 else ("cq", c, n - 2), ops)
                    tick("proj", c, 5 + n)
                if c == 0:
                    for i in range(2):
                        take(("BT", i), lambda b: copy(BT[:, i], b.rearrange("p (q m) -> p q m", q=4)))
                    for i in range(2):
                        take(("CT", i), lambda b: act.mul(CT[:, i], b.rearrange("p (j h) -> p j h", h=32), -1.0 if i else 1.0))

                def ops(b):
                    act.activation(rms[:, 0:TC], b[:, 0:TC], ACT.Sqrt, scale=1.0 / KVL, bias=kc[:, 0:1])
                    return act.activation(rms[:, TC:2 * TC], b[:, TC:2 * TC], ACT.Sqrt, scale=1.0 / QL, bias=kc[:, 0:1])
                take(("ss", c), ops)
                tick("lat", c)
                for g in range(2):
                    take(("qrope", c, g), lambda b: copy(qraw[:, g, :], b[:, 0:TC]))
                tick("qrot", c)
                for i in range(4):
                    def ops(b):
                        copy(qT[0:NOPE, 2 * i, :], b[0:NOPE, 0:TC])
                        return copy(qT[0:NOPE, 2 * i + 1, :], b[NOPE:2 * NOPE, 0:TC])
                    take(("qn", c, i), ops)
                tick("qn", c)
                for i in range(4):
                    def ops(b):
                        copy(kT[0:NOPE, 2 * i, tok], b[0:NOPE, 0:TC])
                        return copy(kT[0:NOPE, 2 * i + 1, tok], b[NOPE:2 * NOPE, 0:TC])
                    take(("kn", c, i), ops)
                tick("kn", c)
                for tb in range(TB):
                    take(("v", c, tb), lambda b: copy(V[:, c * TB + tb, :], b))
                tick("v", c)

                def exps(i):
                    keys = (c * TB + i % TB + 1) * P
                    act.wait_ge(smax, c * JT + i + 1)
                    if i == 0:
                        act.wait_ge(q_ok, 2 * (c + 1))
                    if i >= 2:
                        wait_job(act, ("PT", c, i - 2))
                    take_exp(("sc", c, i), Pq[:, i % 2, 0:keys], DQ ** -0.5, nmax[:, i % 2:i % 2 + 1],
                             rsum[:, i % 2:i % 2 + 1], pexp, c * JT + i + 1)

                for j in range(JT + 1):
                    if j < JT:
                        exps(j)
                    if c == 0 and j < JT:
                        if j < 8:
                            take(("mem", j), lambda b: copy(kTx[:, j, :], b[:, 0:M_MEM]))
                        else:
                            n = (j - 8) // 2
                            take(("mem", j), lambda b: copy(vx[:, j % 2, PW * n:PW * (n + 1)], b[:, 0:PW]))
                    if j:
                        h, qb = (j - 1) // TB, (j - 1) % TB
                        qg = c * TB + qb
                        if qb == 0 and h:
                            wait_job(act, ("pv", c, h - 1))
                        take(("PT", c, j - 1), lambda b: copy(PT[:, 0:qg + 1, qb * P:(qb + 1) * P],
                                                              b[:, 0:(qg + 1) * P].rearrange("p (k t) -> p k t", k=qg + 1)))
                        if qb == TB - 1:
                            rows_ = slice(64 * (h % 2), 64 * (h % 2) + 64)
                            take(("pv", c, h), lambda b: copy(oT[rows_, h // 2, :], b[rows_, 0:TC]))
                    if j < JT:
                        tick("step", c, j)
                yTf, oTf = scratch[:, 1024:2048], scratch[:, 2304:3328]
                act.wait_ge(y_ok, 4 * (c + 1))
                act.activation(g1, yTf, ACT.Square).then_inc(gl_act, 1)
                act.mul(g2, yTf, 0.5).then_inc(gl_act, 1)
                act.wait_ge(gl_dve, 4 * c + 2)
                act.activation(g1, g1, ACT.Tanh, scale=GELU_C).then_inc(gl_act, 1)
                wait_emptied(act, ("pv", c, H - 1))
                wait_job(act, ("pv", c, H - 1))
                act.activation(Pr, oTf, ACT.Square).then_inc(sqm, 1)
                act.wait_ge(sqm, 2 * c + 1)
                for n in range(4):
                    step(act.mul(oT[:, n, :], oT[:, n, :], cols[:, 61 + n:62 + n]))
                tick("gelu", c)
                act.wait_ge(gl_dve, 4 * c + 3)
                for n in range(4):
                    take(("glu", c, n), lambda b: act.activation(g1[:, n * TC:(n + 1) * TC], b[:, 0:TC], ACT.Tanh,
                                                                 scale=0.5, bias=kcol[:, n:n + 1]))
                act.wait_ge(gl_dve, 4 * c + 4)
                act.activation(g1, g2, ACT.Square, scale=0.5).then_inc(sqm, 1)
                for n in range(4):
                    last = act.mul(yT[:, n, :], g2[:, n * TC:(n + 1) * TC], kcol[:, 4 + n:5 + n])
                last.then_inc(mixin, 1)
                take(("ms", c), lambda b: act.activation(rsmix, b[:, 0:4], ACT.Sqrt, scale=1.0 / SW, bias=kc[:, 0:1]))
                tick("glu", c)
                for n in range(4):
                    tick("mix", c, n)
                for tb in range(TB):
                    deviation()
                    tick("ln1", c, tb)
                load_ln("ln2_g", "ln2_b", 2 * TB * c + TB)
                transposed("x1T")
                for n in range(8):
                    take(("qx", c, n), lambda b: copy(qTx[:, n, :], b[:, 0:TC]))
                    tick("qx", c, n)

                def xexps(i):
                    act.wait_ge(xsmax, c * XH * TB + i + 1)
                    if i >= 2:
                        wait_job(act, ("xPT", c, i - 2))
                    take_exp(("xs", c, i), Px[:, i % 2, :], 1.0 / 16, nmax[:, 2 + i % 2:3 + i % 2],
                             rsum[:, 2 + i % 2:3 + i % 2], xexp, c * XH * TB + i + 1)

                for i in range(XH * TB + 1):
                    if i < XH * TB:
                        xexps(i)
                    if i:
                        h, tb = (i - 1) // TB, (i - 1) % TB
                        if tb == 0 and h >= 2:
                            wait_job(act, ("ox", c, h - 2, 1))
                        take(("xPT", c, i - 1), lambda b: copy(PTx[:, h % 2, :, tb * P:(tb + 1) * P],
                                                               b[:, 0:M_MEM].rearrange("p (m t) -> p m t", m=MB)))
                        if tb == TB - 1:
                            for dc in range(2):
                                take(("ox", c, h, dc), lambda b: copy(oTx[:, 2 * h + dc, :], b[:, 0:TC]))
                    if i < XH * TB:
                        tick("xu", c, i)
                for n in range(4):
                    tick("xo", c, n)
                for tb in range(TB):
                    deviation()
                    tick("ln2", c, tb)
                load_ln(*(("ln1_g", "ln1_b") if c + 1 < NC else ("ln3_g", "ln3_b")), 2 * TB * (c + 1))
                transposed("x2T")
                for n in range(16):
                    take(("qq", c, n), lambda b: copy(qTq[:, n, :], b[:, 0:TC]))
                    tick("qq", c, n)
                for tb in range(TB):
                    if tb:
                        act.wait_ge(s_free, c * TB + tb)
                    for g in range(4):
                        take(("ks", c, tb, g), lambda b: copy(S1[:, g * 512:(g + 1) * 512], b))
                    for n in range(9):
                        if n == 8:
                            act.wait_ge(rt_d, c * TB + tb + 1)
                            act.activation(tia, tia, ACT.Exp).then_inc(rt_a, 1)
                        tick("rt", c, tb, n)
            for item in LAST_ITEMS:
                serve(*item)
            serve("w", 2)
            for n in range(2):
                serve("uv", 3, n)
                deviation()
            serve_loop("uv", 3, 32)
            serve("w", 3)
            for n in range(2):
                serve("v", 3, n)
            deviation()
            serve_loop("v", 3, 16)
            deviation()

        @block.gpsimd
        def _(pool):
            chain = [0]

            def step(ins):
                ins.then_inc(pool_c, 1)
                chain[0] += 1
                pool.wait_ge(pool_c, chain[0])

            def gather(s, table, index):
                pool.indirect_dma_start(rowbuf[s], None, a[table][0], bass.IndirectOffsetOnAxis(index, 0)).then_inc(row_land[s], 16)

            def wait_buffer(unit, s, i=0):
                if type(i) is not int:
                    eng, per, at = in_loop(unit, s, 1)
                    pool.wait_ge(used_sem[eng], i * per + at)
                elif UNIT_NO[unit]:
                    eng, at = USED[UNITS[UNIT_NO[unit] - 1]][s]
                    pool.wait_ge(used_sem[eng], at)

            def serve(kind, tb, n=0):
                if kind in ("w", "o"):
                    return
                if n == 0 and kind != "v":
                    pool.wait_ge(route_ok, tb + 1)
                for s in range(NSL):
                    wait_buffer((kind, tb, n), s)
                    if kind == "uv":
                        t_, hk = (tb, 4 * n + s // 2) if s % 2 == 0 else (tb - 1, 4 * n + s // 2)
                    else:
                        t_, hk = tb, NSL * n + s
                    table = "v_tab" if kind == "v" or (kind == "uv" and s % 2) else "u_tab"
                    gather(s, table, ids_t[:, t_ * HK + hk:t_ * HK + hk + 1])

            tick = server(serve)
            stages = [0]

            def serve_loop(kind, tb, units):
                base = stages[0]
                with pool.Fori(1, units // 2) as m:
                    i = m * 2
                    for p in range(2):
                        if kind == "uv":
                            st = idstage[:, p, :].rearrange("p (n e) -> p n e", e=2)
                            pool.tensor_copy(st[:, :, 0], ids_t[:, bass.ds(i * 4 + (tb * HK + 4 * p), 4)])
                            pool.tensor_copy(st[:, :, 1], ids_t[:, bass.ds(i * 4 + ((tb - 1) * HK + 4 * p), 4)]).then_inc(stage_ok, 1)
                        else:
                            pool.tensor_copy(idstage[:, p, :], ids_t[:, bass.ds(i * NSL + (tb * HK + NSL * p), NSL)]).then_inc(stage_ok, 1)
                        pool.wait_ge(stage_ok, i + (base - 2 + p + 1))
                        for s in range(NSL):
                            wait_buffer((kind, tb, p), s, i)
                            pool.nop(nofuse=True)
                            gather(s, "v_tab" if kind == "v" or (kind == "uv" and s % 2) else "u_tab", idstage[:, p, s:s + 1])
                stages[0] += units - 2

            pool.memset(ones, 1.0).then_inc(fills, 1)
            pool.memset(kc[:, 0:1], 1e-6)
            pool.memset(kc[:, 1:2], 1e-5)
            pool.memset(kc[:, 3:4], 0.0)
            pool.memset(kc[:, 2:3], math.pi / 2).then_inc(fills, 1)
            pool.memset(small[:, :], 0.0).then_inc(fills, 1)

            def scale_x(c, name):
                for k in (3, 7):
                    if k == 7:
                        wait_job(pool, (name, c, KD - 1))
                        for tb in range(TB):
                            pool.tensor_scalar(xcur[:, c * TB + tb, :], xcur[:, c * TB + tb, :], ALPHA, 0.0, ALU.mult, ALU.add).then_inc(xscaled, 1)
                    tick(name, c, k)

            for c in range(NC):
                scale_x(c, "xT")
                t1, t2 = pool_t[:, 0:TC].rearrange("p (a b) -> p a b", a=16), pool_t[:, TC:2 * TC].rearrange("p (a b) -> p a b", a=16)
                pool.wait_ge(trig_ok, 4)
                if c:
                    pool.wait_ge(route_ok, TB * c)

                def table(j):
                    if j >= 2:
                        pool.wait_ge(tab_used, c * JT + j - 1)
                    cb, ca = bc(trig[:, 0, j, 0:16], 1, 16), bc(trig[:, 0, j, 16:32], 2, 16)
                    sb_, sa = bc(trig[:, 1, j, 0:16], 1, 16), bc(trig[:, 1, j, 16:32], 2, 16)
                    o = tab[:, j % 2].rearrange("p i (a b) -> p i a b", a=16)
                    pool.tensor_tensor(o[:, 0], cb, ca, ALU.mult)
                    step(pool.tensor_tensor(t1, sb_, sa, ALU.mult))
                    pool.tensor_tensor(o[:, 0], o[:, 0], t1, ALU.subtract)
                    pool.tensor_tensor(o[:, 1], sb_, ca, ALU.mult)
                    step(pool.tensor_tensor(t2, cb, sa, ALU.mult))
                    pool.tensor_tensor(o[:, 1], o[:, 1], t2, ALU.add).then_inc(tab_ok, 1)
                    pool.wait_ge(tab_ok, c * JT + j + 1)

                for n in range(10):
                    tick("proj", c, n)
                table(0)
                table(1)
                for key in ("lat", "qrot", "qn", "kn", "v"):
                    tick(key, c)
                for j in range(JT):
                    if 1 <= j < JT - 1:
                        table(j + 1)
                    tick("step", c, j)
                for key in ("gelu", "glu"):
                    tick(key, c)
                for n in range(4):
                    tick("mix", c, n)
                for tb in range(TB):
                    tick("ln1", c, tb)
                scale_x(c, "x1T")
                for key, count in (("qx", 8), ("xu", XH * TB), ("xo", 4), ("ln2", TB)):
                    for n in range(count):
                        tick(key, c, n)
                for k in (3, 7):
                    tick("x2T", c, k)
                for n in range(16):
                    tick("qq", c, n)
                for tb in range(TB):
                    for n in range(9):
                        tick("rt", c, tb, n)
            for item in LAST_ITEMS:
                serve(*item)
            for kind, tb, units in (("u", 2, 16), ("uv", 3, 32), ("v", 3, 16)):
                serve(kind, tb, 0)
                serve(kind, tb, 1)
                serve_loop(kind, tb, units)

        @block.vector
        def _(dve):
            chain = [0]

            def mark(ins):
                ins.then_inc(dve_c, 1)
                chain[0] += 1

            def settle():
                dve.wait_ge(dve_c, chain[0])

            def step(ins):
                mark(ins)
                settle()

            order = iter([n for n, e in JOBS if e == "dve"])

            def open_job(name):
                assert next(order) == name, name
                wait_job(dve, name)
                return bank_of(name)

            norms = [0]

            def layer_norm(tb, ln_value, signal):
                z = xcur[:, tb, :]
                for i in range(2):
                    mark(dve.bn_stats(st6[:, i, :], z[:, 512 * i:512 * i + 512]))
                settle()
                dve.bn_aggr(mv, st6).then_inc(var_ok, 1)
                norms[0] += 1
                dve.wait_ge(std_ok, norms[0])
                step(dve.reciprocal(std[:, 1:2], std[:, 0:1]))
                step(dve.tensor_scalar(z, z, mv[:, 0:1], std[:, 1:2], ALU.subtract, ALU.mult))
                dve.wait_ge(ln_land, ln_value)
                step(dve.tensor_tensor(z, z, lngb[:, 0:D], ALU.mult))
                dve.tensor_tensor(z, z, lngb[:, D:2 * D], ALU.add).then_inc(signal, 1)

            def dot(unit, s, dst, i=0):
                dve.wait_ge(row_land[s], i * 16 + 16 * (UNIT_NO[unit] + 1))
                dve.tensor_tensor_reduce(out=rowbuf[s], in0=rowbuf[s], in1=xcur[:, unit[1], :], scale=1.0, scalar=0.0,
                                         op0=ALU.mult, op1=ALU.add, accum_out=dst).then_inc(u_done, 1)

            def add_row(unit, s, weight, i=0):
                kind, tb, n = unit
                z = xcur[:, tb - 1 if kind == "uv" else tb, :]
                dve.wait_ge(row_land[s], i * 16 + 16 * (UNIT_NO[unit] + 1))
                if type(i) is not int:
                    _, per, at = in_loop(unit, s, 0)
                    dve.wait_ge(x_done, i * per + (at - 1))
                elif USED[unit][s][1] > 1:
                    dve.wait_ge(x_done, USED[unit][s][1] - 1)
                dve.scalar_tensor_tensor(out=z, in0=rowbuf[s], scalar=weight, in1=z, op0=ALU.mult, op1=ALU.add).then_inc(x_done, 1)

            def serve(kind, tb, n=0):
                if kind == "w":
                    dve.wait_ge(u_done, HK * (tb + 1))
                    z = xcur[:, tb, :]
                    mark(dve.tensor_scalar(z, z, ALPHA, None, ALU.mult))
                    h_, g_, w_ = hbuf[:, tb % 2, :], gel[:, tb % 2, :], wbuf[:, tb % 2, :]
                    step(dve.tensor_tensor(g_, h_, h_, ALU.mult))
                    step(dve.tensor_scalar(g_, g_, 0.044715, 1.0, ALU.mult, ALU.add))
                    dve.tensor_tensor(g_, g_, h_, ALU.mult).then_inc(h_ok, 1)
                    step(dve.tensor_scalar(h_, h_, 0.5, None, ALU.mult))
                    dve.wait_ge(h_act, tb + 1)
                    step(dve.scalar_tensor_tensor(out=g_, in0=g_, scalar=1.0, in1=h_, op0=ALU.add, op1=ALU.mult))
                    dve.tensor_tensor(w_, g_, gates_t[:, tb * HK:(tb + 1) * HK], ALU.mult).then_inc(w_ok, 1)
                    dve.wait_ge(w_ok, tb + 1)
                    return
                if kind == "o":
                    dve.wait_ge(v_done, rows_of_block(tb, "v"))
                    if rows_of_block(tb, "x"):
                        dve.wait_ge(x_done, rows_of_block(tb, "x"))
                    z2 = xcur[:, tb, :].rearrange("p (i n) -> p i n", i=2)
                    dve.tensor_tensor(z2, z2, psum[:, OB:OB + 2, :], ALU.add).then_inc(peer_out, 1)
                    return
                for s in range(NSL):
                    if s in vector_slots(kind, tb, n):
                        vt, hk = (tb - 1, 4 * n + s // 2) if kind == "uv" else (tb, NSL * n + s)
                        add_row((kind, tb, n), s, wbuf[:, vt % 2, hk:hk + 1])
                    elif s not in V_SLOTS[kind]:
                        hk = NSL * n + s if kind == "u" else 4 * n + s // 2
                        dot((kind, tb, n), s, hbuf[:, tb % 2, hk:hk + 1])

            tick = server(serve)
            stored, staged = [0], [0]

            def serve_loop(kind, tb, units):
                s0, w0 = stored[0], staged[0]
                n_dots = NSL - len(V_SLOTS[kind])
                with dve.Fori(1, units // 2) as m:
                    i = m * 2
                    for p in range(2):
                        unit = (kind, tb, p)
                        if vector_slots(*unit):
                            dve.wait_ge(w8_ok, i + (w0 - 2 + p + 1))
                        for s in range(NSL):
                            if s in vector_slots(*unit):
                                at = V_SLOTS[kind].index(s)
                                add_row(unit, s, w8[:, p, at:at + 1], i)
                            elif s not in V_SLOTS[kind]:
                                d = s if kind == "u" else s // 2
                                dot(unit, s, h8[:, p, d:d + 1], i)
                        if n_dots:
                            dve.wait_ge(u_done, i * n_dots + (HK * tb + n_dots * (p + 1)))
                            dve.tensor_copy(hbuf[:, tb % 2, bass.ds(i * n_dots + n_dots * p, n_dots)], h8[:, p, 0:n_dots]).then_inc(dots_ok, 1)
                            dve.wait_ge(dots_ok, i + (s0 - 2 + p + 1))
                if kind != "v":
                    stored[0] += units - 2
                if kind != "u":
                    staged[0] += units - 2

            li, dtl, dt, mag, cosr, sinr, absr, a1, red = par[1:10]
            lr = par[0]
            k_, th, t0, t1, nr, ni, den, fre, fim, rden, rt, rhi, rlo = par[10:23]

            dve.wait_ge(par_land, 16 * 9)
            dve.tensor_copy(rows[32:48, :].rearrange("j (g q) -> j g q", g=2), bc(ldt[32:48, :], 2, NS)).then_inc(rows_ok, 1)
            b = open_job(("cols",))
            dve.tensor_copy(cols[:, 0:69], b[:, 0:69]).then_inc(emptied["dve"], 1)
            wait_emptied(dve, ("cols",))
            dve.tensor_copy(lr, cols[:, 0:16])
            dve.tensor_scalar(kcol[:, 0:4], cols[:, 57:61], 0.5, None, ALU.mult)
            dve.tensor_scalar(kcol[:, 4:8], cols[:, 65:69], 0.5, None, ALU.mult)
            dve.tensor_copy(li, cols[:, 16:32]).then_inc(par_dve, 1)
            dve.wait_ge(par_act, 1)
            step(dve.tensor_tensor(th, li, dt, ALU.mult))
            dve.tensor_tensor(a1, lr, dt, ALU.mult).then_inc(par_dve, 1)

            def reduce_angle(dst, src, kbuf):
                step(dve.tensor_scalar(kbuf, src, INV2PI, MAGIC, ALU.mult, ALU.add))
                step(dve.tensor_scalar(kbuf, kbuf, -MAGIC, None, ALU.add))
                step(dve.scalar_tensor_tensor(out=dst, in0=kbuf, scalar=-C1, in1=src, op0=ALU.mult, op1=ALU.add))
                step(dve.scalar_tensor_tensor(out=dst, in0=kbuf, scalar=-C2, in1=dst, op0=ALU.mult, op1=ALU.add))
                step(dve.scalar_tensor_tensor(out=dst, in0=kbuf, scalar=-C3, in1=dst, op0=ALU.mult, op1=ALU.add))
                return dve.tensor_scalar(dst, dst, PI_IN, -PI_IN, ALU.min, ALU.max)

            reduce_angle(red, th, k_).then_inc(par_dve, 1)
            dve.wait_ge(par_dve, 3)
            step(dve.tensor_scalar(rt, red, INV2PI, None, ALU.mult))
            step(dve.tensor_scalar(rhi, rt, MAGIC / 2 ** 14, None, ALU.add))
            step(dve.tensor_scalar(rhi, rhi, -MAGIC / 2 ** 14, None, ALU.add))
            step(dve.tensor_tensor(rlo, rt, rhi, ALU.subtract))
            m3 = bc(mult32, 1, JT)
            fa = ang[:, 0:512].rearrange("p (j m) -> p j m", j=JT)
            fb = ang[:, 2048:2560].rearrange("p (j m) -> p j m", j=JT)
            fc = ang[:, 2560:3072].rearrange("p (j m) -> p j m", j=JT)
            dve.wait_ge(c_land, 16)
            step(dve.tensor_tensor(fa, m3, bc(rhi, 2, 32), ALU.mult))
            step(dve.tensor_scalar(fb, fa, MAGIC, None, ALU.add))
            step(dve.tensor_scalar(fb, fb, -MAGIC, None, ALU.add))
            step(dve.tensor_tensor(fa, fa, fb, ALU.subtract))
            step(dve.tensor_tensor(fc, m3, bc(rlo, 2, 32), ALU.mult))
            step(dve.tensor_tensor(fa, fa, fc, ALU.add))
            step(dve.tensor_scalar(fb, fa, MAGIC, None, ALU.add))
            step(dve.tensor_scalar(fb, fb, -MAGIC, None, ALU.add))
            dve.tensor_tensor(fa, fa, fb, ALU.subtract).then_inc(par_dve, 1)
            dve.wait_ge(pos_land, 16)
            posf = ang[:, 2048:2560]
            dve.wait_ge(par_dve, 4)
            step(dve.tensor_copy(posf, pos_i))
            step(dve.tensor_scalar(posf, posf, freq, None, ALU.mult))
            reduce_angle(ang[:, 1024:1536], posf, ang[:, 2560:3072]).then_inc(par_dve, 1)

            dve.wait_ge(par_act, 4)
            dve.wait_ge(bc_land, 64)
            step(dve.tensor_tensor(t0, mag, cosr, ALU.mult))
            step(dve.tensor_tensor(ni, mag, sinr, ALU.mult))
            step(dve.tensor_scalar(nr, t0, -1.0, None, ALU.add))
            dve.tensor_copy(magc, mag)
            step(dve.tensor_tensor(den, lr, lr, ALU.mult))
            step(dve.tensor_tensor(t1, li, li, ALU.mult))
            step(dve.tensor_tensor(den, den, t1, ALU.add))
            step(dve.reciprocal(rden, den))
            step(dve.tensor_tensor(fre, nr, lr, ALU.mult))
            step(dve.tensor_tensor(t0, ni, li, ALU.mult))
            step(dve.tensor_tensor(fre, fre, t0, ALU.add))
            step(dve.tensor_tensor(fre, fre, rden, ALU.mult))
            step(dve.tensor_tensor(fim, ni, lr, ALU.mult))
            step(dve.tensor_tensor(t1, nr, li, ALU.mult))
            step(dve.tensor_tensor(fim, fim, t1, ALU.subtract))
            step(dve.tensor_tensor(fim, fim, rden, ALU.mult))
            fr, fi = bc(fre, 2, GC), bc(fim, 2, GC)
            dve.tensor_tensor(bbw[:, 0], bnat[:, 0], fr, ALU.mult)
            dve.tensor_tensor(bbw[:, 1], bnat[:, 1], fi, ALU.mult)
            dve.tensor_tensor(bbw[:, 2], bnat[:, 1], fr, ALU.mult)
            step(dve.tensor_tensor(bbw[:, 3], bnat[:, 0], fi, ALU.mult))
            step(dve.memset(bbpad, 0.0))
            for i, op in enumerate((ALU.subtract, ALU.add)):
                for g in range(2):
                    ps = slice(64 * g, 64 * g + 64)
                    o = bbpad[ps, i].rearrange("p q (r g h) -> p q r g h", g=2, h=GC)[:, :, :, g, :]
                    x0 = bbw[ps, 2 * i].rearrange("p (q r) h -> p q r h", r=4)
                    x1 = bbw[ps, 2 * i + 1].rearrange("p (q r) h -> p q r h", r=4)
                    mark(dve.tensor_tensor(o, x0, x1, op))
            for i in range(2):
                for q in range(4):
                    last = dve.tensor_tensor(cdup[:, i, q, :].rearrange("p (g s) -> p g s", g=2), bc(cnat[:, i, q, :], 1, 2),
                                             parity.rearrange("p (g s) -> p g s", g=2), ALU.mult)
            last.then_inc(bt_ok, 1)

            for c in range(NC):
                tok = slice(c * TC, (c + 1) * TC)
                for k in (3, 7):
                    tick("xT", c, k)
                for n in range(10):
                    tick("proj", c, n)
                b = open_job(("krot", c))
                dve.wait_ge(trig_ok, 4)
                rr = slice(64, 96)
                mark(dve.tensor_tensor(kt1[rr, :], b[rr, 0:TC], ropeC[rr, tok], ALU.mult))
                dve.tensor_tensor(kt2[rr, :], b[rr, TC:2 * TC], ropeS[rr, tok], ALU.mult).then_inc(emptied["dve"], 1)
                settle()
                wait_emptied(dve, ("krot", c))
                if c == 0:
                    wait_job(dve, ("CT", 1))
                dve.tensor_tensor(kT[rr, :, tok], bc(kt1[rr, :], 1, H), bc(kt2[rr, :], 1, H), ALU.add).then_inc(q_ok, 1)
                wait_emptied(dve, ("ss", c))
                step(dve.reciprocal(rms, rms))
                for n in range(5):
                    r_ = rms[:, 0:TC] if n < 2 else rms[:, TC:2 * TC]
                    dve.scalar_tensor_tensor(out=cT[:, n, :], in0=cT[:, n, :], scalar=cols[:, 48 + n:49 + n], in1=r_,
                                             op0=ALU.mult, op1=ALU.mult).then_inc(c_ok, 1)
                tick("lat", c)
                b = open_job(("qrot", c))
                mark(dve.tensor_tensor(qtmp, b.rearrange("p (g t) -> p g t", g=2), bc(ropeS[:, tok], 1, 2), ALU.mult))
                settle()
                dve.sem_inc(emptied["dve"], 1)
                step(dve.tensor_tensor(qraw, qraw, bc(ropeC[:, tok], 1, 2), ALU.mult))
                for g in range(2):
                    for i in range(4):
                        ps = slice(32 * i, 32 * i + 32)
                        last = dve.tensor_tensor(qT[rr, 4 * g + i, :], qraw[ps, g, :], qtmp[ps, g, :], ALU.add)
                last.then_inc(q_ok, 1)
                for key in ("qrot", "qn", "kn", "v"):
                    tick(key, c)

                def row_max(i):
                    keys = (c * TB + i % TB + 1) * P
                    wait_job(dve, ("sc", c, i))
                    if c or i:
                        dve.wait_ge(smax, c * JT + i)
                    b = bank_of(("sc", c, i))
                    step(dve.tensor_tensor(b[:, keys - P:keys], b[:, keys - P:keys], causal, ALU.add))
                    step(dve.tensor_reduce(gsum[:, 0:1], b[:, 0:keys], AX.X, ALU.max, negate=True))
                    dve.tensor_scalar(nmax[:, i % 2:i % 2 + 1], gsum[:, 0:1], DQ ** -0.5, None, ALU.mult).then_inc(smax, 1)

                def take_y(q):
                    dve.wait_ge(y_mm, c * JT + 4 * q + 4)
                    dve.scalar_tensor_tensor(out=yT[:, q, :], in0=uT[:, q, :], scalar=cols[:, 53 + q:54 + q],
                                             in1=psum[:, YBANK, (q % 2) * TC:(q % 2 + 1) * TC], op0=ALU.mult, op1=ALU.add).then_inc(y_ok, 1)

                for j in range(JT):
                    row_max(j)
                    b = open_job(("bu", c, j)).rearrange("p (i t) -> p i t", i=2)
                    dve.wait_ge(tab_ok, c * JT + j + 1)
                    cs, sn = bc(tab[:, j % 2, 0, :], 1, 2), bc(tab[:, j % 2, 1, :], 1, 2)
                    mark(dve.tensor_tensor(sA, b, cs, ALU.mult))
                    mark(dve.tensor_tensor(sB, b, sn, ALU.mult))
                    settle()
                    dve.sem_inc(emptied["dve"], 1)
                    mark(dve.tensor_tensor(sW[:, 0], sA[:, 0], sB[:, 1], ALU.add))
                    mark(dve.tensor_tensor(sW[:, 1], sA[:, 1], sB[:, 0], ALU.subtract))
                    settle()
                    for i in range(2):
                        mark(dve.tensor_tensor_scan(sW[:, i, :], magc[:, j:j + 1].to_broadcast([P, TC]), sW[:, i, :],
                                                    0.0 if c == 0 else carry[:, j, i:i + 1], ALU.mult, ALU.add))
                    settle()
                    keys = (c * TB + j % TB + 1) * P
                    dve.wait_ge(pexp, c * JT + j + 1)
                    step(dve.reciprocal(gsum[:, 1:2], rsum[:, j % 2:j % 2 + 1]))
                    dve.tensor_scalar(Pq[:, j % 2, 0:keys], Pq[:, j % 2, 0:keys], gsum[:, 1:2], None, ALU.mult).then_inc(pn, 1)
                    mark(dve.tensor_tensor(sA, sW, cs, ALU.mult))
                    mark(dve.tensor_tensor(sB, sW, sn, ALU.mult))
                    settle()
                    dve.sem_inc(tab_used, 1)
                    if c * JT + j >= 2:
                        dve.wait_ge(y_mm, c * JT + j - 1)
                    mark(dve.tensor_tensor(sS[:, j % 2, 0, :], sA[:, 0], sB[:, 1], ALU.subtract))
                    mark(dve.tensor_tensor(sS[:, j % 2, 1, :], sA[:, 1], sB[:, 0], ALU.add))
                    settle()
                    dve.tensor_copy(carry[:, j, :], sS[:, j % 2, :, TC - 1]).then_inc(st_ok, 1)
                    if j and j % 4 == 0:
                        take_y(j // 4 - 1)
                    tick("step", c, j)
                take_y(3)
                dve.wait_ge(gl_act, 3 * c + 1)
                dve.tensor_scalar(g1, g1, 0.044715, 1.0, ALU.mult, ALU.add).then_inc(gl_dve, 1)
                dve.wait_ge(gl_dve, 4 * c + 1)
                yTf = scratch[:, 1024:2048]
                dve.tensor_tensor(g1, g1, yTf, ALU.mult).then_inc(gl_dve, 1)
                dve.wait_ge(gl_act, 3 * c + 3)
                dve.scalar_tensor_tensor(out=yTf, in0=g1, scalar=1.0, in1=g2, op0=ALU.add, op1=ALU.mult).then_inc(gl_dve, 1)
                tick("gelu", c)
                wait_emptied(dve, ("glu", c, 3))
                dve.wait_ge(gl_dve, 4 * c + 3)
                dve.scalar_tensor_tensor(out=g2, in0=g1, scalar=1.0, in1=yTf, op0=ALU.add, op1=ALU.mult).then_inc(gl_dve, 1)
                wait_emptied(dve, ("ms", c))
                step(dve.reciprocal(rsmix, rsmix))
                tick("glu", c)
                dve.wait_ge(xscaled, TB * (2 * c + 1))
                for n in range(4):
                    for tb in range(TB):
                        z = xcur[:, c * TB + tb, PW * n:PW * (n + 1)]
                        b = open_job(("mix", c, n, tb))
                        step(dve.scalar_tensor_tensor(out=z, in0=b[:, 0:PW], scalar=rsmix[:, tb:tb + 1], in1=z,
                                                      op0=ALU.mult, op1=ALU.add))
                        dve.scalar_tensor_tensor(out=z, in0=b[:, PW:2 * PW], scalar=rsmix[:, 2 + tb:3 + tb], in1=z,
                                                 op0=ALU.mult, op1=ALU.add).then_inc(emptied["dve"], 1)
                    tick("mix", c, n)
                wait_emptied(dve, ("mix", c, 3, TB - 1))
                for tb in range(TB):
                    layer_norm(c * TB + tb, 32 * (2 * c + 1), ln_ok)
                    tick("ln1", c, tb)
                for k in (3, 7):
                    tick("x1T", c, k)
                for n in range(8):
                    tick("qx", c, n)
                def xrow_max(i):
                    wait_job(dve, ("xs", c, i))
                    if c or i:
                        dve.wait_ge(xsmax, c * XH * TB + i)
                    b = bank_of(("xs", c, i))
                    step(dve.tensor_reduce(gsum[:, 2:3], b[:, 0:M_MEM], AX.X, ALU.max, negate=True))
                    dve.tensor_scalar(nmax[:, 2 + i % 2:3 + i % 2], gsum[:, 2:3], 1.0 / 16, None, ALU.mult).then_inc(xsmax, 1)

                for i in range(XH * TB):
                    xrow_max(i)
                    dve.wait_ge(xexp, c * XH * TB + i + 1)
                    if c or i:
                        dve.wait_ge(xpn, c * XH * TB + i)
                    step(dve.reciprocal(gsum[:, 3:4], rsum[:, 2 + i % 2:3 + i % 2]))
                    dve.tensor_scalar(Px[:, i % 2, :], Px[:, i % 2, :], gsum[:, 3:4], None, ALU.mult).then_inc(xpn, 1)
                    tick("xu", c, i)
                dve.wait_ge(xscaled, TB * (2 * c + 2))
                for n in range(4):
                    for tb in range(TB):
                        z = xcur[:, c * TB + tb, PW * n:PW * (n + 1)]
                        b = open_job(("xo", c, n, tb))
                        dve.tensor_tensor(z, b[:, 0:PW], z, ALU.add).then_inc(emptied["dve"], 1)
                    tick("xo", c, n)
                wait_emptied(dve, ("xo", c, 3, TB - 1))
                for tb in range(TB):
                    layer_norm(c * TB + tb, 32 * (2 * c + 2), ln_ok)
                    tick("ln2", c, tb)
                for k in (3, 7):
                    tick("x2T", c, k)
                for n in range(16):
                    tick("qq", c, n)
                for tb in range(TB):
                    tg = c * TB + tb
                    wait_emptied(dve, ("ks", c, tb, 3))

                    def top16(vals, idx, n, s0, s1):
                        lo, hi = slice(16 * n, 16 * n + 8), slice(16 * n + 8, 16 * n + 16)
                        step(dve.max(vals[:, lo], s0))
                        mark(dve.max_index(idx[:, lo], vals[:, lo], s0))
                        step(dve.match_replace(s1, vals[:, lo], s0, -3e38))
                        step(dve.max(vals[:, hi], s1))
                        mark(dve.max_index(idx[:, hi], vals[:, hi], s1))

                    for n in range(2 * PH):
                        top16(rv, ridx, n, S1[:, n * NK:(n + 1) * NK], rest[:, n % 2, 0:NK])
                        if n % 4 == 3:
                            tick("rt", c, tb, n // 4)
                    settle()
                    mark(dve.tensor_copy(rif, ridx))
                    rvv = rv.rearrange("p (h s k) -> p h s k", h=PH, s=2)
                    cand = S1.rearrange("p (h a b) -> p h a b", h=PH, a=TOPK)
                    step(dve.tensor_tensor(cand, bc(rvv[:, :, 0, :], 3, TOPK), bc(rvv[:, :, 1, :], 2, TOPK), ALU.add))
                    for h in range(PH):
                        top16(tops, tpos, h, S1[:, h * 256:(h + 1) * 256], rest[:, h % 2, :])
                        if h % 4 == 3:
                            tick("rt", c, tb, 4 + h // 4)
                    settle()
                    mark(dve.tensor_scalar(tau, tpos, 4, None, ALU.logical_shift_right))
                    step(dve.tensor_scalar(tbu, tpos, 15, None, ALU.bitwise_and))
                    mark(dve.tensor_copy(tab_a, tau))
                    step(dve.tensor_copy(tab_b, tbu))
                    rifv = rif.rearrange("p (h s k) -> p h s k", h=PH, s=2)
                    e = S1.rearrange("p (h k m) -> p h k m", h=PH, k=TOPK)
                    for s, place, dst in ((0, tab_a, tia), (1, tab_b, tib)):
                        pl = bc(place.rearrange("p (h k) -> p h k", h=PH), 3, TOPK)
                        io = bc(bc(iota16, 1, TOPK), 1, PH)
                        step(dve.tensor_tensor(e, pl, io, ALU.is_equal))
                        step(dve.tensor_tensor(e, e, bc(rifv[:, :, s, :], 2, TOPK), ALU.mult))
                        step(dve.tensor_reduce(dst, e, AX.X, ALU.add))
                        tick("rt", c, tb, 6 + s)
                    step(dve.scalar_tensor_tensor(out=ids_t[:, tg * HK:(tg + 1) * HK], in0=tia, scalar=float(NK), in1=tib,
                                                  op0=ALU.mult, op1=ALU.add))
                    tv, ti = (t.rearrange("p (h k) -> p h k", h=PH) for t in (tops, tia))
                    dve.tensor_tensor(ti, tv, bc(tv[:, :, 0], 2, TOPK), ALU.subtract).then_inc(rt_d, 1)
                    dve.wait_ge(rt_a, tg + 1)
                    step(dve.tensor_reduce(gsum[:, 0:8], ti, AX.X, ALU.add))
                    step(dve.reciprocal(gsum[:, 0:8], gsum[:, 0:8]))
                    step(dve.tensor_tensor(gates_t[:, tg * HK:(tg + 1) * HK].rearrange("p (h k) -> p h k", h=PH),
                                           ti, bc(gsum[:, 0:8], 2, TOPK), ALU.mult))
                    dve.sem_inc(s_free, 1)
                    dve.sem_inc(route_ok, 1)
                    tick("rt", c, tb, 8)

            for item in LAST_ITEMS:
                serve(*item)
            ln3 = 32 * (2 * NC + 1)
            for n in range(2):
                serve("u", 2, n)
            serve_loop("u", 2, 16)
            serve("w", 2)
            for n in range(2):
                serve("uv", 3, n)
                dve.wait_ge(peer_out, 2)
                layer_norm(n, ln3, fin_ok)
            serve_loop("uv", 3, 32)
            serve("o", 2)
            serve("w", 3)
            for n in range(2):
                serve("v", 3, n)
            dve.wait_ge(peer_out, 3)
            layer_norm(2, ln3, fin_ok)
            serve_loop("v", 3, 16)
            serve("o", 3)
            dve.wait_ge(peer_out, 4)
            layer_norm(3, ln3, fin_ok)


NAMES = ["x", "mem", "positions", "w_in", "g_cq", "w_uq", "g_ckv", "w_ukv", "lam_re", "lam_im", "log_dt", "b_re", "b_im",
         "c_re", "c_im", "d_skip", "w_glu", "b_glu", "g_mla_out", "g_ssm_out", "w_out", "ln1_g", "ln1_b", "xq", "xk", "xv",
         "xo", "ln2_g", "ln2_b", "w_query", "sub_keys1", "sub_keys2", "u_tab", "v_tab", "ln3_g", "ln3_b"]
STOP = None


def kernel(**inputs):
    import concourse.bacc as bacc
    from concourse.bass_utils import run_bass_kernel_spmd

    nc = bacc.Bacc("TRN2", target_bir_lowering=False, num_devices=1)
    arrays, args = {}, {}
    for name in NAMES:
        arr = np.ascontiguousarray(inputs[name])
        arrays["in_" + name] = arr
        args[name] = nc.dram_tensor("in_" + name, arr.shape, mybir.dt.from_np(arr.dtype), kind="ExternalInput").ap()
    arrays["in_consts"] = shape_constants()
    consts = nc.dram_tensor("in_consts", (P, CW), F32, kind="ExternalInput").ap()
    out = nc.dram_tensor("out", (1, T, D), F32, kind="ExternalOutput").ap()
    build(nc, args, consts, out, STOP)
    r = run_bass_kernel_spmd(nc, [arrays], core_ids=[0])
    return r.results[0]["out"]
```

```python
import math
from contextlib import ExitStack

import numpy as np
import concourse.bass as bass
from concourse import mybir

F32 = mybir.dt.float32
U32 = mybir.dt.uint32
I32 = mybir.dt.int32
ALU = mybir.AluOpType
ACT = mybir.ActivationFunctionType
AX = mybir.AxisListType

P = 128
D = 1024
T = 512
TC = 256
NC = T // TC
TB = TC // P
NTB = T // P
KD = D // P
M_MEM = 256
MB = M_MEM // P
H = 8
NOPE, ROPE, VH = 64, 32, 64
DQ = NOPE + ROPE
QL, KVL, SW = 384, 256, 512
XH = 4
G, NS, GC = 32, 64, 16
JT = G // 2
PH, NK, TOPK = 8, 128, 16
HK = PH * TOPK
ALPHA = 2.0 ** 0.25
MAGIC = 12582912.0
INV2PI = float(1.0 / (2.0 * math.pi))
C1 = 6.28125
C2 = float(np.float32(round((2 * math.pi - C1) * 2 ** 18) / 2 ** 18))
C3 = float(2 * math.pi - C1 - C2)
PI_IN = 3.1415925
GELU_C = math.sqrt(2.0 / math.pi)
RB = 5
YBANK = 5
OB = 6
SLOTS = 4
SLOT = 2048
PW = 256
NSL = 8
DB = 4
CW = 6 * P + 32 + 16 + 1


def shape_constants():
    c = np.zeros((P, CW), np.float32)
    r = np.arange(P)
    c[:, 0:128] = np.eye(P)
    c[:, 128:256] = np.where(r[None, :] <= r[:, None], 0.0, -1e30)
    c[:, 256:384] = ((r[:, None] // 16) % 2 == (r[None, :] // 64))
    rot = np.zeros((P, P), np.float32)
    for m in range(P):
        if m % 32 < 16:
            rot[m + 16, m] = -1.0
        else:
            rot[m - 16, m] = 1.0
    c[:, 384:512] = rot
    c[0:32, 512:640] = np.tile(np.eye(32), (1, 4))
    c[0:32, 640:768] = np.tile(rot[0:32, 0:32], (1, 4))
    c[:, 768:784] = np.arange(1, 17)
    c[:, 784:800] = 16 * np.arange(16)
    c[:, 800:816] = np.arange(16)
    c[:, 816] = (np.float32(10000.0) ** (-np.arange(16, dtype=np.float32) / 16))[r % 16]
    return c


def bc(ap, axis, n):
    a = ap.unsqueeze(axis)
    shape = list(a.shape)
    shape[axis] = n
    return a.to_broadcast(shape)


def jobs_of_pe():
    jobs = []
    for c in range(NC):
        if c == 0:
            jobs.append((("cols",), "dve"))
        jobs += [(("xT", c, k), "act") for k in range(KD)]
        jobs += [(("u", c, n), "act") for n in range(4)]
        jobs += [(("kr", c), "act")]
        jobs += [(("ckv", c, n), "act") for n in range(2)]
        jobs += [(("cq", c, n), "act") for n in range(3)]
        jobs.append((("krot", c), "dve"))
        if c == 0:
            jobs += [(("BT", i), "act") for i in range(2)] + [(("CT", i), "act") for i in range(2)]
        jobs.append((("ss", c), "act"))
        if c == 0:
            jobs += [(("memT", k), "act") for k in range(KD // 2)]
            jobs.append((("keysT",), "act"))
        jobs += [(("qrope", c, g), "act") for g in range(2)]
        jobs.append((("qrot", c), "dve"))
        jobs += [(("qn", c, i), "act") for i in range(4)]
        jobs += [(("kn", c, i), "act") for i in range(4)]
        jobs += [(("v", c, tb), "act") for tb in range(TB)]
        jobs.append((("bu", c, 0), "dve"))
        jobs.append((("sc", c, 0), "act"))
        for j in range(JT + 1):
            if c == 0 and j < JT:
                jobs.append((("mem", j), "act"))
            if j + 1 < JT:
                jobs.append((("bu", c, j + 1), "dve"))
            if j:
                jobs.append((("PT", c, j - 1), "act"))
            if j and j % TB == 0:
                jobs.append((("pv", c, j // TB - 1), "act"))
            if j + 1 < JT:
                jobs.append((("sc", c, j + 1), "act"))
        jobs += [(("glu", c, n), "act") for n in range(4)]
        jobs.append((("ms", c), "act"))
        jobs += [(("mix", c, n, tb), "dve") for tb in range(TB) for n in range(4)]
        jobs += [(("x1T", c, k), "act") for k in range(KD)]
        jobs += [(("qx", c, n), "act") for n in range(8)]
        jobs += [(("xs", c, i), "act") for i in range(2)]
        for i in range(XH * TB + 1):
            if i:
                jobs.append((("xPT", c, i - 1), "act"))
            if i and i % TB == 0:
                jobs += [(("ox", c, i // TB - 1, dc), "act") for dc in range(2)]
            if i + 2 < XH * TB:
                jobs.append((("xs", c, i + 2), "act"))
        jobs += [(("xo", c, n, tb), "dve") for tb in range(TB) for n in range(4)]
        jobs += [(("x2T", c, k), "act") for k in range(KD)]
        for n in range(17):
            if n < 16:
                jobs.append((("qq", c, n), "act"))
            if n and n % 4 == 0:
                jobs.append((("ks", c, 0, n // 4 - 1), "act"))
        jobs += [(("ks", c, tb, g), "act") for tb in range(1, TB) for g in range(4)]
    return jobs


JOBS = jobs_of_pe()
NUM = {name: n for n, (name, _) in enumerate(JOBS)}
EMPTIED = {}
_count = {"act": 0, "dve": 0}
for _name, _eng in JOBS:
    _count[_eng] += 1
    EMPTIED[_name] = _count[_eng]


def weight_pieces():
    out = []
    for c in range(NC):
        out += [("u", c, n, ("u", c, 2 * n + 1), KD, PW, 1) for n in range(2)]
        out += [("kr", c, 0, ("kr", c), KD, ROPE, 1), ("ckv", c, 0, ("ckv", c, 1), KD, PW, 1)]
        out += [("cq", c, 0, ("cq", c, 1), KD, PW, 1), ("cq", c, 1, ("cq", c, 2), KD, P, 1)]
        out += [("uqr", c, 0, ("qrope", c, 1), 3, H * ROPE, 3), ("uqn", c, 0, ("qn", c, 3), 3, H * NOPE, 3)]
        out += [("ukn", c, 0, ("kn", c, 3), 2, H * NOPE, 2), ("ukv", c, 0, ("v", c, TB - 1), 2, H * VH, 2)]
        if c == 0:
            out += [("xk", 0, n, ("mem", 2 * n + 1), KD, PW, 1) for n in range(4)]
            out += [("xv", 0, n, ("mem", 8 + 2 * n + 1), KD, PW, 1) for n in range(4)]
        out += [("glu", c, 0, ("glu", c, 3), 4, SW, 1)]
        out += [("wo", c, n, ("mix", c, n, TB - 1), KD, PW, 1) for n in range(4)]
        out += [("xq", c, n, ("qx", c, 2 * n + 1), KD, PW, 1) for n in range(4)]
        out += [("xo", c, n, ("xo", c, n, TB - 1), KD, PW, 1) for n in range(4)]
        out += [("wq", c, n, ("qq", c, 2 * n + 1), KD, PW, 1) for n in range(8)]
    return [(p[0:3],) + p[3:] for p in out]


PIECES = weight_pieces()
PNUM = {p[0]: n for n, p in enumerate(PIECES)}
LANDED = {}
_landed = [0] * SLOTS
for _n, _p in enumerate(PIECES):
    _landed[_n % SLOTS] += 16 * _p[4]
    LANDED[_p[0]] = _landed[_n % SLOTS]


def peer_items():
    out = [("u", 0, n) for n in range(HK // NSL)] + [("w", 0)]
    out += [("uv", 1, n) for n in range(2 * HK // NSL)] + [("w", 1), ("o", 0)]
    return out + [("v", 1, n) for n in range(HK // NSL)] + [("o", 1)]


def chain_ticks():
    out = [("rt", 0, tb, n) for tb in range(TB) for n in range(9)]
    c = 1
    out += [("xT", c, k) for k in (3, 7)]
    out += [("proj", c, n) for n in range(10)]
    out += [("lat", c), ("qrot", c), ("qn", c), ("kn", c), ("v", c)]
    out += [("step", c, j) for j in range(JT)]
    out += [("gelu", c), ("glu", c)]
    for tb in range(TB):
        out += [("mix", c, 2 * tb), ("mix", c, 2 * tb + 1), ("ln1", c, tb)]
    out += [("x1T", c, k) for k in (3, 7)]
    out += [("qx", c, n) for n in range(8)]
    out += [("xu", c, i) for i in range(XH * TB)]
    for tb in range(TB):
        out += [("xo", c, 2 * tb), ("xo", c, 2 * tb + 1), ("ln2", c, tb)]
    out += [("x2T", c, k) for k in (3, 7)]
    for n in range(17):
        if n < 16:
            out.append(("qq", c, n))
        if n and n % 4 == 0:
            out += [("rt", c, 0, n // 2 - 2), ("rt", c, 0, n // 2 - 1)]
    out.append(("rt", c, 0, 8))
    return out + [("rt", c, tb, n) for tb in range(1, TB) for n in range(9)]


WEIGHT = {"xT": 0.75, "proj": 3.6, "lat": 5.0, "qrot": 4.0, "qn": 4.85, "kn": 4.0, "v": 3.0, "step": 8.24,
          "gelu": 9.0, "glu": 5.0, "mix": 4.19, "ln1": 6.0, "x1T": 1.5, "qx": 2.1, "xu": 3.0, "xo": 3.4, "ln2": 6.0,
          "x2T": 1.5, "qq": 3.91, "rt": 7.0, "rt with queries": 2.0, "first rt": 1.5}


def weight(key):
    return WEIGHT[{("rt", 0, 0): "first rt", ("rt", 1, 0): "rt with queries"}.get(key[:3], key[0])]


ITEMS = peer_items()
TICKS = chain_ticks()


def items_at_ticks():
    whole = sum(weight(key) for key in TICKS)
    units = sum(kind in V_SLOTS for kind, *_ in ITEMS)
    left = list(ITEMS)
    at, served, out = 0.0, 0, {}
    for key in TICKS:
        at += weight(key)
        out[key] = []
        while left and (served < int(units * at / whole + 1e-6) or key == TICKS[-1]):
            item = left.pop(0)
            out[key].append(item)
            served += item[0] in V_SLOTS
    return out


V_SLOTS = {"u": (), "uv": (1, 3, 5, 7), "v": tuple(range(NSL))}
AT_TICK = items_at_ticks()
STAGE = {item: key[0] for key, items in AT_TICK.items() for item in items}

RUNS = [("u", 0, 16), ("uv", 1, 32), ("v", 1, 16), ("u", 2, 16), ("uv", 3, 32), ("v", 3, 16)]
UNITS = [(kind, tb, n) for kind, tb, units in RUNS for n in range(units)]
UNIT_NO = {unit: i for i, unit in enumerate(UNITS)}
FEW = {"proj": 1, "lat": 1, "glu": 2, "mix": 2, "ln1": 2, "x1T": 3, "qx": 2, "xu": 1, "xo": 1, "ln2": 1, "x2T": 2,
       "qq": 2, "gelu": 2}
HALF = ("qq",)


def vector_slots(kind, tb, n):
    if kind == "v":
        return (1, 3, 5, 7) if STAGE.get((kind, tb, n)) in HALF else (3, 7)
    return V_SLOTS[kind][4 - FEW.get(STAGE.get((kind, tb, n)), 0):] if kind == "uv" else ()


def rows_used():
    count = {"u": 0, "v": 0, "x": 0}
    used, after = {}, []
    for unit in UNITS:
        used[unit] = {}
        v = 0
        for s in range(NSL):
            eng = "u" if s not in V_SLOTS[unit[0]] else "x" if s in vector_slots(*unit) else "v"
            count[eng] += 1
            used[unit][s] = (eng, count[eng])
            v += s in V_SLOTS[unit[0]]
            if eng != "u" and v % DB == 0:
                after.append(count["v"])
    return used, after


USED, AFTER_BATCH = rows_used()


def in_loop(unit, s, back):
    kind, tb, n = unit
    eng, at = USED[(kind, tb, 1)][s]
    per = sum(e == eng for e, _ in USED[(kind, tb, 1)].values())
    return eng, per, at + (n - 1 - back) * per


def rows_of_block(tb, eng):
    last = ("uv", tb + 1, 31) if tb % 2 == 0 else ("v", tb, 15)
    return max((n for i in range(UNIT_NO[last] + 1) for e, n in USED[UNITS[i]].values() if e == eng), default=0)


def build(nc, a, consts, out):
    ctx = ExitStack()
    with ctx:
        def sb(name, cols, dt=F32, rows=P):
            return ctx.enter_context(nc.sbuf_tensor(name, [rows, cols], dt))

        def sem(name):
            return ctx.enter_context(nc.semaphore(name))

        ring = sb("weight_ring", SLOTS * SLOT)
        xcur_t = sb("xcur", NTB * D)
        actT_t = sb("actT", KD * TC)
        kT_t = sb("kT", H * T)
        v_t = sb("v", NTB * H * VH)
        kTx_t = sb("kTx", 8 * M_MEM)
        vx_t = sb("vx", MB * D)
        lngb = sb("lngb", 2 * D)
        BT_t = sb("BT", 4 * 2 * P)
        CT_t = sb("CT", 2 * JT * 32)
        trig_t = sb("trig", 2 * JT * 32)
        cst = sb("cst", CW)
        cols = sb("cols", P)
        ropet = sb("ropet", 2 * T)
        keysT = sb("keysT", 2 * NK)
        ids_t = sb("ids", NTB * HK, U32)
        gates_t = sb("gates", NTB * HK)
        scratch = sb("scratch", 8960)
        rowbuf_t = sb("expert_rows", NSL * D)
        diag_t = sb("diag", 2 * DB * P)
        gelu_t = sb("gelu", 2 * TC)
        peer_t = sb("peer_small", 3 * 2 * HK + 3 * 2 * NSL)
        kc = sb("kc", 4)
        ones = sb("ones_t", P)[:, :]
        small = sb("small", 96)
        kcol = sb("kcol", 8)
        pool_t = sb("pool_t", 512)

        ident = cst[:, 0:128]
        causal = cst[:, 128:256]
        parity = cst[:, 256:384]
        rot = cst[:, 384:512]
        rep = cst[0:32, 512:640]
        reprot = cst[0:32, 640:768]
        mult32 = cst[:, 768:800]
        iota16 = cst[:, 800:816]
        freq = cst[:, 816:817]

        xcur = xcur_t[:, :].rearrange("p (t d) -> p t d", t=NTB)
        memT = xcur_t[:, 2048:4096].rearrange("p (k m) -> p k m", k=KD)
        actT = actT_t[:, :].rearrange("p (k t) -> p k t", k=KD)
        qT = actT_t[:, :].rearrange("p (h t) -> p h t", h=H)
        kT = kT_t[:, :].rearrange("p (h t) -> p h t", h=H)
        V = v_t[:, :].rearrange("p (t n) -> p t n", t=NTB)
        mem_nat = v_t[:, :].rearrange("p (b d) -> p b d", b=MB)
        kTx = kTx_t[:, :].rearrange("p (n m) -> p n m", n=8)
        vx = vx_t[:, :].rearrange("p (b d) -> p b d", b=MB)
        BT = BT_t[:, :].rearrange("p (i c m) -> p i c m", i=2, c=4)
        CT = CT_t[:, :].rearrange("p (i j h) -> p i j h", i=2, j=JT)
        trig = trig_t[:, :].rearrange("p (i j m) -> p i j m", i=2, j=JT)
        ropeC, ropeS = ropet[:, 0:T], ropet[:, T:2 * T]

        rows = kT_t[:, 0:128]
        bnat = kT_t[:, 128:640].rearrange("p (i j h) -> p i j h", i=2, j=JT)
        cnat = kT_t[:, 640:1152].rearrange("p (i c q) -> p i c q", i=2, c=4)
        bbpad = kT_t[:, 1152:2176].rearrange("p (i c m) -> p i c m", i=2, c=4)
        cdup = kT_t[:, 2176:3200].rearrange("p (i c m) -> p i c m", i=2, c=4)
        par = [kT_t[:, 3200 + 16 * i:3216 + 16 * i] for i in range(24)]
        ldt = kT_t[:, 3600:3602]
        keys_nat = kTx_t[:, 0:256].rearrange("p (i d) -> p i d", i=2)
        ang = scratch[:, 0:3072]
        pos_i = scratch[:, 3072:3584].bitcast(I32)
        bbw = scratch[:, 3584:4608].rearrange("p (i j h) -> p i j h", i=4, j=JT)

        uT = scratch[:, 0:1024].rearrange("p (n t) -> p n t", n=4)
        cT = scratch[:, 1024:2304].rearrange("p (n t) -> p n t", n=5)
        yT = scratch[:, 1024:2048].rearrange("p (n t) -> p n t", n=4)
        oT = scratch[:, 2304:3328].rearrange("p (n t) -> p n t", n=4)
        PT = scratch[:, 3328:4352].rearrange("p (k t) -> p k t", k=NTB)
        Pr = scratch[:, 4352:5376]
        Pq = Pr.rearrange("p (i n) -> p i n", i=2)
        qraw = Pr[:, 0:512].rearrange("p (g t) -> p g t", g=2)
        qtmp = Pr[:, 512:1024].rearrange("p (g t) -> p g t", g=2)
        s5 = scratch[:, 5376:8960]
        tab = s5[:, 0:1024].rearrange("p (b i t) -> p b i t", b=2, i=2)
        sA = s5[:, 1024:1536].rearrange("p (i t) -> p i t", i=2)
        sB = s5[:, 1536:2048].rearrange("p (i t) -> p i t", i=2)
        sW = s5[:, 2048:2560].rearrange("p (i t) -> p i t", i=2)
        sS = s5[:, 2560:3584].rearrange("p (b i t) -> p b i t", b=2, i=2)
        sq5 = s5[:, 1024:2304].rearrange("p (n t) -> p n t", n=5)
        kraw = s5[:, 2304:2560]
        kt1, kt2 = s5[:, 2560:2816], s5[:, 2816:3072]
        rms = s5[:, 3072:3584]
        g1, g2 = s5[:, 1024:2048], s5[:, 2048:3072]

        qTx = scratch[:, 0:2048].rearrange("p (n t) -> p n t", n=8)
        oTx = scratch[:, 2048:4096].rearrange("p (n t) -> p n t", n=8)
        Px = scratch[:, 4096:4608].rearrange("p (i m) -> p i m", i=2)
        PTx = scratch[:, 4608:5632].rearrange("p (i m t) -> p i m t", i=2, m=MB)

        qTq = scratch[:, 0:4096].rearrange("p (n t) -> p n t", n=16)
        S1 = scratch[:, 4096:6144]
        rv = scratch[:, 6144:6400]
        ridx = scratch[:, 6400:6656].bitcast(U32)
        rif = scratch[:, 6656:6912]
        tops = scratch[:, 6912:7040]
        tpos = scratch[:, 7040:7168].bitcast(U32)
        tab_a = scratch[:, 7168:7296]
        tab_b = scratch[:, 7296:7424]
        tia = scratch[:, 7424:7552]
        tib = scratch[:, 7552:7680]
        tau = scratch[:, 7680:7808].bitcast(U32)
        tbu = scratch[:, 7808:7936].bitcast(U32)
        rest = scratch[:, 7936:8448].rearrange("p (i n) -> p i n", i=2)

        rowbuf = [rowbuf_t[:, D * s:D * (s + 1)] for s in range(NSL)]
        diag = diag_t[:, :].rearrange("p (q s m) -> p q s m", q=2, s=DB)
        hbuf = peer_t[:, 0:256].rearrange("p (q n) -> p q n", q=2)
        wbuf = peer_t[:, 256:512].rearrange("p (q n) -> p q n", q=2)
        gel = peer_t[:, 512:768].rearrange("p (q n) -> p q n", q=2)
        h8 = peer_t[:, 768:784].rearrange("p (q n) -> p q n", q=2)
        w8 = peer_t[:, 784:800].rearrange("p (q n) -> p q n", q=2)
        idstage = peer_t[:, 800:816].bitcast(U32).rearrange("p (q n) -> p q n", q=2)

        nmax = small[:, 0:4]
        rsum = small[:, 4:8]
        rsmix = small[:, 8:12]
        st6 = small[:, 12:24].rearrange("p (i n) -> p i n", i=2)
        mv = small[:, 24:26]
        std = small[:, 26:28]
        carry = small[:, 32:64].rearrange("p (j i) -> p j i", j=JT)
        magc = small[:, 64:80]
        gsum = small[:, 80:88]

        psum = ctx.enter_context(nc.psum_tensor("banks", [P, 8, 512], F32))

        def bank_of(name):
            return psum[:, NUM[name] % RB, :]

        pe_done = sem("pe_done")
        emptied = {"act": sem("act_emptied"), "dve": sem("dve_emptied")}
        w_land = [sem("w_land%d" % i) for i in range(SLOTS)]
        x_land = sem("x_land")
        mem_land = sem("mem_land")
        c_land = sem("c_land")
        par_land = sem("par_land")
        pos_land = sem("pos_land")
        keys_land = sem("keys_land")
        ln_land = sem("ln_land")
        out_land = sem("out_land")
        ldt_ok = sem("ldt_ok")
        fills = sem("fills")
        dve_c = sem("dve_chain")
        act_c = sem("act_chain")
        pool_c = sem("pool_chain")
        rows_ok = sem("rows_ok")
        par_dve = sem("par_dve")
        par_act = sem("par_act")
        bt_ok = sem("bt_ok")
        trig_ok = sem("trig_ok")
        tab_ok = sem("tab_ok")
        tab_used = sem("tab_used")
        sq_ok = sem("sq_ok")
        rms_ok = sem("rms_ok")
        c_ok = sem("c_ok")
        q_ok = sem("q_ok")
        smax = sem("smax")
        pexp = sem("pexp")
        rinv_ok = sem("rinv_ok")
        pn = sem("pn")
        st_ok = sem("st_ok")
        y_mm = sem("y_mm")
        y_ok = sem("y_ok")
        gl_act = sem("gl_act")
        gl_dve = sem("gl_dve")
        mixin = sem("mixin")
        sqm = sem("sqm")
        rsm = sem("rsm")
        var_ok = sem("var_ok")
        std_ok = sem("std_ok")
        ln_ok = sem("ln_ok")
        xscaled = sem("xscaled")
        xsmax = sem("xsmax")
        xexp = sem("xexp")
        xpn = sem("xpn")
        s_free = sem("s_free")
        rt_d = sem("rt_d")
        rt_a = sem("rt_a")
        ids_ok = sem("ids_ok")
        route_ok = sem("route_ok")
        row_land = [sem("row_land%d" % i) for i in range(NSL)]
        u_done = sem("u_done")
        v_done = sem("v_done")
        x_done = sem("x_done")
        used_sem = {"u": u_done, "v": v_done, "x": x_done}
        stage_ok = sem("stage_ok")
        dots_ok = sem("dots_ok")
        w8_ok = sem("w8_ok")
        h_ok = sem("h_ok")
        h_act = sem("h_act")
        w_ok = sem("w_ok")
        diag_ok = sem("diag_ok")
        peer_out = sem("peer_out")
        fin_ok = sem("fin_ok")
        bc_land = sem("bc_land")

        block = ctx.enter_context(nc.Block())

        def wslot(name):
            n = PNUM[name]
            _, _, k, cols_, _ = PIECES[n]
            at = n % SLOTS * SLOT
            return ring[:, at:at + k * cols_].rearrange("p (k n) -> p k n", k=k)

        def wait_piece(eng, name):
            eng.wait_ge(w_land[PNUM[name] % SLOTS], LANDED[name])
            return wslot(name)

        def wait_emptied(eng, name):
            eng.wait_ge(emptied[JOBS[NUM[name]][1]], EMPTIED[name])

        def wait_job(eng, name):
            eng.wait_ge(pe_done, NUM[name] + 1)

        deep = {n: a[n][0].rearrange("(k p) n -> p k n", p=P) for n in ("w_in", "w_out", "w_query", "xq", "xk", "xv", "xo", "w_glu")}

        def piece_transfers(name):
            kind, _, n = name
            dst = wslot(name)
            if kind in ("uqr", "uqn", "ukn", "ukv"):
                src, wide, lo, hi = {"uqr": ("w_uq", DQ, NOPE, DQ), "uqn": ("w_uq", DQ, 0, NOPE),
                                     "ukn": ("w_ukv", NOPE + VH, 0, NOPE), "ukv": ("w_ukv", NOPE + VH, NOPE, NOPE + VH)}[kind]
                return [(dst[:, k, :].rearrange("p (h d) -> p h d", h=H),
                         a[src][0, k * P:(k + 1) * P, :].rearrange("p (h d) -> p h d", d=wide)[:, :, lo:hi])
                        for k in range(dst.shape[1])]
            src, at = {"u": ("w_in", QL + KVL + ROPE), "kr": ("w_in", QL + KVL), "ckv": ("w_in", QL), "cq": ("w_in", 0),
                       "glu": ("w_glu", 0), "wo": ("w_out", 0), "wq": ("w_query", 0)}.get(kind, (kind, 0))
            at += PW * n
            return [(dst, deep[src][:, :, at:at + dst.shape[2]])]

        @block.sync
        def _(sp):
            def load_x(c):
                if c:
                    wait_job(sp, ("mem", 15))
                sp.dma_start(xcur[:, c * TB:(c + 1) * TB, :],
                             a["x"][0, c * TC:(c + 1) * TC, :].rearrange("(t p) d -> p t d", p=P)).then_inc(x_land, 16)

            def load_piece(n):
                name = PIECES[n][0]
                if n >= SLOTS:
                    wait_job(sp, PIECES[n - SLOTS][1])
                for dst, src in piece_transfers(name):
                    sp.dma_start(dst, src).then_inc(w_land[n % SLOTS], 16)

            sp.dma_start(cst[:, :], consts).then_inc(c_land, 16)
            sp.dma_start(rows[0:16, :], a["lam_re"][0].rearrange("(j g) q -> j (g q)", g=2)).then_inc(par_land, 16)
            sp.dma_start(rows[16:32, :], a["lam_im"][0].rearrange("(j g) q -> j (g q)", g=2)).then_inc(par_land, 16)
            sp.dma_start(ldt[32:48, :], a["log_dt"][0].rearrange("(j g) -> j g", g=2)).then_inc(par_land, 16)
            at = 48
            for name, n in (("g_ckv", 2), ("g_cq", 3), ("d_skip", 4), ("b_glu", 4), ("g_mla_out", 4), ("g_ssm_out", 4)):
                src = a[name][0].rearrange("g h -> (g h)") if name == "d_skip" else a[name][0]
                sp.dma_start(rows[at:at + n, :], src.rearrange("(c p) -> c p", p=P)).then_inc(par_land, 16)
                at += n
            load_x(0)
            load_piece(0)
            sp.dma_start(pos_i, a["positions"][0:1, :].to_broadcast([P, T])).then_inc(pos_land, 16)
            for i, name in enumerate(("b_re", "b_im")):
                sp.dma_start(bnat[:, i], a[name][0].rearrange("(j g) q h -> (g q) j h", g=2)).then_inc(bc_land, 16)
            for i, name in enumerate(("c_re", "c_im")):
                sp.dma_start(cnat[:, i], a[name][0].rearrange("(c g) h q -> (g h) c q", c=4)).then_inc(bc_land, 16)
            for n in range(1, SLOTS):
                load_piece(n)
            sp.dma_start(mem_nat, a["mem"][0].rearrange("(b p) d -> p b d", p=P)).then_inc(mem_land, 16)
            for i, name in enumerate(("sub_keys1", "sub_keys2")):
                sp.dma_start(keys_nat[:, i], a[name][0]).then_inc(keys_land, 16)
            for n in range(SLOTS, len(PIECES)):
                load_piece(n)
                if PIECES[n][0] == ("glu", 0, 0):
                    load_x(1)
            for tb in range(NTB):
                sp.wait_ge(fin_ok, tb + 1)
                sp.dma_start(out[0, tb * P:(tb + 1) * P, :], xcur[:, tb, :]).then_inc(out_land, 16)
            sp.wait_ge(out_land, 16 * NTB)

        def server(serve):
            left = list(TICKS)

            def tick(*key):
                if key in AT_TICK:
                    assert left.pop(0) == key, key
                    for item in AT_TICK[key]:
                        serve(*item)
            return tick

        @block.tensor
        def _(pe):
            order = iter(JOBS)

            def bank(name):
                assert next(order)[0] == name
                n = NUM[name]
                if n >= RB:
                    wait_emptied(pe, JOBS[n - RB][0])
                return psum[:, n % RB, :]

            def product(outp, pairs):
                for i, (l, r) in enumerate(pairs):
                    last = pe.matmul(outp, l, r, start=(i == 0), stop=(i == len(pairs) - 1))
                return last

            def serve_at(kind, tb, n, p, i=0):
                if kind not in ("uv", "v"):
                    return
                first = n == 0 and type(i) is int
                vt = tb - 1 if kind == "uv" else tb
                unit = (kind, tb, n)
                if first and vt:
                    pe.wait_ge(peer_out, vt)
                for m, s in enumerate(V_SLOTS[kind]):
                    half = p if kind == "uv" else m // DB
                    per = len(V_SLOTS[kind]) // DB
                    if m % DB == 0:
                        pe.wait_ge(diag_ok, i * per + (HK * vt // DB + per * n + m // DB + 1))
                    if s in vector_slots(*unit):
                        continue
                    pe.wait_ge(row_land[s], i * 16 + 16 * (UNIT_NO[unit] + 1))
                    row, d = rowbuf[s], diag[:, half, m % DB, :]
                    st = first and m == 0
                    pe.matmul(psum[:, OB, :], d, row[:, 0:512], start=st, stop=False, skip_group_check=True)
                    pe.matmul(psum[:, OB + 1, :], d, row[:, 512:D], start=st, stop=False,
                              skip_group_check=True).then_inc(v_done, 1)

            def serve(kind, tb, n=0):
                serve_at(kind, tb, n, n % 2)

            tick = server(serve)

            def transposed(name, c, ready):
                for k in range(KD):
                    b = bank((name, c, k))
                    if k == 0:
                        ready()
                    for tb in range(TB):
                        last = pe.transpose(b[:, tb * P:(tb + 1) * P], xcur[:, c * TB + tb, k * P:(k + 1) * P], ident)
                    last.then_inc(pe_done, 1)
                    if k in (3, 7):
                        tick(name, c, k)

            def channels(name, w, j, act_in, depth):
                b = bank(name)
                product(b[:, 0:TC], [(w[:, k, j * P:(j + 1) * P], act_in(k)) for k in range(depth)]).then_inc(pe_done, 1)

            pe.wait_ge(c_land, 16)
            for c in range(NC):
                if c == 0:
                    pe.wait_ge(rows_ok, 1)
                    pe.transpose(bank(("cols",))[:, 0:69], rows[0:69, :], ident[0:69, 0:69]).then_inc(pe_done, 1)
                transposed("xT", c, lambda: pe.wait_ge(x_land, 16 * (c + 1)))
                wait_emptied(pe, ("xT", c, KD - 1))
                x_of = lambda k: actT[:, k, :]
                for n in range(4):
                    if n % 2 == 0:
                        w = wait_piece(pe, ("u", c, n // 2))
                    channels(("u", c, n), w, n % 2, x_of, KD)
                    tick("proj", c, n)
                w = wait_piece(pe, ("kr", c, 0))
                b = bank(("kr", c))
                product(b[0:ROPE, 0:TC], [(w[:, k, :], actT[:, k, :]) for k in range(KD)]).then_inc(pe_done, 1)
                tick("proj", c, 4)
                w = wait_piece(pe, ("ckv", c, 0))
                for n in range(2):
                    channels(("ckv", c, n), w, n, x_of, KD)
                    tick("proj", c, 5 + n)
                for n in range(3):
                    if n % 2 == 0:
                        w = wait_piece(pe, ("cq", c, n // 2))
                    channels(("cq", c, n), w, n % 2, x_of, KD)
                    tick("proj", c, 7 + n)
                b = bank(("krot", c))
                wait_emptied(pe, ("kr", c))
                pe.matmul(b[:, 0:TC], rep, kraw[0:ROPE, :], start=True, stop=True)
                pe.matmul(b[:, TC:2 * TC], reprot, kraw[0:ROPE, :], start=True, stop=True).then_inc(pe_done, 1)
                if c == 0:
                    pe.wait_ge(bt_ok, 1)
                    for nm, src in (("BT", bbpad), ("CT", cdup)):
                        for i in range(2):
                            b = bank((nm, i))
                            for q in range(4):
                                last = pe.transpose(b[:, q * P:(q + 1) * P], src[:, i, q, :], ident)
                            last.then_inc(pe_done, 1)
                b = bank(("ss", c))
                pe.wait_ge(sq_ok, 5 * (c + 1))
                pe.wait_ge(fills, 3)
                product(b[:, 0:TC], [(ones, sq5[:, n, :]) for n in (0, 1)])
                product(b[:, TC:2 * TC], [(ones, sq5[:, n, :]) for n in (2, 3, 4)]).then_inc(pe_done, 1)
                if c == 0:
                    pe.wait_ge(mem_land, 16)
                    for kk in range(KD // 2):
                        b = bank(("memT", kk))
                        for i in range(2):
                            for mb in range(MB):
                                k = 2 * kk + i
                                last = pe.transpose(b[:, i * M_MEM + mb * P:i * M_MEM + (mb + 1) * P],
                                                    mem_nat[:, mb, k * P:(k + 1) * P], ident)
                        last.then_inc(pe_done, 1)
                    pe.wait_ge(keys_land, 32)
                    b = bank(("keysT",))
                    for i in range(2):
                        last = pe.transpose(b[:, i * NK:(i + 1) * NK], keys_nat[:, i], ident)
                    last.then_inc(pe_done, 1)
                tick("lat", c)
                pe.wait_ge(c_ok, 5 * (c + 1))
                cq_of = lambda k: cT[:, 2 + k, :]
                w = wait_piece(pe, ("uqr", c, 0))
                for g in range(2):
                    channels(("qrope", c, g), w, g, cq_of, 3)
                b = bank(("qrot", c))
                wait_emptied(pe, ("qrope", c, 1))
                for g in range(2):
                    last = pe.matmul(b[:, g * TC:(g + 1) * TC], rot, qraw[:, g, :], start=True, stop=True)
                last.then_inc(pe_done, 1)
                tick("qrot", c)
                w = wait_piece(pe, ("uqn", c, 0))
                for i in range(4):
                    channels(("qn", c, i), w, i, cq_of, 3)
                tick("qn", c)
                w = wait_piece(pe, ("ukn", c, 0))
                for i in range(4):
                    channels(("kn", c, i), w, i, lambda k: cT[:, k, :], 2)
                tick("kn", c)
                w = wait_piece(pe, ("ukv", c, 0))
                for tb in range(TB):
                    b = bank(("v", c, tb))
                    product(b, [(cT[:, k, tb * P:(tb + 1) * P], w[:, k, :]) for k in range(2)]).then_inc(pe_done, 1)
                tick("v", c)

                def bu(j):
                    b = bank(("bu", c, j))
                    q, r = j // 4, j % 4
                    for i in range(2):
                        last = pe.matmul(b[:, i * TC:(i + 1) * TC], BT[32 * r:32 * r + 32, i, q, :],
                                         uT[32 * r:32 * r + 32, q, :], start=True, stop=True)
                    last.then_inc(pe_done, 1)

                def score(i):
                    h, qb = i // TB, i % TB
                    keys = (c * TB + qb + 1) * P
                    b = bank(("sc", c, i))
                    pe.matmul(b[:, 0:keys], qT[0:DQ, h, qb * P:(qb + 1) * P], kT[0:DQ, h, 0:keys],
                              start=True, stop=True).then_inc(pe_done, 1)

                def mem_kv(i):
                    b = bank(("mem", i))
                    w = wait_piece(pe, ("xk" if i < 8 else "xv", 0, i % 8 // 2))
                    if i < 8:
                        pairs = [(w[:, k, (i % 2) * P:(i % 2 + 1) * P], memT[:, k, :]) for k in range(KD)]
                    else:
                        pairs = [(memT[:, k, (i % 2) * P:(i % 2 + 1) * P], w[:, k, :]) for k in range(KD)]
                    product(b[:, 0:PW], pairs).then_inc(pe_done, 1)

                def behind(j):
                    h, qb = j // TB, j % TB
                    qg = c * TB + qb
                    b = bank(("PT", c, j))
                    pe.wait_ge(pn, c * JT + j + 1)
                    for kb in range(qg + 1):
                        last = pe.transpose(b[:, kb * P:(kb + 1) * P], Pq[:, j % 2, kb * P:(kb + 1) * P], ident)
                    last.then_inc(pe_done, 1)
                    if qb == TB - 1:
                        b = bank(("pv", c, h))
                        wait_emptied(pe, ("PT", c, j))
                        half = 64 * (h % 2)
                        for kb in range((c + 1) * TB):
                            q0 = max(0, kb - c * TB) * P
                            last = pe.matmul(b[half:half + 64, q0:TC], V[:, kb, h * VH:(h + 1) * VH],
                                             PT[:, kb, q0:TC], start=(kb == 0), stop=(kb == (c + 1) * TB - 1))
                        last.then_inc(pe_done, 1)

                def state_out(j):
                    q, r = j // 4, j % 4
                    yb = psum[:, YBANK, (q % 2) * TC:(q % 2 + 1) * TC]
                    pe.wait_ge(st_ok, c * JT + j + 1)
                    if r == 0 and 4 * c + q >= 1:
                        pe.wait_ge(y_ok, 4 * c + q)
                    product(yb[32 * r:32 * r + 32, :],
                            [(CT[:, i, j, :], sS[:, j % 2, i, :]) for i in range(2)]).then_inc(y_mm, 1)

                if c == 0:
                    wait_emptied(pe, ("BT", 1))
                    wait_emptied(pe, ("CT", 1))
                bu(0)
                pe.wait_ge(q_ok, 2 * (c + 1))
                wait_emptied(pe, ("v", c, TB - 1))
                score(0)
                for j in range(JT + 1):
                    if c == 0 and j < JT:
                        mem_kv(j)
                    if j + 1 < JT:
                        bu(j + 1)
                    if j:
                        behind(j - 1)
                    if j + 1 < JT:
                        score(j + 1)
                    if j:
                        state_out(j - 1)
                    if j < JT:
                        tick("step", c, j)
                tick("gelu", c)
                w = wait_piece(pe, ("glu", c, 0))
                pe.wait_ge(gl_dve, 13 * c + 12)
                for n in range(4):
                    channels(("glu", c, n), w, n, lambda k: yT[:, k, :], 4)
                b = bank(("ms", c))
                wait_emptied(pe, ("glu", c, 3))
                first = []
                for n in range(4):
                    w = wait_piece(pe, ("wo", c, n))
                    first.append(bank(("mix", c, n, 0)))
                    product(first[n][:, 0:PW], [(oT[:, k, 0:P], w[:, k, :]) for k in range(4)])
                pe.wait_ge(sqm, 2 * (c + 1))
                for s, sqs in enumerate((Pr, g1)):
                    sv = sqs.rearrange("p (n t) -> p n t", n=4)
                    for tb in range(TB):
                        last = product(b[:, 2 * s + tb:2 * s + tb + 1], [(sv[:, n, tb * P:(tb + 1) * P], ones[:, 0:1]) for n in range(4)])
                last.then_inc(pe_done, 1)
                tick("glu", c)
                pe.wait_ge(mixin, c + 1)
                for tb in range(TB):
                    ts = slice(tb * P, (tb + 1) * P)
                    for n in range(4):
                        w = wslot(("wo", c, n))
                        b = first[n] if tb == 0 else bank(("mix", c, n, tb))
                        if tb:
                            product(b[:, 0:PW], [(oT[:, k, ts], w[:, k, :]) for k in range(4)])
                        product(b[:, PW:2 * PW], [(yT[:, k, ts], w[:, 4 + k, :]) for k in range(4)]).then_inc(pe_done, 1)
                        if n % 2:
                            tick("mix", c, 2 * tb + n // 2)
                    tick("ln1", c, tb)
                transposed("x1T", c, lambda: pe.wait_ge(ln_ok, 2 * TB * c + TB))
                wait_emptied(pe, ("x1T", c, KD - 1))
                for n in range(8):
                    if n % 2 == 0:
                        w = wait_piece(pe, ("xq", c, n // 2))
                    channels(("qx", c, n), w, n % 2, x_of, KD)
                    tick("qx", c, n)
                wait_emptied(pe, ("qx", c, 7))

                def xscore(i):
                    h, tb = i // TB, i % TB
                    b = bank(("xs", c, i))
                    product(b[:, 0:M_MEM], [(qTx[:, 2 * h + dc, tb * P:(tb + 1) * P], kTx[:, 2 * h + dc, :]) for dc in range(2)]).then_inc(pe_done, 1)

                def xbehind(i):
                    b = bank(("xPT", c, i))
                    pe.wait_ge(xpn, c * XH * TB + i + 1)
                    for mb in range(MB):
                        last = pe.transpose(b[:, mb * P:(mb + 1) * P], Px[:, i % 2, mb * P:(mb + 1) * P], ident)
                    last.then_inc(pe_done, 1)
                    if i % TB == TB - 1:
                        h = i // TB
                        wait_emptied(pe, ("xPT", c, i))
                        for dc in range(2):
                            b = bank(("ox", c, h, dc))
                            product(b[:, 0:TC], [(vx[:, mb, (2 * h + dc) * P:(2 * h + dc + 1) * P], PTx[:, h % 2, mb, :]) for mb in range(MB)]).then_inc(pe_done, 1)

                xscore(0)
                xscore(1)
                for i in range(XH * TB + 1):
                    if i:
                        xbehind(i - 1)
                    if i + 2 < XH * TB:
                        xscore(i + 2)
                    if i < XH * TB:
                        tick("xu", c, i)
                wait_emptied(pe, ("ox", c, XH - 1, 1))
                for tb in range(TB):
                    for n in range(4):
                        w = wait_piece(pe, ("xo", c, n))
                        b = bank(("xo", c, n, tb))
                        product(b[:, 0:PW], [(oTx[:, k, tb * P:(tb + 1) * P], w[:, k, :]) for k in range(KD)]).then_inc(pe_done, 1)
                        if n % 2:
                            tick("xo", c, 2 * tb + n // 2)
                    tick("ln2", c, tb)
                transposed("x2T", c, lambda: pe.wait_ge(ln_ok, 2 * TB * c + 2 * TB))
                wait_emptied(pe, ("x2T", c, KD - 1))

                def key_scores(tb, g):
                    b = bank(("ks", c, tb, g))
                    wait_emptied(pe, ("qq", c, 4 * g + 3))
                    for i in range(4):
                        n = 4 * g + i
                        last = pe.matmul(b[:, i * NK:(i + 1) * NK], qTq[:, n, tb * P:(tb + 1) * P],
                                         keysT[:, (n % 2) * NK:(n % 2 + 1) * NK], start=True, stop=True)
                    last.then_inc(pe_done, 1)

                for n in range(17):
                    if n < 16:
                        if n % 2 == 0:
                            w = wait_piece(pe, ("wq", c, n // 2))
                        channels(("qq", c, n), w, n % 2, x_of, KD)
                        tick("qq", c, n)
                    if n and n % 4 == 0:
                        key_scores(0, n // 4 - 1)
                        for m in (2, 1):
                            tick("rt", c, 0, n // 2 - m)
                tick("rt", c, 0, 8)
                for tb in range(1, TB):
                    for g in range(4):
                        key_scores(tb, g)
                    for n in range(9):
                        tick("rt", c, tb, n)
            for kind, units in (("uv", 32), ("v", 16)):
                for p in range(2):
                    serve_at(kind, 3, p, p)
                with pe.Fori(1, units // 2) as m:
                    i = m * 2
                    for p in range(2):
                        serve_at(kind, 3, p, p, i)

        @block.scalar
        def _(act):
            chain = [0]

            def step(ins):
                ins.then_inc(act_c, 1)
                chain[0] += 1
                act.wait_ge(act_c, chain[0])

            order = iter([n for n, e in JOBS if e == "act"])

            def take(name, ops):
                assert next(order) == name, name
                wait_job(act, name)
                ops(bank_of(name)).then_inc(emptied["act"], 1)

            def take_exp(name, out_, scale, bias, total, signal, count):
                assert next(order) == name, name
                wait_job(act, name)
                b = bank_of(name)
                act.activation(out_, b[:, 0:out_.shape[1]], ACT.Exp, bias=bias, scale=scale, accum_out=total).then_inc(signal, 1)
                act.wait_ge(signal, count)
                act.sem_inc(emptied["act"], 1)

            def copy(dst, src):
                return act.copy(dst, src)

            devs = [0]

            def deviation():
                devs[0] += 1
                act.wait_ge(var_ok, devs[0])
                act.activation(std[:, 0:1], mv[:, 1:2], ACT.Sqrt, bias=kc[:, 1:2]).then_inc(std_ok, 1)

            loads = [0]

            def load_ln(g, b, after):
                if after:
                    act.wait_ge(ln_ok, after)
                act.dma_start(lngb[:, 0:D], a[g][0:1, :].to_broadcast([P, D])).then_inc(ln_land, 16)
                act.dma_start(lngb[:, D:2 * D], a[b][0:1, :].to_broadcast([P, D])).then_inc(ln_land, 16)

            def make_diag(unit, half, q, weights, i=0):
                kind, tb, n = unit
                vt = tb - 1 if kind == "uv" else tb
                batches = len(V_SLOTS[kind]) // DB
                batch = HK * vt // DB + batches * n + half
                if type(i) is not int:
                    per = AFTER_BATCH[batch + batches] - AFTER_BATCH[batch]
                    act.wait_ge(v_done, i * per + (AFTER_BATCH[batch] - 2 // batches * per))
                elif batch >= 2:
                    act.wait_ge(v_done, AFTER_BATCH[batch - 2])
                for d in range(DB):
                    if V_SLOTS[kind][DB * half + d] not in vector_slots(*unit):
                        last = act.mul(diag[:, q, d, :], ident, weights[:, d:d + 1])
                last.then_inc(diag_ok, 1)

            def serve(kind, tb, n=0):
                if kind == "w":
                    act.wait_ge(h_ok, tb + 1)
                    act.activation(gel[:, tb % 2, :], gel[:, tb % 2, :], ACT.Tanh, scale=GELU_C).then_inc(h_act, 1)
                elif kind == "uv":
                    if n == 0:
                        act.wait_ge(w_ok, tb)
                    make_diag((kind, tb, n), 0, n % 2, wbuf[:, (tb - 1) % 2, DB * n:DB * (n + 1)])
                elif kind == "v":
                    if n == 0:
                        act.wait_ge(w_ok, tb + 1)
                    for half in range(2):
                        at = NSL * n + DB * half
                        make_diag((kind, tb, n), half, half, wbuf[:, tb % 2, at:at + DB])

            staged = [0]

            def serve_loop(kind, tb, units):
                w0 = staged[0]
                wide, vt = (DB, tb - 1) if kind == "uv" else (NSL, tb)
                with act.Fori(1, units // 2) as m:
                    i = m * 2
                    for p in range(2):
                        for x in vector_slots(kind, tb, 1)[-1:]:
                            _, per, at = in_loop((kind, tb, p), x, 2)
                            act.wait_ge(x_done, i * per + at)
                        act.copy(w8[:, p, 0:wide], wbuf[:, vt % 2, bass.ds(i * wide + wide * p, wide)]).then_inc(w8_ok, 1)
                        act.wait_ge(w8_ok, i + (w0 - 2 + p + 1))
                        for half in range(wide // DB):
                            q = p if kind == "uv" else half
                            make_diag((kind, tb, p), half, q, w8[:, p, DB * half:DB * half + DB], i)
                staged[0] += units - 2

            tick = server(serve)

            load_ln("ln1_g", "ln1_b", 0)
            dt, mag, cosr, sinr, absr, a1, red = par[3:10]
            act.wait_ge(par_dve, 1)
            act.activation(dt, cols[:, 32:48], ACT.Exp).then_inc(par_act, 1)
            act.wait_ge(par_dve, 2)
            act.activation(mag, a1, ACT.Exp).then_inc(par_act, 1)
            act.wait_ge(par_dve, 3)
            act.wait_ge(fills, 3)
            act.activation(sinr, red, ACT.Sin).then_inc(par_act, 1)
            step(act.activation(absr, red, ACT.Abs))
            act.activation(cosr, absr, ACT.Sin, scale=-1.0, bias=kc[:, 2:3]).then_inc(par_act, 1)

            def transposed(name, c):
                for k in range(KD):
                    take((name, c, k), lambda b: copy(actT[:, k, :], b[:, 0:TC]))
                    if k in (3, 7):
                        tick(name, c, k)

            transposed("xT", 0)
            act.wait_ge(par_dve, 4)
            f = ang[:, 0:512]
            act.activation(trig_t[:, 512:1024], f, ACT.Sin, scale=6.283185).then_inc(trig_ok, 1)
            step(act.activation(ang[:, 512:1024], f, ACT.Abs))
            act.activation(trig_t[:, 0:512], ang[:, 512:1024], ACT.Sin, scale=-6.283185, bias=kc[:, 2:3]).then_inc(trig_ok, 1)
            act.wait_ge(par_dve, 5)
            f = ang[:, 1024:1536]
            act.activation(ropeS, f, ACT.Sin).then_inc(trig_ok, 1)
            step(act.activation(ang[:, 1536:2048], f, ACT.Abs))
            act.activation(ropeC, ang[:, 1536:2048], ACT.Sin, scale=-1.0, bias=kc[:, 2:3]).then_inc(trig_ok, 1)

            for c in range(NC):
                tok = slice(c * TC, (c + 1) * TC)

                if c:
                    wait_job(act, ("qq", c - 1, 15))
                    transposed("xT", c)
                if c == 0:
                    act.wait_ge(trig_ok, 4)
                    act.wait_ge(bt_ok, 1)
                else:
                    act.wait_ge(route_ok, TB * c)
                for n in range(4):
                    take(("u", c, n), lambda b: copy(uT[:, n, :], b[:, 0:TC]))
                    tick("proj", c, n)
                take(("kr", c), lambda b: copy(kraw[0:ROPE, :], b[0:ROPE, 0:TC]))
                tick("proj", c, 4)
                for n in range(5):
                    def ops(b):
                        act.activation(sq5[:, n, :], b[:, 0:TC], ACT.Square).then_inc(sq_ok, 1)
                        return copy(cT[:, n, :], b[:, 0:TC])
                    take(("ckv", c, n) if n < 2 else ("cq", c, n - 2), ops)
                    tick("proj", c, 5 + n)
                if c == 0:
                    for i in range(2):
                        take(("BT", i), lambda b: copy(BT[:, i], b.rearrange("p (q m) -> p q m", q=4)))
                    for i in range(2):
                        take(("CT", i), lambda b: act.mul(CT[:, i], b.rearrange("p (j h) -> p j h", h=32), -1.0 if i else 1.0))

                def ops(b):
                    act.activation(rms[:, 0:TC], b[:, 0:TC], ACT.Sqrt, scale=1.0 / KVL, bias=kc[:, 0:1])
                    return act.activation(rms[:, TC:2 * TC], b[:, TC:2 * TC], ACT.Sqrt, scale=1.0 / QL, bias=kc[:, 0:1])
                take(("ss", c), ops)
                if c == 0:
                    for kk in range(KD // 2):
                        take(("memT", kk), lambda b: copy(memT[:, 2 * kk:2 * kk + 2, :], b.rearrange("p (i m) -> p i m", i=2)))
                    take(("keysT",), lambda b: copy(keysT[:, :], b[:, 0:2 * NK]))
                tick("lat", c)
                for g in range(2):
                    take(("qrope", c, g), lambda b: copy(qraw[:, g, :], b[:, 0:TC]))
                tick("qrot", c)
                for i in range(4):
                    def ops(b):
                        copy(qT[0:NOPE, 2 * i, :], b[0:NOPE, 0:TC])
                        return copy(qT[0:NOPE, 2 * i + 1, :], b[NOPE:2 * NOPE, 0:TC])
                    take(("qn", c, i), ops)
                tick("qn", c)
                for i in range(4):
                    def ops(b):
                        copy(kT[0:NOPE, 2 * i, tok], b[0:NOPE, 0:TC])
                        return copy(kT[0:NOPE, 2 * i + 1, tok], b[NOPE:2 * NOPE, 0:TC])
                    take(("kn", c, i), ops)
                tick("kn", c)
                for tb in range(TB):
                    take(("v", c, tb), lambda b: copy(V[:, c * TB + tb, :], b))
                tick("v", c)

                def exps(i):
                    keys = (c * TB + i % TB + 1) * P
                    act.wait_ge(smax, c * JT + i + 1)
                    if i == 0:
                        act.wait_ge(q_ok, 2 * (c + 1))
                    if i >= 2:
                        wait_job(act, ("PT", c, i - 2))
                    if c or i >= 2:
                        act.wait_ge(pn, c * JT + i - 1)
                    take_exp(("sc", c, i), Pq[:, i % 2, 0:keys], DQ ** -0.5, nmax[:, i % 2:i % 2 + 1],
                             rsum[:, i % 2:i % 2 + 1], pexp, c * JT + i + 1)

                ga, gb = gelu_t[:, 0:TC], gelu_t[:, TC:2 * TC]

                def gelu_in(q):
                    n = 4 * c + q
                    act.wait_ge(y_ok, n + 1)
                    if n:
                        act.wait_ge(gl_dve, 13 * c + 3 * q)
                    act.activation(ga, yT[:, q, :], ACT.Square).then_inc(gl_act, 1)
                    act.mul(gb, yT[:, q, :], 0.5).then_inc(gl_act, 1)

                def gelu_tanh(q):
                    act.wait_ge(gl_dve, 13 * c + 3 * q + 2)
                    act.activation(ga, ga, ACT.Tanh, scale=GELU_C).then_inc(gl_act, 1)

                for j in range(JT + 1):
                    if j < JT:
                        exps(j)
                    if j >= 5 and j % 4 == 1 and j < JT:
                        gelu_in(j // 4 - 1)
                    if j >= 6 and j % 4 == 2:
                        gelu_tanh(j // 4 - 1)
                    if c == 0 and j < JT:
                        if j < 8:
                            take(("mem", j), lambda b: copy(kTx[:, j, :], b[:, 0:M_MEM]))
                        else:
                            n = (j - 8) // 2
                            take(("mem", j), lambda b: copy(vx[:, j % 2, PW * n:PW * (n + 1)], b[:, 0:PW]))
                    if j:
                        h, qb = (j - 1) // TB, (j - 1) % TB
                        qg = c * TB + qb
                        if qb == 0 and h:
                            wait_job(act, ("pv", c, h - 1))
                        take(("PT", c, j - 1), lambda b: copy(PT[:, 0:qg + 1, qb * P:(qb + 1) * P],
                                                              b[:, 0:(qg + 1) * P].rearrange("p (k t) -> p k t", k=qg + 1)))
                        if qb == TB - 1:
                            rows_ = slice(64 * (h % 2), 64 * (h % 2) + 64)
                            take(("pv", c, h), lambda b: copy(oT[rows_, h // 2, :], b[rows_, 0:TC]))
                    if j < JT:
                        keys = (c * TB + j % TB + 1) * P
                        act.wait_ge(rinv_ok, c * JT + j + 1)
                        act.mul(Pq[:, j % 2, 0:keys], Pq[:, j % 2, 0:keys], rsum[:, j % 2:j % 2 + 1]).then_inc(pn, 1)
                        tick("step", c, j)
                gelu_in(3)
                gelu_tanh(3)
                oTf = scratch[:, 2304:3328]
                wait_emptied(act, ("pv", c, H - 1))
                wait_job(act, ("pv", c, H - 1))
                act.activation(Pr, oTf, ACT.Square).then_inc(sqm, 1)
                act.wait_ge(sqm, 2 * c + 1)
                for n in range(4):
                    step(act.mul(oT[:, n, :], oT[:, n, :], cols[:, 61 + n:62 + n]))
                tick("gelu", c)
                act.wait_ge(gl_dve, 13 * c + 12)
                for n in range(4):
                    take(("glu", c, n), lambda b: act.activation(g1[:, n * TC:(n + 1) * TC], b[:, 0:TC], ACT.Tanh,
                                                                 scale=0.5, bias=kcol[:, n:n + 1]))
                act.wait_ge(gl_dve, 13 * c + 13)
                act.activation(g1, g2, ACT.Square, scale=0.5).then_inc(sqm, 1)
                for n in range(4):
                    last = act.mul(yT[:, n, :], g2[:, n * TC:(n + 1) * TC], kcol[:, 4 + n:5 + n])
                last.then_inc(mixin, 1)
                take(("ms", c), lambda b: act.activation(rsmix, b[:, 0:4], ACT.Sqrt, scale=1.0 / SW, bias=kc[:, 0:1]))
                tick("glu", c)
                for tb in range(TB):
                    for n in range(2):
                        tick("mix", c, 2 * tb + n)
                    deviation()
                    tick("ln1", c, tb)
                load_ln("ln2_g", "ln2_b", 2 * TB * c + TB)
                transposed("x1T", c)
                for n in range(8):
                    take(("qx", c, n), lambda b: copy(qTx[:, n, :], b[:, 0:TC]))
                    tick("qx", c, n)

                def xexps(i):
                    act.wait_ge(xsmax, c * XH * TB + i + 1)
                    if i >= 2:
                        wait_job(act, ("xPT", c, i - 2))
                    take_exp(("xs", c, i), Px[:, i % 2, :], 1.0 / 16, nmax[:, 2 + i % 2:3 + i % 2],
                             rsum[:, 2 + i % 2:3 + i % 2], xexp, c * XH * TB + i + 1)

                xexps(0)
                for i in range(XH * TB + 1):
                    if i + 1 < XH * TB:
                        xexps(i + 1)
                    if i:
                        h, tb = (i - 1) // TB, (i - 1) % TB
                        if tb == 0 and h >= 2:
                            wait_job(act, ("ox", c, h - 2, 1))
                        take(("xPT", c, i - 1), lambda b: copy(PTx[:, h % 2, :, tb * P:(tb + 1) * P],
                                                               b[:, 0:M_MEM].rearrange("p (m t) -> p m t", m=MB)))
                        if tb == TB - 1:
                            for dc in range(2):
                                take(("ox", c, h, dc), lambda b: copy(oTx[:, 2 * h + dc, :], b[:, 0:TC]))
                    if i < XH * TB:
                        tick("xu", c, i)
                for tb in range(TB):
                    for n in range(2):
                        tick("xo", c, 2 * tb + n)
                    deviation()
                    tick("ln2", c, tb)
                load_ln(*(("ln1_g", "ln1_b") if c + 1 < NC else ("ln3_g", "ln3_b")), 2 * TB * (c + 1))
                transposed("x2T", c)
                for n in range(17):
                    if n < 16:
                        take(("qq", c, n), lambda b: copy(qTq[:, n, :], b[:, 0:TC]))
                        tick("qq", c, n)
                    if n and n % 4 == 0:
                        g = n // 4 - 1
                        take(("ks", c, 0, g), lambda b: copy(S1[:, g * 512:(g + 1) * 512], b))
                        for m in (2, 1):
                            tick("rt", c, 0, n // 2 - m)
                for tb in range(TB):
                    if tb:
                        act.wait_ge(s_free, c * TB + tb)
                        for g in range(4):
                            take(("ks", c, tb, g), lambda b: copy(S1[:, g * 512:(g + 1) * 512], b))
                    for n in range(8 if tb == 0 else 0, 9):
                        if n == 8:
                            act.wait_ge(rt_d, c * TB + tb + 1)
                            act.activation(tia, tia, ACT.Exp).then_inc(rt_a, 1)
                        tick("rt", c, tb, n)
            serve("w", 2)
            for n in range(2):
                serve("uv", 3, n)
                deviation()
            serve_loop("uv", 3, 32)
            serve("w", 3)
            for n in range(2):
                serve("v", 3, n)
            deviation()
            serve_loop("v", 3, 16)
            deviation()

        @block.gpsimd
        def _(pool):
            chain = [0]

            def step(ins):
                ins.then_inc(pool_c, 1)
                chain[0] += 1
                pool.wait_ge(pool_c, chain[0])

            def gather(s, table, index):
                pool.indirect_dma_start(rowbuf[s], None, a[table][0], bass.IndirectOffsetOnAxis(index, 0)).then_inc(row_land[s], 16)

            def wait_buffer(unit, s, i=0):
                if type(i) is not int:
                    eng, per, at = in_loop(unit, s, 1)
                    pool.wait_ge(used_sem[eng], i * per + at)
                elif UNIT_NO[unit]:
                    eng, at = USED[UNITS[UNIT_NO[unit] - 1]][s]
                    pool.wait_ge(used_sem[eng], at)

            def serve(kind, tb, n=0):
                if kind in ("w", "o"):
                    return
                if kind == "u" and n % 4 == 0:
                    pool.wait_ge(ids_ok, 5 * (tb // TB) + n // 4 + 1)
                elif kind == "uv" and n == 0:
                    pool.wait_ge(ids_ok, 5 * (tb // TB) + 5)
                for s in range(NSL):
                    wait_buffer((kind, tb, n), s)
                    if kind == "uv":
                        t_, hk = (tb, 4 * n + s // 2) if s % 2 == 0 else (tb - 1, 4 * n + s // 2)
                    else:
                        t_, hk = tb, NSL * n + s
                    table = "v_tab" if kind == "v" or (kind == "uv" and s % 2) else "u_tab"
                    gather(s, table, ids_t[:, t_ * HK + hk:t_ * HK + hk + 1])

            tick = server(serve)
            stages = [0]

            def serve_loop(kind, tb, units):
                base = stages[0]
                if kind == "u":
                    pool.wait_ge(ids_ok, 5 * (tb // TB) + 4)
                with pool.Fori(1, units // 2) as m:
                    i = m * 2
                    for p in range(2):
                        if kind == "uv":
                            st = idstage[:, p, :].rearrange("p (n e) -> p n e", e=2)
                            pool.tensor_copy(st[:, :, 0], ids_t[:, bass.ds(i * 4 + (tb * HK + 4 * p), 4)])
                            pool.tensor_copy(st[:, :, 1], ids_t[:, bass.ds(i * 4 + ((tb - 1) * HK + 4 * p), 4)]).then_inc(stage_ok, 1)
                        else:
                            pool.tensor_copy(idstage[:, p, :], ids_t[:, bass.ds(i * NSL + (tb * HK + NSL * p), NSL)]).then_inc(stage_ok, 1)
                        pool.wait_ge(stage_ok, i + (base - 2 + p + 1))
                        for s in range(NSL):
                            wait_buffer((kind, tb, p), s, i)
                            pool.nop(nofuse=True)
                            gather(s, "v_tab" if kind == "v" or (kind == "uv" and s % 2) else "u_tab", idstage[:, p, s:s + 1])
                stages[0] += units - 2

            pool.memset(ones, 1.0).then_inc(fills, 1)
            pool.memset(kc[:, 0:1], 1e-6)
            pool.memset(kc[:, 1:2], 1e-5)
            pool.memset(kc[:, 3:4], 0.0)
            pool.memset(kc[:, 2:3], math.pi / 2).then_inc(fills, 1)
            pool.memset(small[:, :], 0.0).then_inc(fills, 1)

            def scale_x(c, name):
                for k in (3, 7):
                    if k == 7:
                        wait_job(pool, (name, c, KD - 1))
                        for tb in range(TB):
                            pool.tensor_scalar(xcur[:, c * TB + tb, :], xcur[:, c * TB + tb, :], ALPHA, 0.0, ALU.mult, ALU.add).then_inc(xscaled, 1)
                    tick(name, c, k)

            for c in range(NC):
                scale_x(c, "xT")
                t1, t2 = pool_t[:, 0:TC].rearrange("p (a b) -> p a b", a=16), pool_t[:, TC:2 * TC].rearrange("p (a b) -> p a b", a=16)
                pool.wait_ge(trig_ok, 4)
                if c:
                    pool.wait_ge(route_ok, TB * c)

                def table(j):
                    if j >= 2:
                        pool.wait_ge(tab_used, c * JT + j - 1)
                    cb, ca = bc(trig[:, 0, j, 0:16], 1, 16), bc(trig[:, 0, j, 16:32], 2, 16)
                    sb_, sa = bc(trig[:, 1, j, 0:16], 1, 16), bc(trig[:, 1, j, 16:32], 2, 16)
                    o = tab[:, j % 2].rearrange("p i (a b) -> p i a b", a=16)
                    pool.tensor_tensor(o[:, 0], cb, ca, ALU.mult)
                    step(pool.tensor_tensor(t1, sb_, sa, ALU.mult))
                    pool.tensor_tensor(o[:, 0], o[:, 0], t1, ALU.subtract)
                    pool.tensor_tensor(o[:, 1], sb_, ca, ALU.mult)
                    step(pool.tensor_tensor(t2, cb, sa, ALU.mult))
                    pool.tensor_tensor(o[:, 1], o[:, 1], t2, ALU.add).then_inc(tab_ok, 1)
                    pool.wait_ge(tab_ok, c * JT + j + 1)

                for n in range(10):
                    tick("proj", c, n)
                table(0)
                table(1)
                for key in ("lat", "qrot", "qn", "kn", "v"):
                    tick(key, c)
                for j in range(JT):
                    if 1 <= j < JT - 1:
                        table(j + 1)
                    tick("step", c, j)
                for key in ("gelu", "glu"):
                    tick(key, c)
                for tb in range(TB):
                    for n in range(2):
                        tick("mix", c, 2 * tb + n)
                    tick("ln1", c, tb)
                scale_x(c, "x1T")
                for key, count in (("qx", 8), ("xu", XH * TB)):
                    for n in range(count):
                        tick(key, c, n)
                for tb in range(TB):
                    for n in range(2):
                        tick("xo", c, 2 * tb + n)
                    tick("ln2", c, tb)
                for k in (3, 7):
                    tick("x2T", c, k)
                for n in range(17):
                    if n < 16:
                        tick("qq", c, n)
                    if n and n % 4 == 0:
                        for m in (2, 1):
                            tick("rt", c, 0, n // 2 - m)
                tick("rt", c, 0, 8)
                for tb in range(1, TB):
                    for n in range(9):
                        tick("rt", c, tb, n)
            for kind, tb, units in (("u", 2, 16), ("uv", 3, 32), ("v", 3, 16)):
                serve(kind, tb, 0)
                serve(kind, tb, 1)
                serve_loop(kind, tb, units)

        @block.vector
        def _(dve):
            chain = [0]

            def mark(ins):
                ins.then_inc(dve_c, 1)
                chain[0] += 1

            def settle():
                dve.wait_ge(dve_c, chain[0])

            def step(ins):
                mark(ins)
                settle()

            order = iter([n for n, e in JOBS if e == "dve"])

            def open_job(name):
                assert next(order) == name, name
                wait_job(dve, name)
                return bank_of(name)

            norms = [0]

            def layer_norm(tb, ln_value, signal):
                z = xcur[:, tb, :]
                for i in range(2):
                    mark(dve.bn_stats(st6[:, i, :], z[:, 512 * i:512 * i + 512]))
                settle()
                dve.bn_aggr(mv, st6).then_inc(var_ok, 1)
                norms[0] += 1
                dve.wait_ge(std_ok, norms[0])
                step(dve.reciprocal(std[:, 1:2], std[:, 0:1]))
                step(dve.tensor_scalar(z, z, mv[:, 0:1], std[:, 1:2], ALU.subtract, ALU.mult))
                dve.wait_ge(ln_land, ln_value)
                step(dve.tensor_tensor(z, z, lngb[:, 0:D], ALU.mult))
                dve.tensor_tensor(z, z, lngb[:, D:2 * D], ALU.add).then_inc(signal, 1)

            def dot(unit, s, dst, i=0):
                dve.wait_ge(row_land[s], i * 16 + 16 * (UNIT_NO[unit] + 1))
                dve.tensor_tensor_reduce(out=rowbuf[s], in0=rowbuf[s], in1=xcur[:, unit[1], :], scale=1.0, scalar=0.0,
                                         op0=ALU.mult, op1=ALU.add, accum_out=dst).then_inc(u_done, 1)

            def add_row(unit, s, weight, i=0):
                kind, tb, n = unit
                z = xcur[:, tb - 1 if kind == "uv" else tb, :]
                dve.wait_ge(row_land[s], i * 16 + 16 * (UNIT_NO[unit] + 1))
                if type(i) is not int:
                    _, per, at = in_loop(unit, s, 0)
                    dve.wait_ge(x_done, i * per + (at - 1))
                elif USED[unit][s][1] > 1:
                    dve.wait_ge(x_done, USED[unit][s][1] - 1)
                dve.scalar_tensor_tensor(out=z, in0=rowbuf[s], scalar=weight, in1=z, op0=ALU.mult, op1=ALU.add).then_inc(x_done, 1)

            def serve(kind, tb, n=0):
                if kind == "w":
                    dve.wait_ge(u_done, HK * (tb + 1))
                    z = xcur[:, tb, :]
                    mark(dve.tensor_scalar(z, z, ALPHA, None, ALU.mult))
                    h_, g_, w_ = hbuf[:, tb % 2, :], gel[:, tb % 2, :], wbuf[:, tb % 2, :]
                    step(dve.tensor_tensor(g_, h_, h_, ALU.mult))
                    step(dve.tensor_scalar(g_, g_, 0.044715, 1.0, ALU.mult, ALU.add))
                    dve.tensor_tensor(g_, g_, h_, ALU.mult).then_inc(h_ok, 1)
                    step(dve.tensor_scalar(h_, h_, 0.5, None, ALU.mult))
                    dve.wait_ge(h_act, tb + 1)
                    step(dve.scalar_tensor_tensor(out=g_, in0=g_, scalar=1.0, in1=h_, op0=ALU.add, op1=ALU.mult))
                    dve.tensor_tensor(w_, g_, gates_t[:, tb * HK:(tb + 1) * HK], ALU.mult).then_inc(w_ok, 1)
                    dve.wait_ge(w_ok, tb + 1)
                    return
                if kind == "o":
                    dve.wait_ge(v_done, rows_of_block(tb, "v"))
                    if rows_of_block(tb, "x"):
                        dve.wait_ge(x_done, rows_of_block(tb, "x"))
                    z2 = xcur[:, tb, :].rearrange("p (i n) -> p i n", i=2)
                    dve.tensor_tensor(z2, z2, psum[:, OB:OB + 2, :], ALU.add).then_inc(peer_out, 1)
                    return
                for s in range(NSL):
                    if s in vector_slots(kind, tb, n):
                        vt, hk = (tb - 1, 4 * n + s // 2) if kind == "uv" else (tb, NSL * n + s)
                        add_row((kind, tb, n), s, wbuf[:, vt % 2, hk:hk + 1])
                    elif s not in V_SLOTS[kind]:
                        hk = NSL * n + s if kind == "u" else 4 * n + s // 2
                        dot((kind, tb, n), s, hbuf[:, tb % 2, hk:hk + 1])

            tick = server(serve)
            stored, staged = [0], [0]

            def serve_loop(kind, tb, units):
                s0, w0 = stored[0], staged[0]
                n_dots = NSL - len(V_SLOTS[kind])
                with dve.Fori(1, units // 2) as m:
                    i = m * 2
                    for p in range(2):
                        unit = (kind, tb, p)
                        if vector_slots(*unit):
                            dve.wait_ge(w8_ok, i + (w0 - 2 + p + 1))
                        for s in range(NSL):
                            if s in vector_slots(*unit):
                                at = V_SLOTS[kind].index(s)
                                add_row(unit, s, w8[:, p, at:at + 1], i)
                            elif s not in V_SLOTS[kind]:
                                d = s if kind == "u" else s // 2
                                dot(unit, s, h8[:, p, d:d + 1], i)
                        if n_dots:
                            dve.wait_ge(u_done, i * n_dots + (HK * tb + n_dots * (p + 1)))
                            dve.tensor_copy(hbuf[:, tb % 2, bass.ds(i * n_dots + n_dots * p, n_dots)], h8[:, p, 0:n_dots]).then_inc(dots_ok, 1)
                            dve.wait_ge(dots_ok, i + (s0 - 2 + p + 1))
                if kind != "v":
                    stored[0] += units - 2
                if kind != "u":
                    staged[0] += units - 2

            li, dtl, dt, mag, cosr, sinr, absr, a1, red = par[1:10]
            lr = par[0]
            k_, th, t0, t1, nr, ni, den, fre, fim, rden, rt, rhi, rlo = par[10:23]

            dve.wait_ge(par_land, 16 * 9)
            dve.tensor_copy(rows[32:48, :].rearrange("j (g q) -> j g q", g=2), bc(ldt[32:48, :], 2, NS)).then_inc(rows_ok, 1)
            b = open_job(("cols",))
            dve.tensor_copy(cols[:, 0:69], b[:, 0:69]).then_inc(emptied["dve"], 1)
            wait_emptied(dve, ("cols",))
            dve.tensor_copy(lr, cols[:, 0:16])
            dve.tensor_scalar(kcol[:, 0:4], cols[:, 57:61], 0.5, None, ALU.mult)
            dve.tensor_scalar(kcol[:, 4:8], cols[:, 65:69], 0.5, None, ALU.mult)
            dve.tensor_copy(li, cols[:, 16:32]).then_inc(par_dve, 1)
            dve.wait_ge(par_act, 1)
            step(dve.tensor_tensor(th, li, dt, ALU.mult))
            dve.tensor_tensor(a1, lr, dt, ALU.mult).then_inc(par_dve, 1)

            def reduce_angle(dst, src, kbuf):
                step(dve.tensor_scalar(kbuf, src, INV2PI, MAGIC, ALU.mult, ALU.add))
                step(dve.tensor_scalar(kbuf, kbuf, -MAGIC, None, ALU.add))
                step(dve.scalar_tensor_tensor(out=dst, in0=kbuf, scalar=-C1, in1=src, op0=ALU.mult, op1=ALU.add))
                step(dve.scalar_tensor_tensor(out=dst, in0=kbuf, scalar=-C2, in1=dst, op0=ALU.mult, op1=ALU.add))
                step(dve.scalar_tensor_tensor(out=dst, in0=kbuf, scalar=-C3, in1=dst, op0=ALU.mult, op1=ALU.add))
                return dve.tensor_scalar(dst, dst, PI_IN, -PI_IN, ALU.min, ALU.max)

            reduce_angle(red, th, k_).then_inc(par_dve, 1)
            dve.wait_ge(par_dve, 3)
            step(dve.tensor_scalar(rt, red, INV2PI, None, ALU.mult))
            step(dve.tensor_scalar(rhi, rt, MAGIC / 2 ** 14, None, ALU.add))
            step(dve.tensor_scalar(rhi, rhi, -MAGIC / 2 ** 14, None, ALU.add))
            step(dve.tensor_tensor(rlo, rt, rhi, ALU.subtract))
            m3 = bc(mult32, 1, JT)
            fa = ang[:, 0:512].rearrange("p (j m) -> p j m", j=JT)
            fb = ang[:, 2048:2560].rearrange("p (j m) -> p j m", j=JT)
            fc = ang[:, 2560:3072].rearrange("p (j m) -> p j m", j=JT)
            dve.wait_ge(c_land, 16)
            step(dve.tensor_tensor(fa, m3, bc(rhi, 2, 32), ALU.mult))
            step(dve.tensor_scalar(fb, fa, MAGIC, None, ALU.add))
            step(dve.tensor_scalar(fb, fb, -MAGIC, None, ALU.add))
            step(dve.tensor_tensor(fa, fa, fb, ALU.subtract))
            step(dve.tensor_tensor(fc, m3, bc(rlo, 2, 32), ALU.mult))
            step(dve.tensor_tensor(fa, fa, fc, ALU.add))
            step(dve.tensor_scalar(fb, fa, MAGIC, None, ALU.add))
            step(dve.tensor_scalar(fb, fb, -MAGIC, None, ALU.add))
            dve.tensor_tensor(fa, fa, fb, ALU.subtract).then_inc(par_dve, 1)
            dve.wait_ge(pos_land, 16)
            posf = ang[:, 2048:2560]
            dve.wait_ge(par_dve, 4)
            step(dve.tensor_copy(posf, pos_i))
            step(dve.tensor_scalar(posf, posf, freq, None, ALU.mult))
            reduce_angle(ang[:, 1024:1536], posf, ang[:, 2560:3072]).then_inc(par_dve, 1)

            dve.wait_ge(par_act, 4)
            dve.wait_ge(bc_land, 64)
            step(dve.tensor_tensor(t0, mag, cosr, ALU.mult))
            step(dve.tensor_tensor(ni, mag, sinr, ALU.mult))
            step(dve.tensor_scalar(nr, t0, -1.0, None, ALU.add))
            dve.tensor_copy(magc, mag)
            step(dve.tensor_tensor(den, lr, lr, ALU.mult))
            step(dve.tensor_tensor(t1, li, li, ALU.mult))
            step(dve.tensor_tensor(den, den, t1, ALU.add))
            step(dve.reciprocal(rden, den))
            step(dve.tensor_tensor(fre, nr, lr, ALU.mult))
            step(dve.tensor_tensor(t0, ni, li, ALU.mult))
            step(dve.tensor_tensor(fre, fre, t0, ALU.add))
            step(dve.tensor_tensor(fre, fre, rden, ALU.mult))
            step(dve.tensor_tensor(fim, ni, lr, ALU.mult))
            step(dve.tensor_tensor(t1, nr, li, ALU.mult))
            step(dve.tensor_tensor(fim, fim, t1, ALU.subtract))
            step(dve.tensor_tensor(fim, fim, rden, ALU.mult))
            fr, fi = bc(fre, 2, GC), bc(fim, 2, GC)
            dve.tensor_tensor(bbw[:, 0], bnat[:, 0], fr, ALU.mult)
            dve.tensor_tensor(bbw[:, 1], bnat[:, 1], fi, ALU.mult)
            dve.tensor_tensor(bbw[:, 2], bnat[:, 1], fr, ALU.mult)
            step(dve.tensor_tensor(bbw[:, 3], bnat[:, 0], fi, ALU.mult))
            step(dve.memset(bbpad, 0.0))
            for i, op in enumerate((ALU.subtract, ALU.add)):
                for g in range(2):
                    ps = slice(64 * g, 64 * g + 64)
                    o = bbpad[ps, i].rearrange("p q (r g h) -> p q r g h", g=2, h=GC)[:, :, :, g, :]
                    x0 = bbw[ps, 2 * i].rearrange("p (q r) h -> p q r h", r=4)
                    x1 = bbw[ps, 2 * i + 1].rearrange("p (q r) h -> p q r h", r=4)
                    mark(dve.tensor_tensor(o, x0, x1, op))
            for i in range(2):
                for q in range(4):
                    last = dve.tensor_tensor(cdup[:, i, q, :].rearrange("p (g s) -> p g s", g=2), bc(cnat[:, i, q, :], 1, 2),
                                             parity.rearrange("p (g s) -> p g s", g=2), ALU.mult)
            last.then_inc(bt_ok, 1)

            for c in range(NC):
                tok = slice(c * TC, (c + 1) * TC)
                for k in (3, 7):
                    tick("xT", c, k)
                for n in range(10):
                    tick("proj", c, n)
                b = open_job(("krot", c))
                dve.wait_ge(trig_ok, 4)
                rr = slice(64, 96)
                mark(dve.tensor_tensor(kt1[rr, :], b[rr, 0:TC], ropeC[rr, tok], ALU.mult))
                dve.tensor_tensor(kt2[rr, :], b[rr, TC:2 * TC], ropeS[rr, tok], ALU.mult).then_inc(emptied["dve"], 1)
                settle()
                wait_emptied(dve, ("krot", c))
                if c == 0:
                    wait_job(dve, ("CT", 1))
                dve.tensor_tensor(kT[rr, :, tok], bc(kt1[rr, :], 1, H), bc(kt2[rr, :], 1, H), ALU.add).then_inc(q_ok, 1)
                wait_emptied(dve, ("ss", c))
                step(dve.reciprocal(rms, rms))
                for n in range(5):
                    r_ = rms[:, 0:TC] if n < 2 else rms[:, TC:2 * TC]
                    dve.scalar_tensor_tensor(out=cT[:, n, :], in0=cT[:, n, :], scalar=cols[:, 48 + n:49 + n], in1=r_,
                                             op0=ALU.mult, op1=ALU.mult).then_inc(c_ok, 1)
                tick("lat", c)
                b = open_job(("qrot", c))
                mark(dve.tensor_tensor(qtmp, b.rearrange("p (g t) -> p g t", g=2), bc(ropeS[:, tok], 1, 2), ALU.mult))
                settle()
                dve.sem_inc(emptied["dve"], 1)
                step(dve.tensor_tensor(qraw, qraw, bc(ropeC[:, tok], 1, 2), ALU.mult))
                for g in range(2):
                    for i in range(4):
                        ps = slice(32 * i, 32 * i + 32)
                        last = dve.tensor_tensor(qT[rr, 4 * g + i, :], qraw[ps, g, :], qtmp[ps, g, :], ALU.add)
                last.then_inc(q_ok, 1)
                for key in ("qrot", "qn", "kn", "v"):
                    tick(key, c)

                def row_max(i):
                    keys = (c * TB + i % TB + 1) * P
                    wait_job(dve, ("sc", c, i))
                    if c or i:
                        dve.wait_ge(smax, c * JT + i)
                    b = bank_of(("sc", c, i))
                    step(dve.tensor_tensor(b[:, keys - P:keys], b[:, keys - P:keys], causal, ALU.add))
                    step(dve.tensor_reduce(gsum[:, 0:1], b[:, 0:keys], AX.X, ALU.max, negate=True))
                    dve.tensor_scalar(nmax[:, i % 2:i % 2 + 1], gsum[:, 0:1], DQ ** -0.5, None, ALU.mult).then_inc(smax, 1)

                def take_y(q):
                    dve.wait_ge(y_mm, c * JT + 4 * q + 4)
                    dve.scalar_tensor_tensor(out=yT[:, q, :], in0=uT[:, q, :], scalar=cols[:, 53 + q:54 + q],
                                             in1=psum[:, YBANK, (q % 2) * TC:(q % 2 + 1) * TC], op0=ALU.mult, op1=ALU.add).then_inc(y_ok, 1)

                ga, gb = gelu_t[:, 0:TC], gelu_t[:, TC:2 * TC]

                def gelu_arg(q):
                    dve.wait_ge(gl_act, 12 * c + 3 * q + 1)
                    dve.tensor_scalar(ga, ga, 0.044715, 1.0, ALU.mult, ALU.add).then_inc(gl_dve, 1)
                    dve.wait_ge(gl_dve, 13 * c + 3 * q + 1)
                    dve.tensor_tensor(ga, ga, yT[:, q, :], ALU.mult).then_inc(gl_dve, 1)

                def gelu_out(q):
                    dve.wait_ge(gl_act, 12 * c + 3 * q + 3)
                    dve.scalar_tensor_tensor(out=yT[:, q, :], in0=ga, scalar=1.0, in1=gb, op0=ALU.add, op1=ALU.mult).then_inc(gl_dve, 1)

                for j in range(JT):
                    row_max(j)
                    b = open_job(("bu", c, j)).rearrange("p (i t) -> p i t", i=2)
                    dve.wait_ge(tab_ok, c * JT + j + 1)
                    cs, sn = bc(tab[:, j % 2, 0, :], 1, 2), bc(tab[:, j % 2, 1, :], 1, 2)
                    mark(dve.tensor_tensor(sA, b, cs, ALU.mult))
                    mark(dve.tensor_tensor(sB, b, sn, ALU.mult))
                    settle()
                    dve.sem_inc(emptied["dve"], 1)
                    mark(dve.tensor_tensor(sW[:, 0], sA[:, 0], sB[:, 1], ALU.add))
                    mark(dve.tensor_tensor(sW[:, 1], sA[:, 1], sB[:, 0], ALU.subtract))
                    settle()
                    for i in range(2):
                        mark(dve.tensor_tensor_scan(sW[:, i, :], magc[:, j:j + 1].to_broadcast([P, TC]), sW[:, i, :],
                                                    0.0 if c == 0 else carry[:, j, i:i + 1], ALU.mult, ALU.add))
                    settle()
                    dve.wait_ge(pexp, c * JT + j + 1)
                    dve.reciprocal(rsum[:, j % 2:j % 2 + 1], rsum[:, j % 2:j % 2 + 1]).then_inc(rinv_ok, 1)
                    mark(dve.tensor_tensor(sA, sW, cs, ALU.mult))
                    mark(dve.tensor_tensor(sB, sW, sn, ALU.mult))
                    settle()
                    dve.sem_inc(tab_used, 1)
                    if c * JT + j >= 2:
                        dve.wait_ge(y_mm, c * JT + j - 1)
                    mark(dve.tensor_tensor(sS[:, j % 2, 0, :], sA[:, 0], sB[:, 1], ALU.subtract))
                    mark(dve.tensor_tensor(sS[:, j % 2, 1, :], sA[:, 1], sB[:, 0], ALU.add))
                    settle()
                    dve.tensor_copy(carry[:, j, :], sS[:, j % 2, :, TC - 1]).then_inc(st_ok, 1)
                    if j and j % 4 == 0:
                        take_y(j // 4 - 1)
                    if j >= 5 and j % 4 == 1:
                        gelu_arg(j // 4 - 1)
                    if j >= 6 and j % 4 == 2:
                        gelu_out(j // 4 - 1)
                    tick("step", c, j)
                take_y(3)
                gelu_arg(3)
                gelu_out(3)
                yTf = scratch[:, 1024:2048]
                tick("gelu", c)
                wait_emptied(dve, ("glu", c, 3))
                dve.wait_ge(gl_dve, 13 * c + 12)
                dve.scalar_tensor_tensor(out=g2, in0=g1, scalar=1.0, in1=yTf, op0=ALU.add, op1=ALU.mult).then_inc(gl_dve, 1)
                wait_emptied(dve, ("ms", c))
                step(dve.reciprocal(rsmix, rsmix))
                tick("glu", c)
                dve.wait_ge(xscaled, TB * (2 * c + 1))
                for tb in range(TB):
                    for n in range(4):
                        z = xcur[:, c * TB + tb, PW * n:PW * (n + 1)]
                        b = open_job(("mix", c, n, tb))
                        step(dve.scalar_tensor_tensor(out=z, in0=b[:, 0:PW], scalar=rsmix[:, tb:tb + 1], in1=z,
                                                      op0=ALU.mult, op1=ALU.add))
                        dve.scalar_tensor_tensor(out=z, in0=b[:, PW:2 * PW], scalar=rsmix[:, 2 + tb:3 + tb], in1=z,
                                                 op0=ALU.mult, op1=ALU.add).then_inc(emptied["dve"], 1)
                        if n % 2:
                            tick("mix", c, 2 * tb + n // 2)
                    wait_emptied(dve, ("mix", c, 3, tb))
                    layer_norm(c * TB + tb, 32 * (2 * c + 1), ln_ok)
                    tick("ln1", c, tb)
                for k in (3, 7):
                    tick("x1T", c, k)
                for n in range(8):
                    tick("qx", c, n)
                def xrow_max(i):
                    wait_job(dve, ("xs", c, i))
                    if c or i:
                        dve.wait_ge(xsmax, c * XH * TB + i)
                    b = bank_of(("xs", c, i))
                    step(dve.tensor_reduce(gsum[:, 2:3], b[:, 0:M_MEM], AX.X, ALU.max, negate=True))
                    dve.tensor_scalar(nmax[:, 2 + i % 2:3 + i % 2], gsum[:, 2:3], 1.0 / 16, None, ALU.mult).then_inc(xsmax, 1)

                xrow_max(0)
                for i in range(XH * TB):
                    if i + 1 < XH * TB:
                        xrow_max(i + 1)
                    dve.wait_ge(xexp, c * XH * TB + i + 1)
                    if c or i:
                        dve.wait_ge(xpn, c * XH * TB + i)
                    step(dve.reciprocal(gsum[:, 3:4], rsum[:, 2 + i % 2:3 + i % 2]))
                    dve.tensor_scalar(Px[:, i % 2, :], Px[:, i % 2, :], gsum[:, 3:4], None, ALU.mult).then_inc(xpn, 1)
                    tick("xu", c, i)
                dve.wait_ge(xscaled, TB * (2 * c + 2))
                for tb in range(TB):
                    for n in range(4):
                        z = xcur[:, c * TB + tb, PW * n:PW * (n + 1)]
                        b = open_job(("xo", c, n, tb))
                        dve.tensor_tensor(z, b[:, 0:PW], z, ALU.add).then_inc(emptied["dve"], 1)
                        if n % 2:
                            tick("xo", c, 2 * tb + n // 2)
                    wait_emptied(dve, ("xo", c, 3, tb))
                    layer_norm(c * TB + tb, 32 * (2 * c + 2), ln_ok)
                    tick("ln2", c, tb)
                for k in (3, 7):
                    tick("x2T", c, k)

                def top16(vals, idx, n, rows_):
                    lo = [slice(16 * (n + i), 16 * (n + i) + 8) for i in range(2)]
                    hi = [slice(16 * (n + i) + 8, 16 * (n + i) + 16) for i in range(2)]
                    left = [rest[:, i, 0:rows_[0].shape[1]] for i in range(2)]
                    for i in range(2):
                        mark(dve.max(vals[:, lo[i]], rows_[i]))
                    settle()
                    for i in range(2):
                        mark(dve.match_replace(left[i], vals[:, lo[i]], rows_[i], -3e38))
                    for i in range(2):
                        mark(dve.max_index(idx[:, lo[i]], vals[:, lo[i]], rows_[i]))
                    settle()
                    for i in range(2):
                        mark(dve.max(vals[:, hi[i]], left[i]))
                    settle()
                    for i in range(2):
                        mark(dve.max_index(idx[:, hi[i]], vals[:, hi[i]], left[i]))

                def route(tb, g0, g1, ticks):
                    ticks = iter(ticks)
                    tg, heads = c * TB + tb, range(2 * g0, 2 * g1)
                    nh = len(heads)
                    wait_emptied(dve, ("ks", c, tb, g1 - 1))
                    for n in range(4 * g0, 4 * g1, 2):
                        top16(rv, ridx, n, [S1[:, (n + i) * NK:(n + i + 1) * NK] for i in range(2)])
                        if n % 4 == 2:
                            tick("rt", c, tb, next(ticks))
                    settle()
                    lists, kept = slice(64 * g0, 64 * g1), slice(32 * g0, 32 * g1)
                    mark(dve.tensor_copy(rif[:, lists], ridx[:, lists]))
                    rvv = rv[:, lists].rearrange("p (h s k) -> p h s k", h=nh, s=2)
                    own = S1[:, 512 * g0:512 * g1]
                    cand = own.rearrange("p (h a b) -> p h a b", h=nh, a=TOPK)
                    step(dve.tensor_tensor(cand, bc(rvv[:, :, 0, :], 3, TOPK), bc(rvv[:, :, 1, :], 2, TOPK), ALU.add))
                    for h in heads[::2]:
                        top16(tops, tpos, h, [S1[:, (h + i) * 256:(h + i + 1) * 256] for i in range(2)])
                        if nh > 2 and h % 4 == 2:
                            tick("rt", c, tb, next(ticks))
                    settle()
                    mark(dve.tensor_scalar(tau[:, kept], tpos[:, kept], 4, None, ALU.logical_shift_right))
                    step(dve.tensor_scalar(tbu[:, kept], tpos[:, kept], 15, None, ALU.bitwise_and))
                    mark(dve.tensor_copy(tab_a[:, kept], tau[:, kept]))
                    step(dve.tensor_copy(tab_b[:, kept], tbu[:, kept]))
                    rifv = rif[:, lists].rearrange("p (h s k) -> p h s k", h=nh, s=2)
                    e = own.rearrange("p (h k m) -> p h k m", h=nh, k=TOPK)
                    for s, place, dst in ((0, tab_a, tia), (1, tab_b, tib)):
                        pl = bc(place[:, kept].rearrange("p (h k) -> p h k", h=nh), 3, TOPK)
                        io = bc(bc(iota16, 1, TOPK), 1, nh)
                        step(dve.tensor_tensor(e, pl, io, ALU.is_equal))
                        step(dve.tensor_tensor(e, e, bc(rifv[:, :, s, :], 2, TOPK), ALU.mult))
                        step(dve.tensor_reduce(dst[:, kept], e, AX.X, ALU.add))
                        if nh > 2 and s == 0:
                            tick("rt", c, tb, next(ticks))
                    step(dve.scalar_tensor_tensor(out=ids_t[:, tg * HK + 32 * g0:tg * HK + 32 * g1], in0=tia[:, kept],
                                                  scalar=float(NK), in1=tib[:, kept], op0=ALU.mult, op1=ALU.add))
                    dve.sem_inc(ids_ok, 1)
                    tick("rt", c, tb, next(ticks))

                def gates(tb):
                    tg = c * TB + tb
                    dve.sem_inc(s_free, 1)
                    tv, ti = (t.rearrange("p (h k) -> p h k", h=PH) for t in (tops, tia))
                    dve.tensor_tensor(ti, tv, bc(tv[:, :, 0], 2, TOPK), ALU.subtract).then_inc(rt_d, 1)
                    dve.wait_ge(rt_a, tg + 1)
                    step(dve.tensor_reduce(gsum[:, 0:8], ti, AX.X, ALU.add))
                    step(dve.reciprocal(gsum[:, 0:8], gsum[:, 0:8]))
                    step(dve.tensor_tensor(gates_t[:, tg * HK:(tg + 1) * HK].rearrange("p (h k) -> p h k", h=PH),
                                           ti, bc(gsum[:, 0:8], 2, TOPK), ALU.mult))
                    dve.sem_inc(route_ok, 1)
                    tick("rt", c, tb, 8)

                for n in range(17):
                    if n < 16:
                        tick("qq", c, n)
                    if n and n % 4 == 0:
                        route(0, n // 4 - 1, n // 4, range(n // 2 - 2, n // 2))
                gates(0)
                for tb in range(1, TB):
                    route(tb, 0, 4, range(8))
                    gates(tb)

            ln3 = 32 * (2 * NC + 1)
            for n in range(2):
                serve("u", 2, n)
            serve_loop("u", 2, 16)
            serve("w", 2)
            for n in range(2):
                serve("uv", 3, n)
                dve.wait_ge(peer_out, 2)
                layer_norm(n, ln3, fin_ok)
            serve_loop("uv", 3, 32)
            serve("o", 2)
            serve("w", 3)
            for n in range(2):
                serve("v", 3, n)
            dve.wait_ge(peer_out, 3)
            layer_norm(2, ln3, fin_ok)
            serve_loop("v", 3, 16)
            serve("o", 3)
            dve.wait_ge(peer_out, 4)
            layer_norm(3, ln3, fin_ok)


NAMES = ["x", "mem", "positions", "w_in", "g_cq", "w_uq", "g_ckv", "w_ukv", "lam_re", "lam_im", "log_dt", "b_re", "b_im",
         "c_re", "c_im", "d_skip", "w_glu", "b_glu", "g_mla_out", "g_ssm_out", "w_out", "ln1_g", "ln1_b", "xq", "xk", "xv",
         "xo", "ln2_g", "ln2_b", "w_query", "sub_keys1", "sub_keys2", "u_tab", "v_tab", "ln3_g", "ln3_b"]


def kernel(**inputs):
    import concourse.bacc as bacc
    from concourse.bass_utils import run_bass_kernel_spmd

    nc = bacc.Bacc("TRN2", target_bir_lowering=False, num_devices=1)
    arrays, args = {}, {}
    for name in NAMES:
        arr = np.ascontiguousarray(inputs[name])
        arrays["in_" + name] = arr
        args[name] = nc.dram_tensor("in_" + name, arr.shape, mybir.dt.from_np(arr.dtype), kind="ExternalInput").ap()
    arrays["in_consts"] = shape_constants()
    consts = nc.dram_tensor("in_consts", (P, CW), F32, kind="ExternalInput").ap()
    out = nc.dram_tensor("out", (1, T, D), F32, kind="ExternalOutput").ap()
    build(nc, args, consts, out)
    r = run_bass_kernel_spmd(nc, [arrays], core_ids=[0])
    return r.results[0]["out"]
```
